# Optimizing a Trainium2 kernel written in Bass

```python
import jax
import jax.numpy as jnp
from jax import lax

D_MODEL = 1024
BATCH = 1
SEQ = 2048
DEPTH = 2
DEC_BATCH = 8
DEC_SEQ = 4
PAST_LEN = 2048
PAGE_SIZE = 128

FOX_HEAD_DIM = 128
FOX_HEADS = D_MODEL // FOX_HEAD_DIM
FOX_WIDTH = FOX_HEADS * FOX_HEAD_DIM
Q_BLOCK = 128
N_MEM = 256
X_HEADS = 4
X_HEAD_DIM = 128
X_WIDTH = X_HEADS * X_HEAD_DIM
POOL_WINDOWS = (2, 4, 8, 16)
POOL_GROUPS = len(POOL_WINDOWS)
POOL_WIDTH = D_MODEL
POOL_GC = POOL_WIDTH // POOL_GROUPS
POOL_HIST = max(POOL_WINDOWS) - 1
BRANCH_WIDTH = FOX_WIDTH + X_WIDTH
FOX_IN = 3 * FOX_WIDTH + FOX_HEADS + X_WIDTH + BRANCH_WIDTH
POOL_IN = POOL_WIDTH + X_WIDTH + BRANCH_WIDTH
EPS = 1e-6

kernel_name = 'hybrid_fox_pool_memxattn_step'

def rmsnorm(x, g):
    xf = x.astype(jnp.float32)
    r = lax.rsqrt(jnp.mean(xf * xf, axis=-1, keepdims=True) + EPS)
    return (xf * r * g.astype(jnp.float32)).astype(x.dtype)

def mem_kv(mem, g, w):
    kv = rmsnorm(mem, g) @ w
    b = mem.shape[0]
    k = kv[..., :X_WIDTH].reshape(b, N_MEM, X_HEADS, X_HEAD_DIM)
    v = kv[..., X_WIDTH:].reshape(b, N_MEM, X_HEADS, X_HEAD_DIM)
    return k, v

def mem_attend(xq, mk, mv):
    b, t, _ = xq.shape
    q = xq.reshape(b, t, X_HEADS, X_HEAD_DIM)
    s = jnp.einsum('bqhd,bmhd->bhqm', q, mk).astype(jnp.float32) * (X_HEAD_DIM ** -0.5)
    p = jax.nn.softmax(s, axis=-1).astype(mv.dtype)
    return jnp.einsum('bhqm,bmhd->bqhd', p, mv).reshape(b, t, X_WIDTH)

def gated_out(mix, xo, gate, w):
    return (jnp.concatenate([mix, xo], axis=-1) * jax.nn.silu(gate)) @ w

def split_fox(z, b_f):
    lead = z.shape[:-1]
    hs = (FOX_HEADS, FOX_HEAD_DIM)
    q = z[..., :FOX_WIDTH].reshape(lead + hs)
    k = z[..., FOX_WIDTH:2 * FOX_WIDTH].reshape(lead + hs)
    v = z[..., 2 * FOX_WIDTH:3 * FOX_WIDTH].reshape(lead + hs)
    o = 3 * FOX_WIDTH
    f = z[..., o:o + FOX_HEADS]
    o += FOX_HEADS
    xq = z[..., o:o + X_WIDTH]
    gate = z[..., o + X_WIDTH:]
    lf = jax.nn.log_sigmoid((f + b_f).astype(jnp.float32))
    return q, k, v, lf, xq, gate

def split_pool(z):
    return z[..., :POOL_WIDTH], z[..., POOL_WIDTH:POOL_WIDTH + X_WIDTH], z[..., POOL_WIDTH + X_WIDTH:]

def fox_prompt(q, k, v, lf):
    b, t, h, hd = q.shape
    nblk = t // Q_BLOCK
    c = jnp.cumsum(lf, axis=1)
    c_keys = c.transpose(0, 2, 1)
    qb = q.reshape(b, nblk, Q_BLOCK, h, hd).transpose(1, 0, 2, 3, 4)
    cb = c.reshape(b, nblk, Q_BLOCK, h).transpose(1, 0, 3, 2)
    kpos = jnp.arange(t)
    scale = hd ** -0.5

    def one_block(args):
        i, q_i, c_i = args
        s = jnp.einsum('bqhd,bkhd->bhqk', q_i, k).astype(jnp.float32) * scale
        s = s + (c_i[..., :, None] - c_keys[:, :, None, :])
        qpos = i * Q_BLOCK + jnp.arange(Q_BLOCK)
        s = jnp.where(kpos[None, :] <= qpos[:, None], s, -jnp.inf)
        p = jax.nn.softmax(s, axis=-1).astype(v.dtype)
        return jnp.einsum('bhqk,bkhd->bqhd', p, v)

    out = lax.map(one_block, (jnp.arange(nblk), qb, cb))
    return out.transpose(1, 0, 2, 3, 4).reshape(b, t, h * hd)

def fox_sample(q, k_new, v_new, lf_new, k_past, v_past, lf_past):
    db, tn, h, hd = q.shape
    scale = hd ** -0.5
    c_new = jnp.cumsum(lf_new, axis=1).transpose(0, 2, 1)
    suf = jnp.flip(jnp.cumsum(jnp.flip(lf_past, 1), axis=1), 1) - lf_past
    suf = suf.transpose(0, 2, 1)
    s_past = jnp.einsum('bqhd,bkhd->bhqk', q, k_past).astype(jnp.float32) * scale
    s_past = s_past + suf[:, :, None, :] + c_new[:, :, :, None]
    s_new = jnp.einsum('bqhd,bkhd->bhqk', q, k_new).astype(jnp.float32) * scale
    s_new = s_new + (c_new[:, :, :, None] - c_new[:, :, None, :])
    tril = jnp.arange(tn)[None, :] <= jnp.arange(tn)[:, None]
    s_new = jnp.where(tril, s_new, -jnp.inf)
    p = jax.nn.softmax(jnp.concatenate([s_past, s_new], axis=-1), axis=-1).astype(v_new.dtype)
    n_past = k_past.shape[1]
    out = (jnp.einsum('bhqk,bkhd->bqhd', p[..., :n_past], v_past)
           + jnp.einsum('bhqk,bkhd->bqhd', p[..., n_past:], v_new))
    return out.reshape(db, tn, h * hd)

def multiscale_pool(u_ext, pos, w_group, scale):
    b, n, c = u_ext.shape
    t = n - POOL_HIST
    s = jnp.cumsum(u_ext.astype(jnp.float32), axis=1)
    s0 = jnp.concatenate([jnp.zeros((b, 1, c), jnp.float32), s], axis=1)
    end = s0[:, 1 + POOL_HIST:]
    outs = []
    for g, w in enumerate(POOL_WINDOWS):
        sl = slice(g * POOL_GC, (g + 1) * POOL_GC)
        start = s0[:, 1 + POOL_HIST - w:1 + POOL_HIST - w + t, sl]
        cnt = jnp.minimum(w, pos + 1).astype(jnp.float32)[None, :, None]
        outs.append((end[..., sl] - start) / cnt)
    pooled = jnp.concatenate(outs, axis=-1)
    d = (pooled - u_ext[:, POOL_HIST:].astype(jnp.float32)).astype(u_ext.dtype)
    y = jnp.einsum('btgc,gcd->btgd', d.reshape(b, t, POOL_GROUPS, POOL_GC), w_group)
    return y.reshape(b, t, c) * scale

def setup_inputs(seed: int = 0) -> dict:
    key = jax.random.key(seed)
    ks = jax.random.split(key, 20)
    f32 = jnp.float32
    n_pages = PAST_LEN // PAGE_SIZE
    n_used = DEC_BATCH * n_pages
    n_pool = n_used + (n_used + 3) // 4

    def nrm(k, shape, s=1.0):
        return s * jax.random.normal(k, shape, f32)

    page_table = jax.random.permutation(ks[9], n_pool)[:n_used].reshape(DEC_BATCH, n_pages).astype(jnp.int32)
    return {
        'x_prompt': nrm(ks[0], (BATCH, SEQ, D_MODEL)),
        'x_sample': nrm(ks[1], (DEC_BATCH, DEC_SEQ, D_MODEL)),
        'mem_prompt': nrm(ks[2], (BATCH, N_MEM, D_MODEL)),
        'cache_fox_k': nrm(ks[3], (n_pool, PAGE_SIZE, FOX_HEADS, FOX_HEAD_DIM)),
        'cache_fox_v': nrm(ks[4], (n_pool, PAGE_SIZE, FOX_HEADS, FOX_HEAD_DIM)),
        'cache_fox_logf': jax.nn.log_sigmoid(nrm(ks[5], (n_pool, PAGE_SIZE, FOX_HEADS)) + 4.0),
        'cache_mem_k': nrm(ks[6], (DEPTH, DEC_BATCH, N_MEM, X_HEADS, X_HEAD_DIM)),
        'cache_mem_v': nrm(ks[7], (DEPTH, DEC_BATCH, N_MEM, X_HEADS, X_HEAD_DIM)),
        'state_pool': nrm(ks[8], (DEC_BATCH, POOL_HIST, POOL_WIDTH)),
        'page_table': page_table,
        'norm_pre': 1.0 + nrm(ks[10], (DEPTH, D_MODEL), 0.1),
        'norm_post': 1.0 + nrm(ks[11], (DEPTH, D_MODEL), 0.1),
        'mem_norm': 1.0 + nrm(ks[12], (DEPTH, D_MODEL), 0.1),
        'w_mem_kv': nrm(ks[13], (DEPTH, D_MODEL, 2 * X_WIDTH), D_MODEL ** -0.5),
        'fox_w_in': nrm(ks[14], (D_MODEL, FOX_IN), D_MODEL ** -0.5),
        'fox_b_f': nrm(ks[15], (FOX_HEADS,), 0.01),
        'pool_w_in': nrm(ks[16], (D_MODEL, POOL_IN), D_MODEL ** -0.5),
        'pool_w_group': nrm(ks[17], (POOL_GROUPS, POOL_GC, POOL_GC), POOL_GC ** -0.5),
        'pool_scale': 1.0 + nrm(ks[18], (POOL_WIDTH,), 0.1),
        'w_out': nrm(ks[19], (DEPTH, BRANCH_WIDTH, D_MODEL), BRANCH_WIDTH ** -0.5),
    }

def reference(x_prompt, x_sample, mem_prompt, cache_fox_k, cache_fox_v, cache_fox_logf, cache_mem_k, cache_mem_v, state_pool, page_table, norm_pre, norm_post, mem_norm, w_mem_kv, fox_w_in, fox_b_f, pool_w_in, pool_w_group, pool_scale, w_out):
    b, t, _ = x_prompt.shape
    db, tn, _ = x_sample.shape
    n_past = page_table.shape[1] * PAGE_SIZE
    y_p, y_s = x_prompt, x_sample
    mem_k_list, mem_v_list = [], []
    for l in range(DEPTH):
        h_p = rmsnorm(y_p, norm_pre[l])
        h_s = rmsnorm(y_s, norm_pre[l])
        mk_p, mv_p = mem_kv(mem_prompt, mem_norm[l], w_mem_kv[l])
        mem_k_list.append(mk_p)
        mem_v_list.append(mv_p)
        mk_s, mv_s = cache_mem_k[l], cache_mem_v[l]
        if l % 2 == 0:
            q, k, v, lf, xq_p, g_p = split_fox(h_p @ fox_w_in, fox_b_f)
            mix_p = fox_prompt(q, k, v, lf)
            fox_k_p = k.reshape(b * t // PAGE_SIZE, PAGE_SIZE, FOX_HEADS, FOX_HEAD_DIM)
            fox_v_p = v.reshape(b * t // PAGE_SIZE, PAGE_SIZE, FOX_HEADS, FOX_HEAD_DIM)
            fox_lf_p = lf.reshape(b * t // PAGE_SIZE, PAGE_SIZE, FOX_HEADS)
            qs, ks_, vs, lfs, xq_s, g_s = split_fox(h_s @ fox_w_in, fox_b_f)
            k_past = cache_fox_k[page_table].reshape(db, n_past, FOX_HEADS, FOX_HEAD_DIM).astype(ks_.dtype)
            v_past = cache_fox_v[page_table].reshape(db, n_past, FOX_HEADS, FOX_HEAD_DIM).astype(vs.dtype)
            lf_past = cache_fox_logf[page_table].reshape(db, n_past, FOX_HEADS).astype(jnp.float32)
            mix_s = fox_sample(qs, ks_, vs, lfs, k_past, v_past, lf_past)
            fox_k_s, fox_v_s, fox_lf_s = ks_, vs, lfs
        else:
            u_p, xq_p, g_p = split_pool(h_p @ pool_w_in)
            u_ext_p = jnp.concatenate([jnp.zeros((b, POOL_HIST, POOL_WIDTH), u_p.dtype), u_p], axis=1)
            mix_p = multiscale_pool(u_ext_p, jnp.arange(t, dtype=jnp.int32), pool_w_group, pool_scale)
            pool_state_p = u_ext_p[:, -POOL_HIST:]
            u_s, xq_s, g_s = split_pool(h_s @ pool_w_in)
            u_ext_s = jnp.concatenate([state_pool.astype(u_s.dtype), u_s], axis=1)
            mix_s = multiscale_pool(u_ext_s, n_past + jnp.arange(tn, dtype=jnp.int32), pool_w_group, pool_scale)
            pool_state_s = u_ext_s[:, -POOL_HIST:]
        y_p = y_p + rmsnorm(gated_out(mix_p, mem_attend(xq_p, mk_p, mv_p), g_p, w_out[l]), norm_post[l])
        y_s = y_s + rmsnorm(gated_out(mix_s, mem_attend(xq_s, mk_s, mv_s), g_s, w_out[l]), norm_post[l])
    mem_k_p = jnp.stack(mem_k_list)
    mem_v_p = jnp.stack(mem_v_list)
    return (y_p, y_s, fox_k_p, fox_v_p, fox_lf_p, fox_k_s, fox_v_s, fox_lf_s, mem_k_p, mem_v_p, pool_state_p, pool_state_s)


_drawn_inputs = setup_inputs


def setup_inputs(seed=0):
    import zlib

    import numpy as np

    out = dict(_drawn_inputs(seed))
    spreads = {}
    factors = {'fox_b_f': 21.467}
    for name, (base, spread) in spreads.items():
        noise = np.random.default_rng([zlib.crc32(name.encode()), seed]).standard_normal(out[name].shape)
        drawn = base * np.exp(spread * noise) if base else spread * noise
        out[name] = jnp.asarray(drawn.astype(out[name].dtype))
    for name, factor in factors.items():
        out[name] = (out[name] * factor).astype(out[name].dtype)
    return out
```

```python
from contextlib import ExitStack

import concourse.bass as bass
from concourse import mybir
from concourse.alu_op_type import AluOpType as ALU

F32 = mybir.dt.float32
F32R = mybir.dt.float32r
BF16 = mybir.dt.bfloat16
I32 = mybir.dt.int32
ACT = mybir.ActivationFunctionType
AX = mybir.AxisListType
ds = bass.ds

P = 128
D = 1024
KT = D // P
SEQ = 2048
NQ = SEQ // P
DB, TN = 8, 4
NS = DB * TN
TOK = SEQ + NS
CH = 5
CW = TOK // CH
FH, XH, HD = 8, 4, 128
XW = XH * HD
BW = D + XW
NM = 256
PAGES = 16
EPS = 1e-6
SCALE = float(HD) ** -0.5
NEG = -1e30
LOWEST = -3e38
HIST = 15


class Core:

    def __init__(self, nc, stack, tag):
        self.nc, self.stack, self.tag = nc, stack, tag
        self.sems = []
        stack.callback(self.clear)

    def clear(self):
        if self.sems:
            self.nc.clear_and_free_semaphores(self.sems)

    def sb(self, name, shape, dt=F32):
        return self.stack.enter_context(self.nc.sbuf_tensor(f"{name}_{self.tag}", shape, dt))

    def sem(self, name):
        free = self.nc.free_semaphores
        self.sems.append(self.nc.alloc_semaphore(f"{name}_{self.tag}", num=free[-1]))
        return self.sems[-1]


def make_constants(nc, stack, banks):
    g = Core(nc, stack, "const")
    ident = g.sb("ident", [P, P])
    ones = g.sb("ones", [P, P])
    ident_b = g.sb("ident_b", [P, P], BF16)
    mask_b = g.sb("mask_b", [P, P], BF16)
    with ExitStack() as s:
        c = Core(nc, s, "mk")
        made = c.sem("const_made")
        block = s.enter_context(nc.Block())

        @block.gpsimd
        def _(pool):
            nc.gpsimd.memset(ident[:, :], 0.0).then_inc(made, 1)
            nc.gpsimd.memset(ident_b[:, :], 0.0).then_inc(made, 1)
            nc.gpsimd.memset(mask_b[:, :], 0.0).then_inc(made, 1)
            nc.gpsimd.memset(ones[:, :], 1.0).then_inc(made, 1)
            pool.wait_ge(made, 4)
            for t in (ident, ident_b):
                nc.gpsimd.affine_select(out=t[:, :], in_=t[:, :], compare_op=ALU.not_equal, fill=1.0,
                                        base=0, pattern=[[-1, P]], channel_multiplier=1).then_inc(made, 1)
            nc.gpsimd.affine_select(out=mask_b[:, :], in_=mask_b[:, :], compare_op=ALU.is_ge, fill=NEG,
                                    base=0, pattern=[[-1, P]], channel_multiplier=1).then_inc(made, 1)
            pool.wait_ge(made, 7)
    return dict(ident=ident, ones=ones, ident_b=ident_b, mask_b=mask_b)


def norm_transpose(nc, tag, const, banks, tiles, gain, hT_hi, hT_lo):
    looped, single = tiles
    pairs = looped.shape[0] // P // 2 if looped is not None else 0
    ident = const["ident"]
    with ExitStack() as s:
        c = Core(nc, s, tag)
        g_bc = c.sb("g_bc", [P, D])
        x = c.sb("x", [P, 2, D])
        xn = c.sb("xn", [P, 2, D])
        ss = c.sb("ss", [P, 2])
        ms = c.sb("ms", [P, 2])
        rt = c.sb("rt", [P, 2])
        ri = c.sb("ri", [P, 2])
        g_in = c.sem("gain_loaded")
        x_in = [c.sem(f"x_loaded{u}") for u in range(2)]
        sq_done = c.sem("sumsq_done")
        ms_done = c.sem("meansq_done")
        rt_done = c.sem("root_done")
        ri_done = c.sem("rinv_done")
        xn_done = c.sem("xn_done")
        tr_done = c.sem("transposed")
        hi_done = c.sem("hi_done")
        lo_done = c.sem("lo_done")
        block = s.enter_context(nc.Block())
        n_pairs = pairs

        def groups(eng, body):
            if n_pairs:
                with eng.Fori(0, n_pairs) as i:
                    body(i, 2 * i, [(u, P, (2 * i + u) * P, None) for u in range(2)])
            base_pair = n_pairs
            todo = list(single)
            while todo:
                now, todo = todo[:2], todo[2:]
                body(base_pair, 2 * base_pair, [(u, rows, col, src) for u, (src, rows, col) in enumerate(now)])
                base_pair += 1

        assert len(single) in (1, 2)

        @block.sync
        def _(sp):
            sp.dma_start(g_bc[:, :], gain.partition_broadcast(P)).then_inc(g_in, 16)

            def body(pair, t0, tl):
                for u, rows, col, src in tl:
                    if src is None:
                        src = looped[ds(col, P), :]
                    sp.wait_ge(xn_done, t0 + u)
                    sp.dma_start(x[0:rows, u, :], src).then_inc(x_in[u], 16)
            groups(sp, body)

        @block.scalar
        def _(act):
            def body(pair, t0, tl):
                n = len(tl)
                for u, rows, col, src in tl:
                    act.wait_ge(x_in[u], 16 * (pair + 1))
                    act.wait_ge(tr_done, 2 * (t0 + u))
                    nc.scalar.activation(xn[0:rows, u, :], x[0:rows, u, :], ACT.Square,
                                         accum_out=ss[0:rows, u:u + 1]).then_inc(sq_done, 1)
                rows = tl[-1][1]
                act.wait_ge(ms_done, pair + 1)
                nc.scalar.activation(rt[0:rows, 0:n], ms[0:rows, 0:n], ACT.Sqrt).then_inc(rt_done, 1)
                for u, rows, col, src in tl:
                    for j in range(2):
                        act.wait_ge(tr_done, 2 * (t0 + u) + j + 3)
                        bank = banks[2 * u + j]
                        nc.scalar.copy(hT_hi[:, 4 * j:4 * j + 4, ds(col, rows)],
                                       bank[:, :].rearrange("p (k n) -> p k n", k=4)[:, :, 0:rows]).then_inc(hi_done, 1)
            groups(act, body)

        @block.vector
        def _(dve):
            dve.sem_inc(xn_done, 1)
            dve.sem_inc(lo_done, 4)
            dve.wait_ge(g_in, 16)

            def body(pair, t0, tl):
                n, rows = len(tl), tl[-1][1]
                dve.wait_ge(sq_done, t0 + n)
                nc.vector.tensor_scalar(ms[0:rows, 0:n], ss[0:rows, 0:n], 1.0 / D, EPS, ALU.mult,
                                        ALU.add).then_inc(ms_done, 1)
                dve.wait_ge(rt_done, pair + 1)
                nc.vector.reciprocal(ri[0:rows, 0:n], rt[0:rows, 0:n]).then_inc(ri_done, 1)
                dve.wait_ge(ri_done, pair + 1)
                for u, rows, col, src in tl:
                    dve.wait_ge(tr_done, 2 * (t0 + u))
                    nc.vector.scalar_tensor_tensor(xn[0:rows, u, :], x[0:rows, u, :], ri[0:rows, u:u + 1],
                                                   g_bc[0:rows, :], ALU.mult, ALU.mult).then_inc(xn_done, 1)
                for u, rows, col, src in tl:
                    for j in range(2):
                        dve.wait_ge(hi_done, 2 * (t0 + u) + j + 1)
                        bank = banks[2 * u + j]
                        at = (slice(None), slice(4 * j, 4 * j + 4), ds(col, rows))
                        nc.vector.tensor_tensor(hT_lo[at], bank[:, :].rearrange("p (k n) -> p k n", k=4)[:, :, 0:rows],
                                                hT_hi[at].bitcast(F32), ALU.subtract).then_inc(lo_done, 1)
            groups(dve, body)

        @block.tensor
        def _(pe):
            pe.sem_inc(tr_done, 2)

            def body(pair, t0, tl):
                for u, rows, col, src in tl:
                    pe.wait_ge(xn_done, t0 + u + 2)
                    for j in range(2):
                        pe.wait_ge(lo_done, 2 * (t0 + u) + j + 1)
                        for k in range(4):
                            last = nc.tensor.transpose(banks[2 * u + j][:, k * P:k * P + rows],
                                                       xn[0:rows, u, (4 * j + k) * P:(4 * j + k + 1) * P],
                                                       ident[0:rows, 0:rows])
                        last.then_inc(tr_done, 1)
            groups(pe, body)


def project(nc, tag, banks, w, hT_hi, hT_lo, zT, segments, gate_cols=None, fT=None, bias_f=None):
    n_tiles = sum(seg[1] for seg in segments)
    n_pairs = n_tiles // 2
    with ExitStack() as s:
        c = Core(nc, s, tag)
        w_raw = c.sb("w_raw", [P, 2, KT, P])
        w_hi = c.sb("w_hi", [P, 2, KT, P], F32R)
        w_lo = c.sb("w_lo", [P, 2, KT, P], F32R)
        z_st = c.sb("z_st", [P, 2, TOK])
        w_in = [c.sem(f"w_loaded{u}") for u in range(2)]
        whi_done = c.sem("w_hi_done")
        wlo_done = c.sem("w_lo_done")
        z_done = c.sem("z_done")
        z_read = c.sem("z_read")
        z_out = [c.sem(f"z_stored{u}") for u in range(2)]
        if fT is not None:
            wf_raw = c.sb("wf_raw", [P, KT, FH])
            b_col = c.sb("b_col", [FH, 1])
            wf_in, b_in = c.sem("wf_loaded"), c.sem("bias_loaded")
        block = s.enter_context(nc.Block())
        w_v = w.rearrange("(k p) n -> p k n", p=P)

        def pairs(eng, body):
            base = 0
            for col0, n, row0, func in segments:
                with eng.Fori(0, n // 2) as i:
                    for u in range(2):
                        body(base // 2 + i, u, col0 + (2 * i + u) * P, row0 + (2 * i + u) * P, func)
                base += n

        @block.sync
        def _(sp):
            if fT is not None:
                sp.dma_start(wf_raw[:, :, :], w_v[:, :, gate_cols:gate_cols + FH]).then_inc(wf_in, 16)
                sp.dma_start(b_col[:, :], bias_f.unsqueeze(1)).then_inc(b_in, 16)

            def body(pair, u, col, row, func):
                sp.wait_ge(wlo_done, 2 * pair + u)
                sp.dma_start(w_raw[:, u, :, :], w_v[:, :, ds(col, P)]).then_inc(w_in[u], 16)
            pairs(sp, body)

        @block.vector
        def _(dve):
            dve.sem_inc(wlo_done, 1)

            def body(pair, u, col, row, func):
                dve.wait_ge(w_in[u], 16 * (pair + 1))
                dve.wait_ge(z_done, CH * (2 * pair + u + 1))
                nc.vector.tensor_copy(w_hi[:, u, :, :], w_raw[:, u, :, :]).then_inc(whi_done, 1)
                dve.wait_ge(whi_done, 2 * pair + u + 1)
                nc.vector.tensor_tensor(w_lo[:, u, :, :], w_raw[:, u, :, :], w_hi[:, u, :, :].bitcast(F32),
                                        ALU.subtract).then_inc(wlo_done, 1)
            pairs(dve, body)
            if fT is not None:
                dve.wait_ge(wf_in, 16)
                dve.wait_ge(z_done, CH * (n_tiles + 1))
                nc.vector.tensor_copy(w_hi[:, 0, :, 0:FH], wf_raw[:, :, :]).then_inc(whi_done, 1)
                dve.wait_ge(whi_done, n_tiles + 1)
                nc.vector.tensor_tensor(w_lo[:, 0, :, 0:FH], wf_raw[:, :, :], w_hi[:, 0, :, 0:FH].bitcast(F32),
                                        ALU.subtract).then_inc(wlo_done, 1)

        @block.tensor
        def _(pe):
            pe.sem_inc(z_done, 2 * CH)

            def chunk(hi, lo, ch):
                out = banks[ch][:, 0:CW]
                for k in range(KT):
                    h_h, h_l = hT_hi[:, k, ch * CW:(ch + 1) * CW], hT_lo[:, k, ch * CW:(ch + 1) * CW]
                    nc.tensor.matmul(out, hi[:, k, :], h_h, start=(k == 0), stop=False)
                    nc.tensor.matmul(out, hi[:, k, :], h_l, start=False, stop=False)
                    last = nc.tensor.matmul(out, lo[:, k, :], h_h, start=False, stop=(k == KT - 1))
                return last

            def body(pair, u, col, row, func):
                pe.wait_ge(wlo_done, 2 * pair + u + 2)
                for ch in range(CH):
                    pe.wait_ge(z_read, CH * (2 * pair + u) + ch + 1)
                    last = chunk(w_hi[:, u, :, :], w_lo[:, u, :, :], ch)
                    last.then_inc(z_done, 1)
            pairs(pe, body)
            if fT is not None:
                pe.wait_ge(wlo_done, n_tiles + 2)
                for ch in range(CH):
                    pe.wait_ge(z_read, CH * n_tiles + ch + 1)
                    chunk(w_hi[:, 0, :, :], w_lo[:, 0, :, :], ch).then_inc(z_done, 1)

        @block.scalar
        def _(act):
            act.sem_inc(z_read, CH)

            def body(pair, u, col, row, func):
                act.wait_ge(z_out[u], 16 * pair)
                for ch in range(CH):
                    act.wait_ge(z_done, CH * (2 * pair + u + 2) + ch + 1)
                    nc.scalar.activation(z_st[:, u, ch * CW:(ch + 1) * CW], banks[ch][:, 0:CW],
                                         func).then_inc(z_read, 1)
                act.wait_ge(z_read, CH + CH * (2 * pair + u) + CH)
                act.dma_start(zT[ds(row, P), :], z_st[:, u, :]).then_inc(z_out[u], 16)
            pairs(act, body)
            if fT is not None:
                act.wait_ge(b_in, 16)
                for ch in range(CH):
                    act.wait_ge(z_done, CH * (n_tiles + 2) + ch + 1)
                    nc.scalar.activation(fT[:, ch * CW:(ch + 1) * CW], banks[ch][0:FH, 0:CW], ACT.Identity,
                                         bias=b_col[:, :]).then_inc(z_read, 1)
            for u in range(2):
                act.wait_ge(z_out[u], 16 * n_pairs)


def forget_gates(nc, const, banks, fT, logf_cache, page_table, lf_prompt, lf_sample, cT, sufT, cnew, cnew_q):
    ident, ones = const["ident"], const["ones"]
    NPG = DB * PAGES
    with ExitStack() as s:
        c = Core(nc, s, "fg")
        upto = c.sb("upto", [P, P])
        after = c.sb("after", [P, P])
        mag = c.sb("mag", [FH, TOK])
        e = c.sb("e", [FH, TOK])
        low = c.sb("low", [FH, TOK])
        lfT = c.sb("lfT", [FH, TOK])
        lf = c.sb("lf", [P, NQ + 1, FH])
        pad = [c.sb(f"pad{n}", [P, NQ // 2 + NQ, FH]) for n in range(2)]
        past = [c.sb(f"past{n}", [P, DB, PAGES + PAGES // 2, FH]) for n in range(2)]
        past_e = c.sb("past_e", [P, DB * FH])
        lfp = c.sb("lfp", [P, PAGES, DB * FH])
        ex = c.sb("ex", [P, PAGES, DB * FH])
        c_row = c.sb("c_row", [FH, SEQ])
        suf_row = c.sb("suf_row", [DB * FH, SEQ])
        cn = c.sb("cn", [FH, 2, NS])
        ptab = c.sb("ptab", [1, NPG], I32)
        tri = c.sem("triangles_made")
        pt_in, past_in = c.sem("page_table_loaded"), c.sem("past_gates_loaded")
        act_d, dve_d = c.sem("act_steps"), c.sem("dve_steps")
        zer, scan_d, pscan_d = c.sem("zeroed"), c.sem("scan_steps"), c.sem("past_scan_steps")
        tr_d, lf_d, ct_d, suf_d = c.sem("gates_transposed"), c.sem("lf_ready"), c.sem("c_summed"), c.sem("suf_summed")
        row_d, cn_d, out_d = c.sem("rows_ready"), c.sem("cnew_ready"), c.sem("stored")
        block = s.enter_context(nc.Block())

        @block.sync
        def _(sp):
            sp.dma_start(ptab[:, :], page_table.rearrange("(o b) n -> o (b n)", o=1)).then_inc(pt_in, 16)
            sp.wait_ge(pt_in, 16)
            sp.wait_ge(zer, 4)
            for b in range(DB):
                with sp.Fori(0, PAGES) as n:
                    page = sp.value_load(ptab[0:1, ds(b * PAGES + n, 1)], min_val=0, max_val=logf_cache.shape[0] - 1)
                    sp.dma_start(past[0][:, b, ds(n, 1), :].rearrange("p o h -> p (o h)"),
                                 logf_cache[ds(page, 1), :, :].rearrange("o p h -> (o p) h")).then_inc(past_in, 16)
            sp.wait_ge(lf_d, 2)
            sp.dma_start(lf_prompt.rearrange("n p h -> p n h"), lf[:, 0:NQ, :]).then_inc(out_d, 16)
            sp.dma_start(lf_sample.rearrange("b t h -> (b t) h"), lf[0:NS, NQ, :]).then_inc(out_d, 16)
            sp.wait_ge(cn_d, TN + 1)
            sp.dma_start(cnew[:, :], cn[:, 0, :]).then_inc(out_d, 16)
            sp.dma_start(cnew_q.rearrange("h (t b) -> h t b", t=TN),
                         cn[:, 1, :].rearrange("h (t b) -> h t b", t=TN)).then_inc(out_d, 16)
            sp.wait_ge(row_d, 4)
            sp.dma_start(cT[:, :], c_row[:, :]).then_inc(out_d, 16)
            sp.wait_ge(row_d, 8)
            for q in range(TN):
                sp.dma_start(sufT.rearrange("(r q) n -> q r n", q=TN)[q], suf_row[:, :]).then_inc(out_d, 16)
            sp.wait_ge(out_d, 16 * (5 + TN))

        @block.gpsimd
        def _(pool):
            nc.gpsimd.memset(upto[:, :], 1.0).then_inc(tri, 1)
            nc.gpsimd.memset(after[:, :], 1.0).then_inc(tri, 1)
            nc.gpsimd.memset(pad[0][:, :, :], 0.0).then_inc(zer, 1)
            nc.gpsimd.memset(pad[1][:, :, :], 0.0).then_inc(zer, 1)
            nc.gpsimd.memset(past[0][:, :, :, :], 0.0).then_inc(zer, 1)
            nc.gpsimd.memset(past[1][:, :, :, :], 0.0).then_inc(zer, 1)
            pool.wait_ge(tri, 2)
            nc.gpsimd.affine_select(out=upto[:, :], in_=upto[:, :], compare_op=ALU.is_ge, fill=0.0, base=0,
                                    pattern=[[1, P]], channel_multiplier=-1).then_inc(tri, 1)
            nc.gpsimd.affine_select(out=after[:, :], in_=after[:, :], compare_op=ALU.is_gt, fill=0.0, base=0,
                                    pattern=[[-1, P]], channel_multiplier=1).then_inc(tri, 1)
            pool.wait_ge(tri, 4)

        @block.scalar
        def _(act):
            nc.scalar.activation(mag[:, :], fT[:, :], ACT.Abs).then_inc(act_d, 1)
            act.wait_ge(act_d, 1)
            nc.scalar.activation(e[:, :], mag[:, :], ACT.Exp, scale=-1.0).then_inc(act_d, 1)
            act.wait_ge(act_d, 2)
            nc.scalar.activation(e[:, :], e[:, :], ACT.Ln, bias=1.0).then_inc(act_d, 1)
            for n in range(4):
                act.wait_ge(ct_d, n + 1)
                nc.scalar.copy(c_row[:, n * 512:(n + 1) * 512], banks[n][0:FH, :]).then_inc(row_d, 1)
            for n in range(4):
                act.wait_ge(suf_d, n + 1)
                nc.scalar.copy(suf_row[:, n * 512:(n + 1) * 512], banks[4 + n % 2][0:DB * FH, :]).then_inc(row_d, 1)

        @block.vector
        def _(dve):
            nc.vector.tensor_scalar_min(low[:, :], fT[:, :], 0.0).then_inc(dve_d, 1)
            dve.wait_ge(dve_d, 1)
            dve.wait_ge(act_d, 3)
            nc.vector.tensor_sub(lfT[:, :], low[:, :], e[:, :]).then_inc(dve_d, 1)
            dve.wait_ge(dve_d, 2)
            news = lfT[:, SEQ:TOK].rearrange("h (b t) -> h b t", t=TN)
            sums = cn[:, 0, :].rearrange("h (b t) -> h b t", t=TN)
            nc.vector.tensor_copy(sums[:, :, 0], news[:, :, 0]).then_inc(cn_d, 1)
            for t in range(1, TN):
                dve.wait_ge(cn_d, t)
                nc.vector.tensor_add(sums[:, :, t], sums[:, :, t - 1], news[:, :, t]).then_inc(cn_d, 1)
            dve.wait_ge(cn_d, TN)
            nc.vector.tensor_copy(cn[:, 1, :].rearrange("h (t b) -> h b t", t=TN), sums).then_inc(cn_d, 1)
            dve.wait_ge(tr_d, 1)
            gates = banks[6][:, 0:(NQ + 1) * FH].rearrange("p (n h) -> p n h", h=FH)
            nc.vector.tensor_copy(lf[:, 0:NQ, :], gates[:, 0:NQ, :]).then_inc(lf_d, 1)
            nc.vector.tensor_copy(lf[0:NS, NQ, :], gates[0:NS, NQ, :]).then_inc(lf_d, 1)
            dve.wait_ge(lf_d, 2)
            dve.wait_ge(zer, 4)
            Z = NQ // 2
            nc.vector.tensor_copy(pad[0][:, Z:, :], lf[:, 0:NQ, :]).then_inc(scan_d, 1)
            for n, step in enumerate((1, 2, 4, 8)):
                dve.wait_ge(scan_d, n + 1)
                nc.vector.tensor_add(pad[(n + 1) % 2][:, Z:, :], pad[n % 2][:, Z:, :],
                                     pad[n % 2][:, Z - step:Z - step + NQ, :]).then_inc(scan_d, 1)
            dve.wait_ge(past_in, 16 * NPG)
            nc.vector.tensor_copy(lfp[:, :, :].rearrange("p n (b h) -> p b n h", b=DB),
                                  past[0][:, :, 0:PAGES, :]).then_inc(pscan_d, 1)
            for n, step in enumerate((1, 2, 4, 8)):
                dve.wait_ge(pscan_d, n + 1)
                nc.vector.tensor_add(past[(n + 1) % 2][:, :, 0:PAGES, :], past[n % 2][:, :, 0:PAGES, :],
                                     past[n % 2][:, :, step:step + PAGES, :]).then_inc(pscan_d, 1)
            dve.wait_ge(pscan_d, 5)
            nc.vector.tensor_copy(ex[:, :, :].rearrange("p n (b h) -> p b n h", b=DB),
                                  past[0][:, :, 1:PAGES + 1, :]).then_inc(pscan_d, 1)

        @block.tensor
        def _(pe):
            pe.wait_ge(dve_d, 2)
            for n in range(NQ + 1):
                rows = min(P, TOK - n * P)
                last = nc.tensor.transpose(banks[6][0:rows, n * FH:(n + 1) * FH], lfT[:, n * P:n * P + rows],
                                           ident[0:FH, 0:FH])
            last.then_inc(tr_d, 1)
            pe.wait_ge(scan_d, 5)
            pe.wait_ge(tri, 4)
            Z = NQ // 2
            for n in range(NQ):
                out = banks[n // 4][0:FH, n % 4 * P:(n % 4 + 1) * P]
                nc.tensor.matmul(out, lf[:, n, :], upto[:, :], start=True, stop=False)
                last = nc.tensor.matmul(out, pad[0][:, Z - 1 + n, :], ones[:, :], start=False, stop=True)
                if n % 4 == 3:
                    last.then_inc(ct_d, 1)
            pe.wait_ge(pscan_d, 6)
            for n in range(PAGES):
                g = n // 4
                if n % 4 == 0 and g >= 2:
                    pe.wait_ge(row_d, 4 + g - 1)
                out = banks[4 + g % 2][0:DB * FH, n % 4 * P:(n % 4 + 1) * P]
                nc.tensor.matmul(out, lfp[:, n, :], after[:, :], start=True, stop=False)
                last = nc.tensor.matmul(out, ex[:, n, :], ones[:, :], start=False, stop=True)
                if n % 4 == 3:
                    last.then_inc(suf_d, 1)


def fox_attention(nc, const, banks, zT, cT, bT, k_out, v_out):
    ident, ones, ident_b, mask_b = (const[n] for n in ("ident", "ones", "ident_b", "mask_b"))
    NCH = NQ // 4
    pieces = [(q + 4) // 4 for q in range(NQ)]
    first = [sum(pieces[:q]) for q in range(NQ + 1)]
    NP = first[NQ]
    TG = 8
    S_BANKS, T_BANKS = banks[0:4], banks[4:6]
    O_BANK, R_BANK = banks[6], banks[7]
    NB = 4
    LAG = 2
    with ExitStack() as s:
        c = Core(nc, s, "fa")
        q_raw, k_raw, v_raw = (c.sb(n, [P, SEQ]) for n in ("q_raw", "k_raw", "v_raw"))
        q_hi, q_lo, k_hi, k_lo = (c.sb(n, [P, SEQ], F32R) for n in ("q_hi", "q_lo", "k_hi", "k_lo"))
        v_hi, v_lo = (c.sb(n, [P, NQ, P], F32R) for n in ("v_hi", "v_lo"))
        c_bc = c.sb("c_bc", [P, SEQ])
        decay = c.sb("decay", [P, SEQ])
        tok = c.sb("tok", [P, 4, 4, P])
        sc = c.sb("sc", [P, NB, SEQ])
        pT_hi, pT_lo = (c.sb(n, [P, NQ, 512], F32R) for n in ("pT_hi", "pT_lo"))
        gate = c.sb("gate", [P, 2, 512])
        mix = c.sb("mix", [P, 2, 512])
        mx = c.sb("mx", [P, NB, 4])
        nm = c.sb("nm", [P, NB])
        rs = c.sb("rs", [P, 2, 4])
        rr = c.sb("rr", [P, 2, 4])
        dg = c.sb("dg", [P, 4, P])

        q_in, k_in, v_in, c_in = (c.sem(n) for n in ("q_loaded", "k_loaded", "v_loaded", "c_loaded"))
        g_in = [c.sem(f"gate_loaded{n}") for n in range(2)]
        hi_d = c.sem("qk_hi_done")
        lo_d = c.sem("qk_lo_done")
        kvt = c.sem("kv_transposed")
        kve = c.sem("kv_tokens_ready")
        vhi, vlo = c.sem("v_hi_done"), c.sem("v_lo_done")
        tok_out = [c.sem(f"tokens_stored{n}") for n in range(4)]
        dec_d = c.sem("decay_ready")
        s_done = c.sem("scores_done")
        seen = c.sem("scores_seen")
        s_used = c.sem("scores_used")
        nm_d = c.sem("maxima_ready")
        p_done = c.sem("exp_done")
        t_done = c.sem("p_transposed")
        th_d = c.sem("pT_hi_done")
        tl_d = c.sem("pT_lo_done")
        rr_d = c.sem("row_inverse_ready")
        dg_d = c.sem("diagonals_ready")
        r_done = c.sem("inverse_spread")
        o_done = c.sem("pv_done")
        gr_d = c.sem("gate_scaled")
        mix_d = c.sem("mix_ready")
        mix_out = [c.sem(f"mix_stored{n}") for n in range(2)]
        block = s.enter_context(nc.Block())

        @block.sync
        def _(sp):
            with sp.Fori(0, FH) as h:
                sp.wait_ge(lo_d, 2 * h)
                sp.dma_start(q_raw[:, :], zT[ds(h * P, P), 0:SEQ]).then_inc(q_in, 16)
                sp.wait_ge(kvt, TG * h)
                sp.dma_start(k_raw[:, :], zT[ds(FH * P + h * P, P), 0:SEQ]).then_inc(k_in, 16)
                sp.dma_start(v_raw[:, :], zT[ds(2 * FH * P + h * P, P), 0:SEQ]).then_inc(v_in, 16)
                sp.wait_ge(dec_d, NCH * h)
                sp.dma_start(c_bc[:, :], cT[ds(h, 1), :].rearrange("o n -> (o n)").partition_broadcast(P)).then_inc(c_in, 16)
                for j in range(NCH):
                    sp.wait_ge(mix_d, NCH * h + j)
                    sp.dma_start(gate[:, j % 2, :], zT[ds(3 * D + XW + h * P, P), 512 * j:512 * (j + 1)]).then_inc(g_in[j % 2], 16)

        @block.gpsimd
        def _(pool):
            with pool.Fori(0, FH) as h:
                for j in range(NCH):
                    pool.wait_ge(rr_d, NCH * h + j + 1)
                    pool.wait_ge(r_done, NCH * h + j)
                    nc.gpsimd.tensor_tensor(dg[:, :, :], ident[:, :].unsqueeze(1).broadcast_to([P, 4, P]),
                                            rr[:, j % 2, :].unsqueeze(2).broadcast_to([P, 4, P]), ALU.mult).then_inc(dg_d, 1)
                    pool.wait_ge(mix_d, NCH * h + j + 2)
                    pool.dma_start(bT[ds(h * P, P), 512 * j:512 * (j + 1)], mix[:, j % 2, :]).then_inc(mix_out[j % 2], 16)
            for n in range(2):
                pool.wait_ge(mix_out[n], 16 * FH * NCH // 2)

        def steps():
            for q in range(NQ + LAG + 1):
                yield q if q < NQ else None, q - LAG if LAG <= q < NQ + LAG else None, (
                    (q - LAG - 4) // 4 if q >= LAG + 4 and (q - LAG) % 4 == 0 else None)

        @block.tensor
        def _(pe):
            pe.sem_inc(t_done, NP)
            with pe.Fori(0, FH) as h:
                for g in range(TG):
                    raw = k_raw if g < 4 else v_raw
                    if g == 0:
                        pe.wait_ge(k_in, 16 * (h + 1))
                        pe.wait_ge(tl_d, NP * h + 2)
                    if g == 4:
                        pe.wait_ge(v_in, 16 * (h + 1))
                    if g >= 2:
                        pe.wait_ge(kve, TG * h + g - 1)
                    for n in range(4):
                        last = nc.tensor.transpose(T_BANKS[g % 2][:, n * P:(n + 1) * P],
                                                   raw[:, (g % 4 * 4 + n) * P:(g % 4 * 4 + n + 1) * P], ident[:, :])
                    last.then_inc(kvt, 1)
                pe.wait_ge(lo_d, 2 * h + 2)
                for qs, qt, j in steps():
                    if j is not None:
                        pe.wait_ge(dg_d, NCH * h + j + 1)
                        pe.wait_ge(mix_d, NCH * h + j + 1)
                        nc.tensor.matmul(R_BANK[:, :], ones[:, :], dg[:, :, :].rearrange("p a n -> p (a n)"),
                                         start=True, stop=True).then_inc(r_done, 1)
                        pe.wait_ge(tl_d, NP * h + first[4 * j + 4] + 2)
                        if j == 0:
                            pe.wait_ge(vlo, 4 * h + 4)
                        for n in range(4 * j + 4):
                            c0 = max(0, n - 4 * j) * P
                            out = O_BANK[:, c0:512]
                            nc.tensor.matmul(out, v_hi[:, n, :], pT_hi[:, n, c0:512], start=(n == 0), stop=False)
                            nc.tensor.matmul(out, v_lo[:, n, :], pT_hi[:, n, c0:512], start=False, stop=False)
                            last = nc.tensor.matmul(out, v_hi[:, n, :], pT_lo[:, n, c0:512], start=False,
                                                    stop=(n == 4 * j + 3))
                        last.then_inc(o_done, 1)
                    for p in range(max(pieces[qs] if qs is not None else 0, pieces[qt] if qt is not None else 0)):
                        if qs is not None and p < pieces[qs]:
                            g = first[qs] + p
                            k0, w = 512 * p, min(512, (qs + 1) * P - 512 * p)
                            out = S_BANKS[g % 4][:, 0:w]
                            qh, ql = q_hi[:, qs * P:(qs + 1) * P], q_lo[:, qs * P:(qs + 1) * P]
                            last_piece = p == pieces[qs] - 1
                            pe.wait_ge(s_used, NP * h + g + 1)
                            nc.tensor.matmul(out, qh, k_hi[:, k0:k0 + w], start=True, stop=False)
                            nc.tensor.matmul(out, ql, k_hi[:, k0:k0 + w], start=False, stop=False)
                            last = nc.tensor.matmul(out, qh, k_lo[:, k0:k0 + w], start=False, stop=not last_piece)
                            if last_piece:
                                last = nc.tensor.matmul(out[:, w - P:w], ident_b[:, :], mask_b[:, :], start=False, stop=True)
                            last.then_inc(s_done, 1)
                        if qt is not None and p < pieces[qt]:
                            g = first[qt] + p
                            if p == 0:
                                pe.wait_ge(p_done, NQ * h + qt + 1)
                            if g < 2:
                                pe.wait_ge(kve, TG * h + TG - 1 + g)
                            else:
                                pe.wait_ge(tl_d, NP * h + g + 1)
                            for n in range(min(4, qt + 1 - 4 * p)):
                                last = nc.tensor.transpose(T_BANKS[g % 2][:, n * P:(n + 1) * P],
                                                           sc[:, qt % NB, (4 * p + n) * P:(4 * p + n + 1) * P], ident[:, :])
                            last.then_inc(t_done, 1)

        @block.scalar
        def _(act):
            with act.Fori(0, FH) as h:
                act.wait_ge(s_done, NP * h)
                act.wait_ge(q_in, 16 * (h + 1))
                nc.scalar.activation(q_hi[:, :], q_raw[:, :], ACT.Copy, scale=SCALE).then_inc(hi_d, 1)
                act.wait_ge(k_in, 16 * (h + 1))
                nc.scalar.activation(k_hi[:, :], k_raw[:, :], ACT.Copy).then_inc(hi_d, 1)
                for g in range(TG):
                    act.wait_ge(kvt, TG * h + g + 1)
                    n = g % 4
                    act.wait_ge(tok_out[n], 16 * (2 * h + g // 4))
                    if g < 4:
                        act.wait_ge(vlo, 4 * h)
                    nc.scalar.copy(tok[:, n, :, :], T_BANKS[g % 2][:, :].rearrange("p (n d) -> p n d", n=4)).then_inc(kve, 1)
                    act.wait_ge(kve, TG * h + g + 1)
                    dst = (k_out if g < 4 else v_out)[4 * n:4 * n + 4, :, ds(h, 1), :]
                    act.dma_start(dst.rearrange("n p o d -> p n (o d)"), tok[:, n, :, :]).then_inc(tok_out[n], 16)
                for qs, qt, j in steps():
                    if qt is not None:
                        for p in range(pieces[qt]):
                            g = first[qt] + p
                            a, jt = qt % 4, qt // 4
                            nk = min(4, qt + 1 - 4 * p)
                            act.wait_ge(t_done, NP + NP * h + g + 1)
                            if p == 0:
                                act.wait_ge(o_done, NCH * h + jt)
                            nc.scalar.copy(pT_hi[:, 4 * p:4 * p + nk, a * P:(a + 1) * P],
                                           T_BANKS[g % 2][:, 0:nk * P].rearrange("p (n q) -> p n q", q=P)).then_inc(th_d, 1)
                    if qs is not None:
                        act.wait_ge(nm_d, NQ * h + qs + 1)
                        w = (qs + 1) * P
                        nc.scalar.activation(sc[:, qs % NB, 0:w], sc[:, qs % NB, 0:w], ACT.Exp,
                                             bias=nm[:, qs % NB:qs % NB + 1],
                                             accum_out=rs[:, qs // 4 % 2, qs % 4:qs % 4 + 1]).then_inc(p_done, 1)
            for n in range(4):
                act.wait_ge(tok_out[n], 16 * 2 * FH)

        @block.vector
        def _(dve):
            dve.sem_inc(s_used, 4)
            dve.sem_inc(tl_d, 2)
            dve.sem_inc(mix_d, 1)
            with dve.Fori(0, FH) as h:
                dve.wait_ge(hi_d, 2 * h + 1)
                nc.vector.scalar_tensor_tensor(q_lo[:, :], q_raw[:, :], SCALE, q_hi[:, :].bitcast(F32), ALU.mult,
                                               ALU.subtract).then_inc(lo_d, 1)
                dve.wait_ge(hi_d, 2 * h + 2)
                nc.vector.tensor_tensor(k_lo[:, :], k_raw[:, :], k_hi[:, :].bitcast(F32), ALU.subtract).then_inc(lo_d, 1)
                dve.wait_ge(c_in, 16 * (h + 1))
                for qs, qt, j in steps():
                    if j is not None:
                        dve.wait_ge(r_done, NCH * h + j + 1)
                        dve.wait_ge(g_in[j % 2], 16 * (NCH // 2 * h + j // 2 + 1))
                        nc.vector.tensor_tensor(gate[:, j % 2, :], gate[:, j % 2, :], R_BANK[:, :], ALU.mult).then_inc(gr_d, 1)
                        dve.wait_ge(gr_d, NCH * h + j + 1)
                        dve.wait_ge(o_done, NCH * h + j + 1)
                        dve.wait_ge(mix_out[j % 2], 16 * (NCH // 2 * h + j // 2))
                        nc.vector.tensor_tensor(mix[:, j % 2, :], gate[:, j % 2, :], O_BANK[:, :], ALU.mult).then_inc(mix_d, 1)
                    if qs is not None and qs % 4 == 0:
                        jn, w = qs // 4, 512 * (qs // 4 + 1)
                        dve.wait_ge(s_used, 4 + NP * h + first[qs])
                        nc.vector.tensor_scalar(decay[:, 0:w], c_bc[:, 0:w], c_bc[:, qs * P:qs * P + 1], -1.0,
                                                ALU.subtract, ALU.mult).then_inc(dec_d, 1)
                        dve.wait_ge(dec_d, NCH * h + jn + 1)
                    for p in range(max(pieces[qs] if qs is not None else 0, pieces[qt] if qt is not None else 0)):
                        if qs is not None and p < pieces[qs]:
                            g, b = first[qs] + p, qs % NB
                            k0, w = 512 * p, min(512, (qs + 1) * P - 512 * p)
                            if p == 0:
                                dve.wait_ge(t_done, NP * h + (NP + first[qs - NB + 1] if qs >= NB else first[qs + NQ - NB + 1]))
                            dve.wait_ge(s_done, NP * h + g + 1)
                            dve.sem_inc(seen, 1)
                            nc.vector.tensor_tensor_reduce(out=sc[:, b, k0:k0 + w], in0=S_BANKS[g % 4][:, 0:w],
                                                           in1=decay[:, k0:k0 + w], scale=1.0, scalar=LOWEST, op0=ALU.add,
                                                           op1=ALU.max, accum_out=mx[:, b, p:p + 1]).then_inc(s_used, 1)
                        if qt is not None and p < pieces[qt]:
                            g = first[qt] + p
                            a = qt % 4
                            nk = min(4, qt + 1 - 4 * p)
                            at = (slice(None), slice(4 * p, 4 * p + nk), slice(a * P, (a + 1) * P))
                            dve.wait_ge(th_d, NP * h + g + 1)
                            nc.vector.tensor_tensor(pT_lo[at], T_BANKS[g % 2][:, 0:nk * P].rearrange("p (n q) -> p n q", q=P),
                                                    pT_hi[at].bitcast(F32), ALU.subtract).then_inc(tl_d, 1)
                        if qs is not None and p == pieces[qs] - 1:
                            b = qs % NB
                            dve.wait_ge(s_used, 4 + NP * h + first[qs + 1])
                            nc.vector.tensor_reduce(nm[:, b:b + 1], mx[:, b, 0:pieces[qs]], axis=AX.X, op=ALU.max,
                                                    negate=True).then_inc(nm_d, 1)
                    if qs is None or qs % 4 == 0:
                        if qs is not None and qs == 0:
                            continue
                        jr = (qs if qs is not None else NQ) // 4 - 1
                        if qs is None and qt != NQ - LAG:
                            continue
                        dve.wait_ge(p_done, NQ * h + 4 * jr + 4)
                        nc.vector.reciprocal(rr[:, jr % 2, :], rs[:, jr % 2, :]).then_inc(rr_d, 1)
                    if qs is not None and qs % 4 == 1 and qs < 4:
                        for n in range(4):
                            dve.wait_ge(kve, TG * h + 4 + n + 1)
                            dve.wait_ge(o_done, NCH * h)
                            nc.vector.tensor_copy(v_hi[:, 4 * n:4 * n + 4, :], tok[:, n, :, :]).then_inc(vhi, 1)
                            dve.wait_ge(vhi, 4 * h + n + 1)
                            nc.vector.tensor_tensor(v_lo[:, 4 * n:4 * n + 4, :], tok[:, n, :, :],
                                                    v_hi[:, 4 * n:4 * n + 4, :].bitcast(F32), ALU.subtract).then_inc(vlo, 1)


def memory_kv(nc, tag, const, banks, mem, gain, w, k_out, v_out):
    NT = NM // P
    with ExitStack() as outer:
        m = Core(nc, outer, tag)
        mT_hi, mT_lo = (m.sb(n, [P, KT, NM], F32R) for n in ("mT_hi", "mT_lo"))
        norm_transpose(nc, tag + "n", const, banks, (None, [(mem[0:P, :], P, 0), (mem[P:NM, :], P, P)]), gain, mT_hi, mT_lo)
        with ExitStack() as s:
            c = Core(nc, s, tag + "p")
            raw = c.sb("raw", [P, 2, 2 * XW])
            w_hi, w_lo = (c.sb(n, [P, KT, 2 * XW], F32R) for n in ("w_hi", "w_lo"))
            kv = c.sb("kv", [P, NT, 2, XW])
            w_in = [c.sem(f"w_loaded{n}") for n in range(2)]
            hi_d, lo_d = c.sem("w_hi_done"), c.sem("w_lo_done")
            mm, ev, out_d = c.sem("multiplied"), c.sem("copied"), c.sem("stored")
            block = s.enter_context(nc.Block())

            @block.sync
            def _(sp):
                for k in range(KT):
                    if k >= 2:
                        sp.wait_ge(lo_d, k - 1)
                    sp.dma_start(raw[:, k % 2, :], w[k * P:(k + 1) * P, :]).then_inc(w_in[k % 2], 16)
                for t in range(NT):
                    for half, dst in enumerate((k_out, v_out)):
                        sp.wait_ge(ev, 2 * t + half + 1)
                        sp.dma_start(dst[t * P:(t + 1) * P, :], kv[:, t, half, :]).then_inc(out_d, 16)
                sp.wait_ge(out_d, 16 * 2 * NT)

            @block.vector
            def _(dve):
                for k in range(KT):
                    dve.wait_ge(w_in[k % 2], 16 * (k // 2 + 1))
                    nc.vector.tensor_copy(w_hi[:, k, :], raw[:, k % 2, :]).then_inc(hi_d, 1)
                    dve.wait_ge(hi_d, k + 1)
                    nc.vector.tensor_tensor(w_lo[:, k, :], raw[:, k % 2, :], w_hi[:, k, :].bitcast(F32),
                                            ALU.subtract).then_inc(lo_d, 1)

            @block.tensor
            def _(pe):
                for k in range(KT):
                    pe.wait_ge(lo_d, k + 1)
                    for t in range(NT):
                        for half in range(2):
                            out = banks[2 * t + half][:, :]
                            cols = slice(half * XW, (half + 1) * XW)
                            a_hi, a_lo = mT_hi[:, k, t * P:(t + 1) * P], mT_lo[:, k, t * P:(t + 1) * P]
                            nc.tensor.matmul(out, a_hi, w_hi[:, k, cols], start=(k == 0), stop=False)
                            nc.tensor.matmul(out, a_lo, w_hi[:, k, cols], start=False, stop=False)
                            last = nc.tensor.matmul(out, a_hi, w_lo[:, k, cols], start=False, stop=(k == KT - 1))
                            if k == KT - 1:
                                last.then_inc(mm, 1)

            @block.scalar
            def _(act):
                for n in range(2 * NT):
                    act.wait_ge(mm, n + 1)
                    nc.scalar.copy(kv[:, n // 2, n % 2, :], banks[n][:, :]).then_inc(ev, 1)


def memory_attention(nc, tag, const, banks, zT, xq_row, gate_row, bT, k_mem, v_mem):
    ident, ones = const["ident"], const["ones"]
    NT = NM // P
    NCH, NPR = NQ // 4, NQ // 2
    S_BANKS, T_BANKS, O_BANKS, R_BANK, K_BANK = banks[0:2], banks[2:4], banks[4:6], banks[6], banks[7]
    with ExitStack() as s:
        c = Core(nc, s, tag)
        kv_raw = c.sb("kv_raw", [P, 2, NT, XW])
        k_hi, k_lo = (c.sb(n, [P, XH, NM], F32R) for n in ("k_hi", "k_lo"))
        v_hi, v_lo = (c.sb(n, [P, NT, XW], F32R) for n in ("v_hi", "v_lo"))
        q_raw = c.sb("q_raw", [P, 2, 512])
        q_hi, q_lo = (c.sb(n, [P, 2, 512], F32R) for n in ("q_hi", "q_lo"))
        gate, mix = c.sb("gate", [P, 2, 512]), c.sb("mix", [P, 2, 512])
        pr = c.sb("pr", [P, 2, 2, NM])
        pT_hi, pT_lo = (c.sb(n, [P, 2, NT, 512], F32R) for n in ("pT_hi", "pT_lo"))
        nm, rs = c.sb("nm", [P, 2, 2]), c.sb("rs", [P, 2, 4])
        rr, dg = c.sb("rr", [P, 2, 4]), c.sb("dg", [P, 4, P])
        kx = c.sb("kx", [P, 2, NM], F32R)
        vx = c.sb("vx", [P, 2, NT, P], F32R)
        head_part, head_d = c.sem("head_part_copied"), c.sem("head_ready")
        kv_in, kt_d, khi_d, klo_d = (c.sem(n) for n in ("kv_loaded", "k_transposed", "k_hi_done", "k_lo_done"))
        vhi_d, vlo_d = c.sem("v_hi_done"), c.sem("v_lo_done")
        q_in, g_in, mix_out = ([c.sem(f"{n}{u}") for u in range(2)] for n in ("q_loaded", "gate_loaded", "mix_stored"))
        qhi_d, qlo_d = c.sem("q_hi_done"), c.sem("q_lo_done")
        s_done, nm_d, p_done, t_done, th_d, tl_d = (c.sem(n) for n in (
            "scores_done", "maxima_ready", "exp_done", "p_transposed", "pT_hi_done", "pT_lo_done"))
        rr_d, dg_d, r_done, o_done, gr_d, mix_d = (c.sem(n) for n in (
            "row_inverse_ready", "diagonals_ready", "inverse_spread", "pv_done", "gate_scaled", "mix_ready"))
        block = s.enter_context(nc.Block())

        @block.sync
        def _(sp):
            sp.dma_start(kv_raw[:, 0, :, :], k_mem.rearrange("(t p) n -> p t n", p=P)).then_inc(kv_in, 16)
            sp.dma_start(kv_raw[:, 1, :, :], v_mem.rearrange("(t p) n -> p t n", p=P)).then_inc(kv_in, 16)
            with sp.Fori(0, XH) as h:
                for j in range(NCH):
                    sp.wait_ge(qlo_d, NCH * h + j)
                    sp.dma_start(q_raw[:, j % 2, :], zT[ds(xq_row + h * P, P), 512 * j:512 * (j + 1)]).then_inc(q_in[j % 2], 16)
                    sp.wait_ge(mix_d, NCH * h + j)
                    sp.dma_start(gate[:, j % 2, :], zT[ds(gate_row + h * P, P), 512 * j:512 * (j + 1)]).then_inc(g_in[j % 2], 16)

        @block.gpsimd
        def _(pool):
            with pool.Fori(0, XH) as h:
                for j in range(NCH):
                    pool.wait_ge(rr_d, NCH * h + j + 1)
                    pool.wait_ge(r_done, NCH * h + j)
                    nc.gpsimd.tensor_tensor(dg[:, :, :], ident[:, :].unsqueeze(1).broadcast_to([P, 4, P]),
                                            rr[:, j % 2, :].unsqueeze(2).broadcast_to([P, 4, P]), ALU.mult).then_inc(dg_d, 1)
                    pool.wait_ge(mix_d, NCH * h + j + 2)
                    pool.dma_start(bT[ds(D + h * P, P), 512 * j:512 * (j + 1)], mix[:, j % 2, :]).then_inc(mix_out[j % 2], 16)
            for n in range(2):
                pool.wait_ge(mix_out[n], 16 * XH * NCH // 2)

        def scores(pe, h, n):
            if n % 2 == 0:
                pe.wait_ge(qlo_d, NCH * h + n // 2 + 2)
            pe.wait_ge(p_done, 2 * (NPR * h + n))
            for a in range(2):
                cols = slice((n % 2 * 2 + a) * P, (n % 2 * 2 + a + 1) * P)
                qh, ql = q_hi[:, n // 2 % 2, cols], q_lo[:, n // 2 % 2, cols]
                out = S_BANKS[n % 2][:, a * NM:(a + 1) * NM]
                yield out, qh, ql

        @block.tensor
        def _(pe):
            pe.sem_inc(s_done, 2)
            pe.sem_inc(t_done, 2)
            pe.sem_inc(o_done, 2)
            pe.wait_ge(kv_in, 32)
            for n in range(XH // 2):
                if n >= 1:
                    pe.wait_ge(klo_d, n)
                for a in range(2):
                    for t in range(NT):
                        h = 2 * n + a
                        last = nc.tensor.transpose(K_BANK[:, a * NM + t * P:a * NM + (t + 1) * P],
                                                   kv_raw[:, 0, t, h * P:(h + 1) * P], ident[:, :])
                last.then_inc(kt_d, 1)
            pe.wait_ge(klo_d, XH // 2)
            pe.wait_ge(vlo_d, 1)

            with pe.Fori(0, XH) as h:
                pe.wait_ge(head_d, h + 1)
                for n in range(NPR + 2):
                    if n < NPR:
                        for a, (out, qh, ql) in enumerate(scores(pe, h, n)):
                            nc.tensor.matmul(out, qh, kx[:, 0, :], start=True, stop=False)
                            nc.tensor.matmul(out, ql, kx[:, 0, :], start=False, stop=False)
                            last = nc.tensor.matmul(out, qh, kx[:, 1, :], start=False, stop=True)
                        last.then_inc(s_done, 1)
                    if n >= 3 and n % 2 == 1:
                        j = (n - 3) // 2
                        jj = NCH * h + j
                        pe.wait_ge(tl_d, NPR * h + 2 * j + 2 + 2)
                        pe.wait_ge(mix_d, jj + 1)
                        out = O_BANKS[j % 2][:, :]
                        for t in range(NT):
                            nc.tensor.matmul(out, vx[:, 0, t, :], pT_hi[:, j % 2, t, :], start=(t == 0), stop=False)
                            nc.tensor.matmul(out, vx[:, 1, t, :], pT_hi[:, j % 2, t, :], start=False, stop=False)
                            last = nc.tensor.matmul(out, vx[:, 0, t, :], pT_lo[:, j % 2, t, :], start=False, stop=(t == NT - 1))
                        last.then_inc(o_done, 1)
                        pe.wait_ge(dg_d, jj + 1)
                        pe.wait_ge(gr_d, jj)
                        nc.tensor.matmul(R_BANK[:, :], ones[:, :], dg[:, :, :].rearrange("p a n -> p (a n)"),
                                         start=True, stop=True).then_inc(r_done, 1)
                    if 1 <= n <= NPR:
                        m = n - 1
                        pe.wait_ge(p_done, 2 * (NPR * h + m) + 2 + 2)
                        pe.wait_ge(tl_d, NPR * h + m + 1)
                        for t in range(NT):
                            for a in range(2):
                                last = nc.tensor.transpose(T_BANKS[m % 2][:, (2 * t + a) * P:(2 * t + a + 1) * P],
                                                           pr[:, m % 2, a, t * P:(t + 1) * P], ident[:, :])
                        last.then_inc(t_done, 1)

        @block.scalar
        def _(act):
            act.sem_inc(p_done, 2)
            for n in range(XH // 2):
                act.wait_ge(kt_d, n + 1)
                nc.scalar.copy(k_hi[:, 2 * n:2 * n + 2, :], K_BANK[:, :].rearrange("p (a m) -> p a m", a=2)).then_inc(khi_d, 1)
            with act.Fori(0, XH) as h:
                for n in range(NPR + 2):
                    if n < NPR:
                        if n % 2 == 0:
                            j = n // 2
                            act.wait_ge(q_in[j % 2], 16 * (NCH // 2 * h + j // 2 + 1))
                            act.wait_ge(s_done, NPR * h + n + 2 - 2)
                            nc.scalar.activation(q_hi[:, j % 2, :], q_raw[:, j % 2, :], ACT.Copy, scale=SCALE).then_inc(qhi_d, 1)
                        for a in range(2):
                            act.wait_ge(nm_d, NPR * h + n + 1)
                            if a == 0:
                                act.wait_ge(t_done, NPR * h + n + 1)
                            nc.scalar.activation(pr[:, n % 2, a, :], S_BANKS[n % 2][:, a * NM:(a + 1) * NM], ACT.Exp,
                                                 bias=nm[:, n % 2, a:a + 1],
                                                 accum_out=rs[:, n // 2 % 2, n % 2 * 2 + a:n % 2 * 2 + a + 1]).then_inc(p_done, 1)
                    if 1 <= n <= NPR:
                        m = n - 1
                        act.wait_ge(t_done, NPR * h + m + 3)
                        if m % 2 == 0:
                            act.wait_ge(o_done, NCH * h + m // 2 + 1)
                        nc.scalar.copy(pT_hi[:, m // 2 % 2, :, m % 2 * 256:m % 2 * 256 + 256],
                                       T_BANKS[m % 2][:, :].rearrange("p (t q) -> p t q", t=NT)).then_inc(th_d, 1)

        @block.vector
        def _(dve):
            dve.sem_inc(tl_d, 2)
            dve.sem_inc(qlo_d, 1)
            dve.sem_inc(mix_d, 1)
            for n in range(XH // 2):
                dve.wait_ge(khi_d, n + 1)
                nc.vector.tensor_tensor(k_lo[:, 2 * n:2 * n + 2, :], K_BANK[:, :].rearrange("p (a m) -> p a m", a=2),
                                        k_hi[:, 2 * n:2 * n + 2, :].bitcast(F32), ALU.subtract).then_inc(klo_d, 1)
            dve.wait_ge(kv_in, 32)
            nc.vector.tensor_copy(v_hi[:, :, :], kv_raw[:, 1, :, :]).then_inc(vhi_d, 1)
            dve.wait_ge(vhi_d, 1)
            nc.vector.tensor_tensor(v_lo[:, :, :], kv_raw[:, 1, :, :], v_hi[:, :, :].bitcast(F32), ALU.subtract).then_inc(vlo_d, 1)
            dve.wait_ge(vlo_d, 1)
            dve.wait_ge(klo_d, XH // 2)
            with dve.Fori(0, XH) as h:
                dve.wait_ge(o_done, NCH * h + 2)
                nc.vector.tensor_copy(kx[:, 0, :], k_hi[:, ds(h, 1), :].rearrange("p o m -> p (o m)").bitcast(F32)).then_inc(head_part, 1)
                nc.vector.tensor_copy(kx[:, 1, :], k_lo[:, ds(h, 1), :].rearrange("p o m -> p (o m)").bitcast(F32)).then_inc(head_part, 1)
                nc.vector.tensor_copy(vx[:, 0, :, :], v_hi[:, :, ds(h * P, P)].bitcast(F32)).then_inc(head_part, 1)
                dve.wait_ge(head_part, 3 * h + 3)
                nc.vector.tensor_copy(vx[:, 1, :, :], v_lo[:, :, ds(h * P, P)].bitcast(F32)).then_inc(head_d, 1)
                for n in range(NPR + 2):
                    if n < NPR:
                        if n % 2 == 0:
                            j = n // 2
                            dve.wait_ge(qhi_d, NCH * h + j + 1)
                            nc.vector.scalar_tensor_tensor(q_lo[:, j % 2, :], q_raw[:, j % 2, :], SCALE,
                                                           q_hi[:, j % 2, :].bitcast(F32), ALU.mult, ALU.subtract).then_inc(qlo_d, 1)
                        dve.wait_ge(s_done, NPR * h + n + 3)
                        dve.wait_ge(p_done, 2 * (NPR * h + n))
                        nc.vector.tensor_reduce(nm[:, n % 2, :], S_BANKS[n % 2][:, :].rearrange("p (a m) -> p a m", a=2),
                                                axis=AX.X, op=ALU.max, negate=True).then_inc(nm_d, 1)
                    if 1 <= n <= NPR:
                        m = n - 1
                        dve.wait_ge(th_d, NPR * h + m + 1)
                        at = (slice(None), m // 2 % 2, slice(None), slice(m % 2 * 256, m % 2 * 256 + 256))
                        nc.vector.tensor_tensor(pT_lo[at], T_BANKS[m % 2][:, :].rearrange("p (t q) -> p t q", t=NT),
                                                pT_hi[at].bitcast(F32), ALU.subtract).then_inc(tl_d, 1)
                        if m % 2 == 1:
                            dve.wait_ge(p_done, 2 * (NPR * h + m) + 4)
                            nc.vector.reciprocal(rr[:, m // 2 % 2, :], rs[:, m // 2 % 2, :]).then_inc(rr_d, 1)
                    if n >= 3 and n % 2 == 1:
                        j = (n - 3) // 2
                        jj = NCH * h + j
                        dve.wait_ge(r_done, jj + 1)
                        dve.wait_ge(g_in[j % 2], 16 * (NCH // 2 * h + j // 2 + 1))
                        nc.vector.tensor_tensor(gate[:, j % 2, :], gate[:, j % 2, :], R_BANK[:, :], ALU.mult).then_inc(gr_d, 1)
                        dve.wait_ge(gr_d, jj + 1)
                        dve.wait_ge(o_done, jj + 3)
                        dve.wait_ge(mix_out[j % 2], 16 * (NCH // 2 * h + j // 2))
                        nc.vector.tensor_tensor(mix[:, j % 2, :], gate[:, j % 2, :], O_BANKS[j % 2][:, :], ALU.mult).then_inc(mix_d, 1)


def output_projection(nc, tag, banks, bT, w, gain, x_prompt, x_sample, y_prompt, y_sample):
    NK = BW // P
    with ExitStack() as s:
        c = Core(nc, s, tag)
        w_raw = c.sb("w_raw", [P, 2, D])
        w_hi, w_lo = (c.sb(n, [P, NK, D], F32R) for n in ("w_hi", "w_lo"))
        b_raw = c.sb("b_raw", [P, 2, NK, P])
        b_hi, b_lo = (c.sb(n, [P, 2, NK, P], F32R) for n in ("b_hi", "b_lo"))
        x = c.sb("x", [P, 2, D])
        y = c.sb("y", [P, 2, D])
        g_bc = c.sb("g_bc", [P, D])
        ss, st = c.sb("ss", [P, 2, 2]), c.sb("st", [P, 2, 4])
        w_in, b_in, x_in, y_out = ([c.sem(f"{n}{u}") for u in range(2)] for n in ("w_loaded", "b_loaded", "x_loaded", "y_stored"))
        g_in, whi_d, wlo_d = c.sem("gain_loaded"), c.sem("w_hi_done"), c.sem("w_lo_done")
        bhi_d, blo_d = c.sem("b_hi_done"), c.sem("b_lo_done")
        mm = c.sem("multiplied")
        sq_d, ms_d, rt_d, ri_d = (c.sem(n) for n in ("sumsq_done", "meansq_done", "root_done", "rinv_done"))
        yn_d, yx_d = c.sem("y_normed"), c.sem("y_ready")
        block = s.enter_context(nc.Block())
        b_v = bT.rearrange("(k p) n -> p k n", p=P)
        T = NQ + 1

        def tiles(eng, body):
            with eng.Fori(0, NQ // 2) as i:
                for u in range(2):
                    body(i, u, 2 * i + u, P, (2 * i + u) * P, x_prompt, y_prompt)
            body(NQ // 2, 0, NQ, NS, SEQ, None, None)

        @block.sync
        def _(sp):
            sp.dma_start(g_bc[:, :], gain.partition_broadcast(P)).then_inc(g_in, 16)

            def body(pair, u, t, rows, col, xs, ys):
                sp.wait_ge(blo_d, t)
                sp.dma_start(b_raw[:, u, :, 0:rows], b_v[:, :, ds(col, rows)]).then_inc(b_in[u], 16)
                sp.wait_ge(yx_d, t)
                src = x_sample[:, :] if xs is None else xs[ds(col, rows), :]
                sp.dma_start(x[0:rows, u, :], src).then_inc(x_in[u], 16)
            tiles(sp, body)

        @block.gpsimd
        def _(pool):
            def body(pair, u, t, rows, col, xs, ys):
                pool.wait_ge(yx_d, t + 2)
                dst = y_sample[:, :] if ys is None else ys[ds(col, rows), :]
                pool.dma_start(dst, y[0:rows, u, :]).then_inc(y_out[u], 16)
            tiles(pool, body)
            pool.wait_ge(y_out[0], 16 * (NQ // 2 + 1))
            pool.wait_ge(y_out[1], 16 * (NQ // 2))

        @block.tensor
        def _(pe):
            pe.sem_inc(mm, 4)

            def body(pair, u, t, rows, col, xs, ys):
                pe.wait_ge(blo_d, t + 2)
                for half in range(2):
                    pe.wait_ge(yn_d, 2 * t + half + 1)
                    out = banks[2 * u + half][:, :]
                    cols = slice(half * 512, (half + 1) * 512)
                    for k in range(NK):
                        if half == 0 and not isinstance(t, int) and u == 0:
                            pe.wait_ge(wlo_d, k + 1)
                        bh, bl = b_hi[:, u, k, :], b_lo[:, u, k, :]
                        nc.tensor.matmul(out, bh, w_hi[:, k, cols], start=(k == 0), stop=False)
                        nc.tensor.matmul(out, bl, w_hi[:, k, cols], start=False, stop=False)
                        last = nc.tensor.matmul(out, bh, w_lo[:, k, cols], start=False, stop=(k == NK - 1))
                    last.then_inc(mm, 1)
            tiles(pe, body)

        @block.scalar
        def _(act):
            for k in range(NK):
                if k >= 2:
                    act.wait_ge(wlo_d, k - 1)
                act.dma_start(w_raw[:, k % 2, :], w[k * P:(k + 1) * P, :]).then_inc(w_in[k % 2], 16)

            def body(pair, u, t, rows, col, xs, ys):
                act.wait_ge(y_out[u], 16 * pair)
                for half in range(2):
                    act.wait_ge(mm, 2 * t + half + 5)
                    nc.scalar.activation(y[0:rows, u, half * 512:(half + 1) * 512], banks[2 * u + half][0:rows, :],
                                         ACT.Square, accum_out=ss[0:rows, u, half:half + 1]).then_inc(sq_d, 1)
                act.wait_ge(ms_d, 2 * t + 2)
                nc.scalar.activation(st[0:rows, u, 2:3], st[0:rows, u, 1:2], ACT.Sqrt).then_inc(rt_d, 1)
            tiles(act, body)

        @block.vector
        def _(dve):
            dve.sem_inc(blo_d, 1)
            dve.sem_inc(yx_d, 1)
            dve.sem_inc(yn_d, 4)

            def split(pair, u, t, rows):
                dve.wait_ge(b_in[u], 16 * (pair + 1))
                dve.wait_ge(mm, 2 * t + 2)
                nc.vector.tensor_copy(b_hi[:, u, :, 0:rows], b_raw[:, u, :, 0:rows]).then_inc(bhi_d, 1)
                dve.wait_ge(bhi_d, t + 1)
                nc.vector.tensor_tensor(b_lo[:, u, :, 0:rows], b_raw[:, u, :, 0:rows], b_hi[:, u, :, 0:rows].bitcast(F32),
                                        ALU.subtract).then_inc(blo_d, 1)

            split(0, 0, 0, P)
            for k in range(NK):
                dve.wait_ge(w_in[k % 2], 16 * (k // 2 + 1))
                nc.vector.tensor_copy(w_hi[:, k, :], w_raw[:, k % 2, :]).then_inc(whi_d, 1)
                dve.wait_ge(whi_d, k + 1)
                nc.vector.tensor_tensor(w_lo[:, k, :], w_raw[:, k % 2, :], w_hi[:, k, :].bitcast(F32),
                                        ALU.subtract).then_inc(wlo_d, 1)
            dve.wait_ge(g_in, 16)

            def body(pair, u, t, rows, col, xs, ys):
                if u == 0 and rows == P:
                    split(pair, 1, t + 1, P)
                elif rows == P:
                    split_next(pair, t)
                dve.wait_ge(sq_d, 2 * t + 2)
                nc.vector.tensor_tensor(st[0:rows, u, 0:1], ss[0:rows, u, 0:1], ss[0:rows, u, 1:2], ALU.add).then_inc(ms_d, 1)
                dve.wait_ge(ms_d, 2 * t + 1)
                nc.vector.tensor_scalar(st[0:rows, u, 1:2], st[0:rows, u, 0:1], 1.0 / D, EPS, ALU.mult, ALU.add).then_inc(ms_d, 1)
                dve.wait_ge(rt_d, t + 1)
                nc.vector.reciprocal(st[0:rows, u, 3:4], st[0:rows, u, 2:3]).then_inc(ri_d, 1)
                dve.wait_ge(ri_d, t + 1)
                for half in range(2):
                    cols = slice(half * 512, (half + 1) * 512)
                    nc.vector.scalar_tensor_tensor(y[0:rows, u, cols], banks[2 * u + half][0:rows, :], st[0:rows, u, 3:4],
                                                   g_bc[0:rows, cols], ALU.mult, ALU.mult).then_inc(yn_d, 1)
                dve.wait_ge(yn_d, 2 * t + 6)
                dve.wait_ge(x_in[u], 16 * (pair + 1))
                nc.vector.tensor_tensor(y[0:rows, u, :], y[0:rows, u, :], x[0:rows, u, :], ALU.add).then_inc(yx_d, 1)

            def split_next(pair, t):
                split(pair + 1, 0, t + 1, NS_OR_P)

            NS_OR_P = P
            with dve.Fori(0, NQ // 2 - 1) as i:
                for u in range(2):
                    body(i, u, 2 * i + u, P, None, True, True)
            last = NQ // 2 - 1
            NS_OR_P = NS
            for u in range(2):
                body(last, u, 2 * last + u, P, None, True, True)
            body(NQ // 2, 0, NQ, NS, None, None, None)


def sample_attention(nc, tag, const, banks, zT, q_row, gate_row, mix_row, bT, heads, pages, k_page, v_page,
                     page_table=None, sufT=None, cnew=None, cnew_q=None, k_new=None, v_new=None):
    ident = const["ident"]
    fox = sufT is not None
    R = heads * TN
    LO = 32
    GP = 2
    NG = pages // GP
    NB = 2 if NG > 1 else 1
    TB = heads // 4
    KS = min(4, pages)
    NV = pages + (1 if fox else 0)
    NSC = NG + (1 if fox else 0)
    HW = heads * HD
    W = pages * P
    WP = NV * P
    S_BANKS, T_BANKS, O_BANKS, PT_BANK, X_BANK = banks[0:2], banks[2:4], banks[4:6], banks[6], banks[7]
    with ExitStack() as s:
        c = Core(nc, s, tag)
        q_raw, g_all, out_all = (c.sb(n, [P, heads, NS]) for n in ("q_raw", "gate", "out_all"))
        qs_hi, qs_lo = c.sb("qs_hi", [P, heads, NS], F32R), c.sb("qs_lo", [P, heads, NS], F32R)
        qx = c.sb("qx", [P, heads * (P + TN) + P], F32R)
        k_raw = c.sb("k_raw", [P, KS, HW])
        kT_hi, kT_lo = (c.sb(n, [P, NB, heads, GP * P], F32R) for n in ("kT_hi", "kT_lo"))
        v_raw = c.sb("v_raw", [P, NV, HW])
        v_hi, v_lo = (c.sb(n, [P, 2, HW], F32R) for n in ("v_hi", "v_lo"))
        low = c.sb("low", [LO, GP * P])
        sc = c.sb("sc", [LO, W + (TN if fox else 0)])
        pb = c.sb("pb", [LO, WP])
        pT = c.sb("pT", [P, NV, P], F32R)
        o_sb = c.sb("o_sb", [2 * LO, HW])
        eye2 = c.sb("eye2", [2 * LO, LO])
        nm, rs, rr = c.sb("nm", [LO, 1]), c.sb("rs", [LO, 1]), c.sb("rr", [LO, 1])
        if fox:
            suf = c.sb("suf", [LO, W])
            c_key, c_bias, mask = c.sb("c_key", [R, DB, TN]), c.sb("c_bias", [R, DB, TN]), c.sb("mask", [R, TN])
            c_qry, low_n = c.sb("c_qry", [R, DB]), c.sb("low_n", [LO, TN])
            maskf = c.sb("maskf", [TN, TN])
            kn_raw = c.sb("kn_raw", [P, heads, NS])
            kn_hi, kn_lo = (c.sb(n, [P, heads, NS], F32R) for n in ("kn_hi", "kn_lo"))
            ptab, ptab_v = (c.sb(n, [1, DB * PAGES], I32) for n in ("ptab", "ptab_v"))
            suf_in, tab_in, tabv_in, vn_in, kn_in, mf_d, bias_d, kn_d = (c.sem(n) for n in (
                "suffix_loaded", "table_loaded", "table_v_loaded", "v_new_loaded", "setup_loaded", "mask_made",
                "new_bias_ready", "k_new_split"))
        zero_d, set_in, set_d, eye_d = (c.sem(n) for n in ("zeroed", "queries_loaded", "queries_split", "eye2_made"))
        k_in = [c.sem(f"k_loaded{n}") for n in range(KS)]
        v_in = [c.sem(f"v_loaded{n}") for n in range(pages)]
        kt_d = c.sem("k_transposed")
        kth_d = c.sem("kT_hi_done")
        ktl_d = c.sem("kT_lo_done")
        qx_d = c.sem("queries_placed")
        s_done = c.sem("scores_done")
        low_d = c.sem("low_rows_copied")
        hi_d = c.sem("high_rows_biased")
        sc_d = c.sem("scores_ready")
        nm_d, p_d, rr_d, pn_d = (c.sem(n) for n in ("maximum_ready", "exp_done", "inverse_ready", "p_normalised"))
        pt_d = c.sem("p_transposed")
        p_seen = c.sem("p_seen")
        pth_d, ptl_d = c.sem("pT_hi_done"), c.sem("pT_lo_done")
        vh_d = c.sem("v_hi_done")
        vl_d = c.sem("v_lo_done")
        pv_d = c.sem("pv_done")
        o_d = c.sem("o_copied")
        x_d = c.sem("o_transposed")
        m_d = c.sem("mixed")
        out_d = c.sem("stored")
        NPT = 2 if fox else 1
        block = s.enter_context(nc.Block())
        cols = slice(SEQ, TOK)

        def bodies(eng, body):
            body(0, None)
            with eng.Fori(1, DB) as b:
                body(b, b - 1)
            body(None, DB - 1)

        @block.sync
        def _(sp):
            row = lambda r0: zT[r0:r0 + HW, cols].rearrange("(h p) n -> p h n", p=P)
            sp.dma_start(q_raw[:, :, :], row(q_row)).then_inc(set_in, 16)
            sp.dma_start(g_all[:, :, :], row(gate_row)).then_inc(set_in, 16)
            if fox:
                sp.dma_start(ptab[:, :], page_table.rearrange("(o b) n -> o (b n)", o=1)).then_inc(tab_in, 16)
                sp.dma_start(kn_raw[:, :, :], row(D)).then_inc(kn_in, 16)
                sp.wait_ge(mf_d, 2)
                for h in range(heads):
                    at = slice(TN * h, TN * h + TN)
                    sp.dma_start(mask[at, :], maskf[:, :]).then_inc(kn_in, 16)
                    sp.dma_start(c_key[at, :, :].rearrange("q b t -> q (b t)"),
                                 cnew[h, :].partition_broadcast(TN)).then_inc(kn_in, 16)
                    sp.dma_start(c_qry[at, :], cnew_q[h, :].rearrange("(t b) -> t b", t=TN)).then_inc(kn_in, 16)
                sp.wait_ge(tab_in, 16)

            def body(bk, bv):
                if bk is None:
                    return
                if fox:
                    sp.wait_ge(sc_d, NSC * bk)
                    sp.dma_start(suf[0:R, :], sufT[ds(bk * R, R), :]).then_inc(suf_in, 16)
                for p in range(pages):
                    src = k_page(sp, bk, p, ptab if fox else None)
                    sp.wait_ge(kt_d, TB * (pages * bk + p + 1))
                    sp.dma_start(k_raw[:, p % KS, :], src).then_inc(k_in[p % KS], 16)
            bodies(sp, body)
            sp.wait_ge(m_d, DB)
            sp.dma_start(bT[mix_row:mix_row + HW, cols].rearrange("(h p) n -> p h n", p=P), out_all[:, :, :]).then_inc(out_d, 16)
            sp.wait_ge(out_d, 16)

        @block.gpsimd
        def _(pool):
            if fox:
                pool.dma_start(ptab_v[:, :], page_table.rearrange("(o b) n -> o (b n)", o=1)).then_inc(tabv_in, 16)
                nc.gpsimd.memset(maskf[:, :], 0.0).then_inc(mf_d, 1)
                pool.wait_ge(mf_d, 1)
                nc.gpsimd.affine_select(out=maskf[:, :], in_=maskf[:, :], compare_op=ALU.is_ge, fill=NEG, base=0,
                                        pattern=[[-1, TN]], channel_multiplier=1).then_inc(mf_d, 1)
                nc.gpsimd.memset(v_raw[:, pages, :], 0.0).then_inc(zero_d, 1)
            nc.gpsimd.memset(qx[:, :].bitcast(F32), 0.0).then_inc(zero_d, 1)
            nc.gpsimd.memset(pT[:, :, :].bitcast(F32), 0.0).then_inc(zero_d, 1)
            nc.gpsimd.memset(pb[:, :], 0.0).then_inc(zero_d, 1)
            if fox:
                pool.wait_ge(tabv_in, 16)
                pool.wait_ge(zero_d, 4)

            def body(bk, bv):
                if bk is None:
                    return
                for p in range(pages):
                    src = v_page(pool, bk, p, ptab_v if fox else None)
                    pool.wait_ge(vl_d, NV * bk + p + 1)
                    pool.dma_start(v_raw[:, p, :], src).then_inc(v_in[p], 16)
                if fox:
                    pool.wait_ge(vl_d, NV * bk + NV)
                    pool.dma_start(v_raw[0:TN, pages, :], v_new[ds(TN * bk, TN), :]).then_inc(vn_in, 16)
            bodies(pool, body)

        def order():
            for g in range(NG + 1):
                yield g if g < NG else None, g - 1 if g >= 1 else None, g - 1 if g >= 1 else None

        def v_pages(g):
            return list(range(g * GP, (g + 1) * GP)) + ([pages] if fox and g == NG - 1 else [])

        @block.tensor
        def _(pe):
            pe.sem_inc(kt_d, TB * KS)
            pe.sem_inc(s_done, NB)
            pe.sem_inc(pv_d, NV)
            pe.wait_ge(zero_d, 4 if fox else 3)
            pe.wait_ge(eye_d, 1)
            if fox:
                pe.wait_ge(kn_d, 2)

            def body(bk, bv):
                for gt, gs, gv in order():
                    if bk is not None and gt is not None:
                        for p in range(gt * GP, (gt + 1) * GP):
                            pe.wait_ge(k_in[p % KS], 16 * ((pages // KS) * bk + p // KS + 1))
                            for n in range(TB):
                                i = TB * p + n
                                pe.wait_ge(ktl_d, TB * pages * bk + i + 1)
                                for h in range(4):
                                    last = nc.tensor.transpose(T_BANKS[i % 2][:, h * P:(h + 1) * P],
                                                               k_raw[:, p % KS, (4 * n + h) * P:(4 * n + h + 1) * P], ident[:, :])
                                last.then_inc(kt_d, 1)
                    if bk is not None and gs is not None:
                        if gs == 0:
                            pe.wait_ge(qx_d, 2 * bk + 2)
                        pe.wait_ge(ktl_d, TB * (pages * bk + (gs + 1) * GP) + 2)
                        pe.wait_ge(hi_d, NSC * bk + gs + 1)
                        pe.wait_ge(low_d, NSC * bk + gs - NB + 1 if gs >= NB else NSC * bk)
                        out = S_BANKS[gs % NB][:, 0:GP * P]
                        for h in range(heads):
                            q = qx[:, h * P:(h + 1) * P]
                            nc.tensor.matmul(out, q, kT_hi[:, gs % NB, h, :], start=(h == 0), stop=False)
                            last = nc.tensor.matmul(out, q, kT_lo[:, gs % NB, h, :], start=False, stop=(h == heads - 1))
                        last.then_inc(s_done, 1)
                        if fox and gs == NG - 1:
                            pe.wait_ge(ptl_d, NPT * bk)
                            out = PT_BANK[:, 0:TN]
                            for h in range(heads):
                                q = qx[:, h * P:(h + 1) * P]
                                nc.tensor.matmul(out, q, kn_hi[:, h, ds(TN * bk, TN)], start=(h == 0), stop=False)
                                last = nc.tensor.matmul(out, q, kn_lo[:, h, ds(TN * bk, TN)], start=False, stop=(h == heads - 1))
                            last.then_inc(s_done, 1)
                    if bv is not None and gv is not None:
                        if gv == 0:
                            pe.wait_ge(pn_d, bv + 1)
                            for p in range(NV):
                                if p == 0:
                                    pe.wait_ge(low_d, NSC * (bv + 1))
                                    pe.wait_ge(hi_d, NSC * (bv + 1) + NB)
                                if p == 16:
                                    pe.wait_ge(m_d, bv)
                                bank = PT_BANK[:, p * LO:(p + 1) * LO] if p < 16 else X_BANK[:, 0:LO]
                                if p in (0, 16):
                                    pe.sem_inc(p_seen, 1)
                                last = nc.tensor.transpose(bank[:, 0:R], pb[0:R, p * P:(p + 1) * P], ident[0:R, 0:R])
                                if p in (min(NV, 16) - 1, 16):
                                    last.then_inc(pt_d, 1)
                            pe.wait_ge(ptl_d, NPT * bv + NPT)
                            pe.wait_ge(o_d, TB * bv)
                        for p in v_pages(gv):
                            pe.wait_ge(vl_d, NV + NV * bv + p + 1)
                            for n in range(TB):
                                out = O_BANKS[n][:, :]
                                vs = slice(n * 512, (n + 1) * 512)
                                nc.tensor.matmul(out, pT[:, p, :], v_hi[:, p % 2, vs], start=(p == 0), stop=False)
                                last = nc.tensor.matmul(out, pT[:, p, :], v_lo[:, p % 2, vs], start=False, stop=(p == NV - 1))
                            last.then_inc(pv_d, 1)
                    if bv is not None and gv == NG - 1:
                        pe.wait_ge(o_d, TB * bv + TB)
                        if not fox:
                            pe.wait_ge(m_d, bv)
                        for h in range(heads):
                            last = nc.tensor.matmul(X_BANK[:, h * LO:(h + 1) * LO], o_sb[:, h * P:(h + 1) * P], eye2[:, :],
                                                    start=True, stop=True)
                        last.then_inc(x_d, 1)
            bodies(pe, body)

        @block.scalar
        def _(act):
            act.wait_ge(set_in, 32)
            nc.scalar.activation(qs_hi[:, :, :], q_raw[:, :, :], ACT.Copy, scale=SCALE).then_inc(set_d, 1)
            act.wait_ge(zero_d, 4 if fox else 3)

            def body(bk, bv):
                for gt, gs, gv in order():
                    if bk is not None and gt is not None:
                        for p in range(gt * GP, (gt + 1) * GP):
                            for n in range(TB):
                                i = TB * p + n
                                act.wait_ge(kt_d, TB * KS + TB * pages * bk + i + 1)
                                act.wait_ge(s_done, NSC * bk + gt + 1 if gt < NB else NSC * bk + gt + 1)
                                nc.scalar.copy(kT_hi[:, gt % NB, 4 * n:4 * n + 4, (p % GP) * P:(p % GP + 1) * P],
                                               T_BANKS[i % 2][:, :].rearrange("p (h n) -> p h n", h=4)).then_inc(kth_d, 1)
                    if bv is not None and gv is not None:
                        if gv == 0:
                            act.wait_ge(pt_d, NPT * bv + 1)
                            act.wait_ge(pv_d, NV * bv + NV)
                            n = min(NV, 16)
                            nc.scalar.copy(pT[:, 0:n, 0:R], PT_BANK[:, 0:n * LO].rearrange("p (n r) -> p n r", r=LO)[:, :, 0:R]).then_inc(pth_d, 1)
                            if fox:
                                act.wait_ge(pt_d, NPT * bv + 2)
                                nc.scalar.copy(pT[:, 16, 0:R], X_BANK[:, 0:R]).then_inc(pth_d, 1)
                        for p in v_pages(gv):
                            if p < pages:
                                act.wait_ge(v_in[p], 16 * (bv + 1))
                            else:
                                act.wait_ge(vn_in, 16 * (bv + 1))
                            prev = p - 2 if p >= 2 else (NV - 1 if NV % 2 == 1 and p == 0 else NV - 2 if NV % 2 == 1 or p == 0 else NV - 1) - NV
                            act.wait_ge(pv_d, NV + NV * bv + prev + 1)
                            nc.scalar.copy(v_hi[:, p % 2, :], v_raw[:, p, :]).then_inc(vh_d, 1)
                    if bk is not None and gs is not None:
                        act.wait_ge(s_done, NB + NSC * bk + gs + 1)
                        act.wait_ge(sc_d, NSC * bk + gs)
                        nc.scalar.copy(low[0:R, :], S_BANKS[gs % NB][LO:LO + R, 0:GP * P]).then_inc(low_d, 1)
                        if fox and gs == NG - 1:
                            act.wait_ge(s_done, NB + NSC * bk + NSC)
                            nc.scalar.copy(low_n[0:R, :], PT_BANK[LO:LO + R, 0:TN]).then_inc(low_d, 1)
                    if bv is not None and gv == NG - 1:
                        for n in range(TB):
                            act.wait_ge(pv_d, NV + NV * bv + NV)
                            act.wait_ge(x_d, bv)
                            nc.scalar.copy(o_sb[:, n * 512:(n + 1) * 512], O_BANKS[n][0:2 * LO, :]).then_inc(o_d, 1)
                    if bk is not None and gs == NG - 1:
                        act.wait_ge(nm_d, bk + 1)
                        act.wait_ge(pt_d, NPT * bk)
                        w = W + (TN if fox else 0)
                        nc.scalar.activation(pb[0:R, 0:w], sc[0:R, 0:w], ACT.Exp, bias=nm[0:R, :],
                                             accum_out=rs[0:R, :]).then_inc(p_d, 1)
            bodies(act, body)

        @block.vector
        def _(dve):
            dve.sem_inc(ktl_d, 2)
            dve.sem_inc(hi_d, NB)
            dve.sem_inc(vl_d, NV)
            nc.vector.tensor_add(eye2[:, :], ident[0:2 * LO, 0:LO], ident[0:2 * LO, LO:2 * LO]).then_inc(eye_d, 1)
            dve.wait_ge(set_d, 1)
            dve.wait_ge(zero_d, 4 if fox else 3)
            nc.vector.scalar_tensor_tensor(qs_lo[:, :, :], q_raw[:, :, :], SCALE, qs_hi[:, :, :].bitcast(F32), ALU.mult,
                                           ALU.subtract).then_inc(set_d, 1)
            if fox:
                dve.wait_ge(kn_in, 16 * (1 + 3 * heads))
                nc.vector.tensor_copy(kn_hi[:, :, :], kn_raw[:, :, :]).then_inc(kn_d, 1)
                dve.wait_ge(kn_d, 1)
                nc.vector.tensor_tensor(kn_lo[:, :, :], kn_raw[:, :, :], kn_hi[:, :, :].bitcast(F32), ALU.subtract).then_inc(kn_d, 1)
                nc.vector.tensor_tensor(c_bias[:, :, :], c_qry[:, :].unsqueeze(2).broadcast_to([R, DB, TN]),
                                        c_key[:, :, :], ALU.subtract).then_inc(bias_d, 1)
                dve.wait_ge(bias_d, 1)
                nc.vector.tensor_tensor(c_bias[:, :, :], c_bias[:, :, :], mask[:, :].unsqueeze(1).broadcast_to([R, DB, TN]),
                                        ALU.add).then_inc(bias_d, 1)
                dve.wait_ge(bias_d, 2)
            dve.wait_ge(set_d, 2)
            dve.wait_ge(set_in, 32)

            def diag(t, off):
                return t[:, off:off + heads * (P + TN)].rearrange("p (h x) -> p h x", x=P + TN)[:, :, 0:TN]

            def body(bk, bv):
                if bk is not None:
                    dve.wait_ge(s_done, NB + NSC * bk)
                    nc.vector.tensor_copy(diag(qx, 0), qs_hi[:, :, ds(TN * bk, TN)].bitcast(F32)).then_inc(qx_d, 1)
                    nc.vector.tensor_copy(diag(qx, LO), qs_lo[:, :, ds(TN * bk, TN)].bitcast(F32)).then_inc(qx_d, 1)
                for gt, gs, gv in order():
                    if bv is not None and gt == 0:
                        dve.wait_ge(p_d, bv + 1)
                        nc.vector.reciprocal(rr[0:R, :], rs[0:R, :]).then_inc(rr_d, 1)
                        dve.wait_ge(rr_d, bv + 1)
                        w = W + (TN if fox else 0)
                        nc.vector.tensor_scalar(pb[0:R, 0:w], pb[0:R, 0:w], rr[0:R, :], None, ALU.mult).then_inc(pn_d, 1)
                    if bk is not None and gt is not None:
                        for p in range(gt * GP, (gt + 1) * GP):
                            for n in range(TB):
                                i = TB * p + n
                                at = (slice(None), gt % NB, slice(4 * n, 4 * n + 4), slice((p % GP) * P, (p % GP + 1) * P))
                                dve.wait_ge(kth_d, TB * pages * bk + i + 1)
                                nc.vector.tensor_tensor(kT_lo[at], T_BANKS[i % 2][:, :].rearrange("p (h n) -> p h n", h=4),
                                                        kT_hi[at].bitcast(F32), ALU.subtract).then_inc(ktl_d, 1)
                    if bv is not None and gv is not None:
                        if gv == 0:
                            n = min(NV, 16)
                            dve.wait_ge(pth_d, NPT * bv + 1)
                            nc.vector.tensor_tensor(pT[:, 0:n, LO:LO + R],
                                                    PT_BANK[:, 0:n * LO].rearrange("p (n r) -> p n r", r=LO)[:, :, 0:R],
                                                    pT[:, 0:n, 0:R].bitcast(F32), ALU.subtract).then_inc(ptl_d, 1)
                            if fox:
                                dve.wait_ge(pth_d, NPT * bv + 2)
                                nc.vector.tensor_tensor(pT[:, 16, LO:LO + R], X_BANK[:, 0:R], pT[:, 16, 0:R].bitcast(F32),
                                                        ALU.subtract).then_inc(ptl_d, 1)
                        for p in v_pages(gv):
                            dve.wait_ge(vh_d, NV * bv + p + 1)
                            nc.vector.tensor_tensor(v_lo[:, p % 2, :], v_raw[:, p, :], v_hi[:, p % 2, :].bitcast(F32),
                                                    ALU.subtract).then_inc(vl_d, 1)
                    if bk is not None and gs is not None:
                        k0 = gs * GP * P
                        dst = sc[0:R, k0:k0 + GP * P]
                        src = S_BANKS[gs % NB][0:R, 0:GP * P]
                        if gs == 0:
                            dve.wait_ge(p_d, bk)
                        if fox:
                            dve.wait_ge(suf_in, 16 * (bk + 1))
                            dve.wait_ge(s_done, NB + NSC * bk + gs + 1)
                            nc.vector.scalar_tensor_tensor(dst, suf[0:R, k0:k0 + GP * P], c_qry[:, ds(bk, 1)], src,
                                                           ALU.add, ALU.add).then_inc(hi_d, 1)
                            dve.wait_ge(hi_d, NB + NSC * bk + gs + 1)
                            dve.wait_ge(low_d, NSC * bk + gs + 1)
                            nc.vector.tensor_tensor(dst, dst, low[0:R, :], ALU.add).then_inc(sc_d, 1)
                        else:
                            dve.wait_ge(low_d, NSC * bk + gs + 1)
                            nc.vector.tensor_tensor(dst, src, low[0:R, :], ALU.add).then_inc(hi_d, 1)
                            dve.wait_ge(hi_d, NB + NSC * bk + gs + 1)
                            dve.sem_inc(sc_d, 1)
                        if fox and gs == NG - 1:
                            dst = sc[0:R, W:W + TN]
                            dve.wait_ge(s_done, NB + NSC * bk + NSC)
                            nc.vector.tensor_tensor(dst, c_bias[:, ds(bk, 1), :].rearrange("r o t -> r (o t)"),
                                                    PT_BANK[0:R, 0:TN], ALU.add).then_inc(hi_d, 1)
                            dve.wait_ge(hi_d, NB + NSC * bk + NSC)
                            dve.wait_ge(low_d, NSC * bk + NSC)
                            nc.vector.tensor_tensor(dst, dst, low_n[0:R, :], ALU.add).then_inc(sc_d, 1)
                        if gs == NG - 1:
                            dve.wait_ge(sc_d, NSC * bk + NSC)
                            nc.vector.tensor_reduce(nm[0:R, :], sc[0:R, :], axis=AX.X, op=ALU.max, negate=True).then_inc(nm_d, 1)
                    if bv is not None and gv == NG - 1:
                        dve.wait_ge(x_d, bv + 1)
                        at = (slice(None), slice(None), ds(TN * bv, TN))
                        own = X_BANK[:, 0:heads * (LO + TN)].rearrange("p (h x) -> p h x", x=LO + TN)[:, :, 0:TN]
                        nc.vector.tensor_tensor(out_all[at], own, g_all[at], ALU.mult).then_inc(m_d, 1)
            bodies(dve, body)


def pool_mixing(nc, const, banks, zT, state, w_group, scale, bT, state_prompt, state_sample):
    ident = const["ident"]
    G, CT = 4, 2
    Z = 16
    EXT = HIST + TN
    TAIL = TOK - (SEQ - HIST)
    with ExitStack() as s:
        c = Core(nc, s, "pm")
        u = c.sb("u", [P, 2, CT, Z + SEQ])
        acc = [c.sb(f"acc{n}", [P, CT, Z + SEQ]) for n in range(2)]
        tail, tail_t = c.sb("tail", [P, KT, TAIL]), c.sb("tail_t", [TAIL, D])
        st_raw, ext = c.sb("st_raw", [DB * HIST, D]), c.sb("ext", [P, KT, DB, EXT])
        exa = [c.sb(f"exa{n}", [P, CT, DB, EXT]) for n in range(2)]
        inv = c.sb("inv", [P, Z])
        dd = c.sb("dd", [P, CT, TOK])
        d_hi, d_lo = (c.sb(n, [P, CT, TOK], F32R) for n in ("d_hi", "d_lo"))
        wg_raw = c.sb("wg_raw", [P, G, CT, CT * P])
        wg_hi, wg_lo = (c.sb(n, [P, G, CT, CT * P], F32R) for n in ("wg_hi", "wg_lo"))
        sc_col = c.sb("sc_col", [P, KT])
        gate = c.sb("gate", [P, CT, TOK])
        mix = c.sb("mix", [P, CT, TOK])
        u_in, g_in, m_out = ([c.sem(f"{n}{i}") for i in range(2)] for n in ("u_loaded", "gate_loaded", "mix_stored"))
        tl_in, st_in, w_in, s_in = (c.sem(n) for n in ("tail_loaded", "state_loaded", "w_loaded", "scale_loaded"))
        z_d, inv_d, wh_d, wl_d = (c.sem(n) for n in ("zeroed", "inverse_counts", "w_hi_done", "w_lo_done"))
        tt_d, tc_d, stt_d, ext_d = (c.sem(n) for n in ("tail_transposed", "tail_copied", "state_transposed", "state_copied"))
        sum_v, sum_p, ex_d = c.sem("sums_dve"), c.sem("sums_pool"), c.sem("sample_sums")
        d_d, dh_d, dl_d, y_d, mx_d, out_d = (c.sem(n) for n in ("d_ready", "d_hi_done", "d_lo_done", "y_done", "mix_ready", "stored"))
        block = s.enter_context(nc.Block())
        levels = [g + 1 for g in range(G)]
        before = [sum(levels[:g]) for g in range(G + 1)]

        @block.sync
        def _(sp):
            sp.dma_start(tail[:, :, :], zT[0:D, SEQ - HIST:TOK].rearrange("(k p) n -> p k n", p=P)).then_inc(tl_in, 16)
            sp.dma_start(st_raw[:, :], state.rearrange("b n d -> (b n) d")).then_inc(st_in, 16)
            for g in range(G):
                if g == 0:
                    sp.wait_ge(z_d, 4)
                if g >= 2:
                    sp.wait_ge(d_d, 4 * (g - 1))
                sp.dma_start(u[:, g % 2, :, Z:], zT[g * CT * P:(g + 1) * CT * P, 0:SEQ].rearrange("(c p) n -> p c n", p=P)).then_inc(u_in[g % 2], 16)
                if g == 0:
                    sp.dma_start(wg_raw[:, :, :, :], w_group.rearrange("g (c p) n -> p g c n", p=P)).then_inc(w_in, 16)
                    sp.dma_start(sc_col[:, :], scale.rearrange("(k p) -> p k", p=P), allow_slow_non_contiguous=True).then_inc(s_in, 16)
                if g >= 1:
                    sp.wait_ge(mx_d, CT * CH * g)
                r0 = D + XW + g * CT * P
                sp.dma_start(gate[:, :, :], zT[r0:r0 + CT * P, :].rearrange("(c p) n -> p c n", p=P)).then_inc(g_in[g % 2], 16)
            sp.dma_start(state_sample[:, 0:HIST - TN, :], state[:, TN:HIST, :]).then_inc(out_d, 16)
            sp.wait_ge(tc_d, 2)
            sp.dma_start(state_prompt[:, :], tail_t[0:HIST, :]).then_inc(out_d, 16)
            for b in range(DB):
                sp.dma_start(state_sample[b, HIST - TN:HIST, :], tail_t[HIST + TN * b:HIST + TN * (b + 1), :]).then_inc(out_d, 16)
            sp.wait_ge(out_d, 16 * (2 + DB))

        @block.gpsimd
        def _(pool):
            nc.gpsimd.memset(u[:, 0, :, 0:Z], 0.0).then_inc(z_d, 1)
            nc.gpsimd.memset(u[:, 1, :, 0:Z], 0.0).then_inc(z_d, 1)
            for n in range(2):
                nc.gpsimd.memset(acc[n][:, :, 0:Z], 0.0).then_inc(z_d, 1)
            for t in range(Z):
                nc.gpsimd.memset(inv[:, t:t + 1], 1.0 / (t + 1)).then_inc(inv_d, 1)
            pool.wait_ge(z_d, 4)
            for g in range(G):
                pool.wait_ge(u_in[g % 2], 16 * (g // 2 + 1))
                src = u[:, g % 2, 1, :]
                for n in range(levels[g]):
                    if n:
                        pool.wait_ge(sum_p, before[g] + n)
                    elif g:
                        pool.wait_ge(d_d, 4 * g)
                    dst = acc[n % 2][:, 1, :]
                    nc.gpsimd.tensor_tensor(dst[:, Z:], src[:, Z:], src[:, Z - 2 ** n:Z + SEQ - 2 ** n], ALU.add).then_inc(sum_p, 1)
                    src = dst

        @block.vector
        def _(dve):
            dve.wait_ge(w_in, 16)
            nc.vector.tensor_copy(wg_hi[:, :, :, :], wg_raw[:, :, :, :]).then_inc(wh_d, 1)
            dve.wait_ge(wh_d, 1)
            nc.vector.tensor_tensor(wg_lo[:, :, :, :], wg_raw[:, :, :, :], wg_hi[:, :, :, :].bitcast(F32), ALU.subtract).then_inc(wl_d, 1)
            dve.wait_ge(z_d, 4)
            dve.wait_ge(tl_in, 16)
            nc.vector.tensor_copy(ext[:, :, :, HIST:], tail[:, :, HIST:].rearrange("p k (b t) -> p k b t", b=DB)).then_inc(ext_d, 1)
            for n in range(2):
                dve.wait_ge(stt_d, n + 1)
                nc.vector.tensor_copy(ext[:, 4 * n:4 * n + 4, :, 0:HIST],
                                      banks[6 + n][:, 0:4 * DB * HIST].rearrange("p (k b n) -> p k b n", k=4, b=DB)).then_inc(ext_d, 1)
            dve.wait_ge(ext_d, 3)
            dve.wait_ge(inv_d, Z)
            dve.wait_ge(s_in, 16)
            n_ex = 0
            for g in range(G):
                w = 2 ** (g + 1)
                dve.wait_ge(u_in[g % 2], 16 * (g // 2 + 1))
                src, exs = u[:, g % 2, 0, :], ext[:, CT * g:CT * g + CT, :, :]
                for n in range(levels[g]):
                    sh = 2 ** n
                    if n:
                        dve.wait_ge(sum_v, before[g] + n)
                        dve.wait_ge(ex_d, n_ex)
                    dst = acc[n % 2][:, 0, :]
                    nc.vector.tensor_tensor(dst[:, Z:], src[:, Z:], src[:, Z - sh:Z + SEQ - sh], ALU.add).then_inc(sum_v, 1)
                    src = dst
                    lo = 2 * sh - 1
                    for ct in range(CT):
                        nc.vector.tensor_tensor(exa[n % 2][:, ct, :, lo:], exs[:, ct, :, lo:], exs[:, ct, :, lo - sh:EXT - sh], ALU.add).then_inc(ex_d, 1)
                    n_ex += CT
                    exs = exa[n % 2][:, :, :, :]
                last = acc[(levels[g] - 1) % 2]
                dve.wait_ge(sum_v, before[g + 1])
                dve.wait_ge(sum_p, before[g + 1])
                dve.wait_ge(ex_d, n_ex)
                if g:
                    dve.wait_ge(dl_d, g)
                nc.vector.scalar_tensor_tensor(dd[:, :, 0:SEQ], last[:, :, Z:], 1.0 / w, u[:, g % 2, :, Z:], ALU.mult,
                                               ALU.subtract).then_inc(d_d, 1)
                for ct in range(CT):
                    last_d = nc.vector.scalar_tensor_tensor(
                        dd[:, ct, SEQ:].rearrange("p (b t) -> p b t", t=TN), exs[:, ct, :, HIST:], 1.0 / w,
                        ext[:, CT * g + ct, :, HIST:], ALU.mult, ALU.subtract)
                last_d.then_inc(d_d, 1)
                dve.wait_ge(d_d, 4 * g + 2)
                head = last[:, :, Z:Z + w]
                nc.vector.tensor_tensor(dd[:, :, 0:w], head, inv[:, 0:w].unsqueeze(1).broadcast_to([P, CT, w]), ALU.mult).then_inc(d_d, 1)
                dve.wait_ge(d_d, 4 * g + 3)
                nc.vector.tensor_tensor(dd[:, :, 0:w], dd[:, :, 0:w], u[:, g % 2, :, Z:Z + w], ALU.subtract).then_inc(d_d, 1)
                dve.wait_ge(dh_d, g + 1)
                nc.vector.tensor_tensor(d_lo[:, :, :], dd[:, :, :], d_hi[:, :, :].bitcast(F32), ALU.subtract).then_inc(dl_d, 1)
                dve.wait_ge(g_in[g % 2], 16 * (g // 2 + 1))
                for i in range(CT * CH):
                    ct, ch = i // CH, i % CH
                    at = (slice(None), ct, slice(ch * CW, (ch + 1) * CW))
                    if i == 0 and g:
                        dve.wait_ge(m_out[(g - 1) % 2], 16 * ((g - 1) // 2 + 1))
                    dve.wait_ge(y_d, CT * CH * g + i + 1)
                    nc.vector.scalar_tensor_tensor(mix[at], banks[ch][:, 0:CW], sc_col[:, CT * g + ct:CT * g + ct + 1],
                                                   gate[at], ALU.mult, ALU.mult).then_inc(mx_d, 1)

        @block.tensor
        def _(pe):
            pe.wait_ge(tl_in, 16)
            for k in range(KT):
                last = nc.tensor.transpose(banks[5 if k < 4 else 0][0:TAIL, k % 4 * P:(k % 4 + 1) * P], tail[:, k, :], ident[:, :])
                if k % 4 == 3:
                    last.then_inc(tt_d, 1)
            pe.wait_ge(st_in, 16)
            for k in range(KT):
                n = DB * HIST
                last = nc.tensor.transpose(banks[6 + k // 4][:, k % 4 * n:(k % 4 + 1) * n], st_raw[:, k * P:(k + 1) * P], ident[0:n, 0:n])
                if k % 4 == 3:
                    last.then_inc(stt_d, 1)
            pe.wait_ge(wl_d, 1)
            pe.wait_ge(tc_d, 2)
            for g in range(G):
                pe.wait_ge(dl_d, g + 1)
                for i in range(CT * CH):
                    dt, ch = i // CH, i % CH
                    n = CT * CH * g + i
                    if n >= CH:
                        pe.wait_ge(mx_d, n - CH + 1)
                    out = banks[ch][:, 0:CW]
                    for ct in range(CT):
                        wh, wl = wg_hi[:, g, ct, dt * P:(dt + 1) * P], wg_lo[:, g, ct, dt * P:(dt + 1) * P]
                        dh, dl = d_hi[:, ct, ch * CW:(ch + 1) * CW], d_lo[:, ct, ch * CW:(ch + 1) * CW]
                        nc.tensor.matmul(out, wh, dh, start=(ct == 0), stop=False)
                        nc.tensor.matmul(out, wh, dl, start=False, stop=False)
                        last = nc.tensor.matmul(out, wl, dh, start=False, stop=(ct == CT - 1))
                    last.then_inc(y_d, 1)

        @block.scalar
        def _(act):
            for n in range(2):
                act.wait_ge(tt_d, n + 1)
                nc.scalar.copy(tail_t[:, n * 512:(n + 1) * 512], banks[5 if n == 0 else 0][0:TAIL, :]).then_inc(tc_d, 1)
            for g in range(G):
                act.wait_ge(d_d, 4 * g + 4)
                if g:
                    act.wait_ge(y_d, CT * CH * g)
                nc.scalar.copy(d_hi[:, :, :], dd[:, :, :]).then_inc(dh_d, 1)
                act.wait_ge(mx_d, CT * CH * (g + 1))
                r0 = g * CT * P
                act.dma_start(bT[r0:r0 + CT * P, :].rearrange("(c p) n -> p c n", p=P), mix[:, :, :]).then_inc(m_out[g % 2], 16)
            for n in range(2):
                act.wait_ge(m_out[n], 16 * 2)


def decoder_step(nc, ins, outs):
    (x_prompt, x_sample, mem_prompt, cache_k, cache_v, cache_logf, cache_mem_k, cache_mem_v, state_pool, page_table,
     norm_pre, norm_post, mem_norm, w_mem_kv, fox_w_in, fox_b_f, pool_w_in, pool_w_group, pool_scale, w_out) = ins
    (y_prompt, y_sample, fox_k_p, fox_v_p, fox_lf_p, fox_k_s, fox_v_s, fox_lf_s, mem_k, mem_v, pool_p, pool_s) = outs
    xp = x_prompt.rearrange("a t d -> (a t) d")
    xs = x_sample.rearrange("b t d -> (b t) d")
    yp = y_prompt.rearrange("a t d -> (a t) d")
    ys = y_sample.rearrange("b t d -> (b t) d")

    def scratch(name, shape):
        return nc.dram_tensor(name, shape, F32, kind="Internal").ap()

    z0 = scratch("z0", (3 * D + XW + BW, TOK))
    z1 = scratch("z1", (D + XW + BW, TOK))
    bT = scratch("bT", (BW, TOK))
    x1p, x1s = scratch("x1p", (SEQ, D)), scratch("x1s", (NS, D))
    cT, sufT = scratch("cT", (FH, SEQ)), scratch("sufT", (DB * FH * TN, PAGES * P))
    cnew, cnew_q = scratch("cnew", (FH, NS)), scratch("cnew_q", (FH, NS))

    with ExitStack() as s:
        banks = [s.enter_context(nc.psum_tensor(f"bank{i}", [P, 512], F32)) for i in range(8)]
        const = make_constants(nc, s, banks)

        def mem(l, z, q_row, gate_row):
            kp, vp = (t[l].rearrange("a m h d -> (a m) (h d)") for t in (mem_k, mem_v))
            memory_kv(nc, f"mk{l}", const, banks, mem_prompt.rearrange("a m d -> (a m) d"), mem_norm[l], w_mem_kv[l], kp, vp)
            memory_attention(nc, f"ma{l}", const, banks, z, q_row, gate_row, bT, kp, vp)

            def page(cache):
                return lambda eng, b, p, tab: cache[l][ds(b, 1), p * P:(p + 1) * P, :, :].rearrange("o t h d -> (o t) (h d)")
            sample_attention(nc, f"sm{l}", const, banks, z, q_row, gate_row, D, bT, XH, NM // P, page(cache_mem_k), page(cache_mem_v))

        with ExitStack() as s0:
            fT = s0.enter_context(nc.sbuf_tensor("fT", [FH, TOK], F32))
            with ExitStack() as s1:
                hi, lo = (s1.enter_context(nc.sbuf_tensor(f"h0{n}", [P, KT, TOK], F32R)) for n in ("hi", "lo"))
                norm_transpose(nc, "n0", const, banks, (xp, [(xs, NS, SEQ)]), norm_pre[0], hi, lo)
                o = 3 * D + FH
                project(nc, "p0", banks, fox_w_in, hi, lo, z0,
                        [(0, 3 * KT, 0, ACT.Copy), (o, XH, 3 * D, ACT.Copy), (o + XW, BW // P, 3 * D + XW, ACT.Silu)],
                        3 * D, fT, fox_b_f)
            forget_gates(nc, const, banks, fT, cache_logf, page_table, fox_lf_p, fox_lf_s, cT, sufT, cnew, cnew_q)
        sample_kv_out(nc, const, banks, z0, fox_k_s, fox_v_s)
        fox_attention(nc, const, banks, z0, cT, bT, fox_k_p, fox_v_p)

        def page(cache):
            def of(eng, b, p, tab):
                n = eng.value_load(tab[0:1, ds(b * PAGES + p, 1)], min_val=0, max_val=cache.shape[0] - 1)
                return cache[ds(n, 1), :, :, :].rearrange("o t h d -> (o t) (h d)")
            return of
        sample_attention(nc, "sf", const, banks, z0, 0, 3 * D + XW, 0, bT, FH, PAGES, page(cache_k), page(cache_v),
                         page_table, sufT, cnew, cnew_q, fox_k_s, fox_v_s.rearrange("b t h d -> (b t) (h d)"))
        mem(0, z0, 3 * D, 3 * D + XW + D)
        output_projection(nc, "o0", banks, bT, w_out[0], norm_post[0], xp, xs, x1p, x1s)

        with ExitStack() as s1:
            hi, lo = (s1.enter_context(nc.sbuf_tensor(f"h1{n}", [P, KT, TOK], F32R)) for n in ("hi", "lo"))
            norm_transpose(nc, "n1", const, banks, (x1p, [(x1s, NS, SEQ)]), norm_pre[1], hi, lo)
            project(nc, "p1", banks, pool_w_in, hi, lo, z1,
                    [(0, KT + XH, 0, ACT.Copy), (D + XW, BW // P, D + XW, ACT.Silu)])
        pool_mixing(nc, const, banks, z1, state_pool, pool_w_group, pool_scale, bT,
                    pool_p.rearrange("a n d -> (a n) d"), pool_s)
        mem(1, z1, D, D + XW + D)
        output_projection(nc, "o1", banks, bT, w_out[1], norm_post[1], x1p, x1s, yp, ys)


def sample_kv_out(nc, const, banks, zT, k_out, v_out):
    with ExitStack() as s:
        c = Core(nc, s, "so")
        raw, tok = c.sb("raw", [P, 2, FH, NS]), c.sb("tok", [NS, 2, D])
        ld, tr, cp, out = (c.sem(n) for n in ("loaded", "transposed", "copied", "stored"))
        block = s.enter_context(nc.Block())

        @block.sync
        def _(sp):
            for n in range(2):
                sp.dma_start(raw[:, n, :, :], zT[(n + 1) * D:(n + 2) * D, SEQ:TOK].rearrange("(h p) n -> p h n", p=P)).then_inc(ld, 16)
            sp.wait_ge(cp, 4)
            for n, dst in enumerate((k_out, v_out)):
                sp.dma_start(dst.rearrange("b t h d -> (b t) (h d)"), tok[:, n, :]).then_inc(out, 16)
            sp.wait_ge(out, 32)

        @block.tensor
        def _(pe):
            pe.wait_ge(ld, 32)
            for i in range(2 * FH):
                last = nc.tensor.transpose(banks[i // 4][0:NS, i % 4 * P:(i % 4 + 1) * P], raw[:, i // FH, i % FH, :], const["ident"][:, :])
                if i % 4 == 3:
                    last.then_inc(tr, 1)

        @block.scalar
        def _(act):
            for n in range(4):
                act.wait_ge(tr, n + 1)
                nc.scalar.copy(tok[:, n // 2, n % 2 * 512:(n % 2 + 1) * 512], banks[n][0:NS, :]).then_inc(cp, 1)


_INS = ["x_prompt", "x_sample", "mem_prompt", "cache_fox_k", "cache_fox_v", "cache_fox_logf", "cache_mem_k", "cache_mem_v",
        "state_pool", "page_table", "norm_pre", "norm_post", "mem_norm", "w_mem_kv", "fox_w_in", "fox_b_f", "pool_w_in",
        "pool_w_group", "pool_scale", "w_out"]
_OUTS = [(1, SEQ, D), (DB, TN, D), (NQ, P, FH, HD), (NQ, P, FH, HD), (NQ, P, FH), (DB, TN, FH, HD), (DB, TN, FH, HD),
         (DB, TN, FH), (2, 1, NM, XH, HD), (2, 1, NM, XH, HD), (1, HIST, D), (DB, HIST, D)]


def kernel(**inputs):
    import numpy as _np
    import concourse.bacc as _bacc
    from concourse.bass_utils import run_bass_kernel_spmd as _run

    nc = _bacc.Bacc("TRN2", target_bir_lowering=False, num_devices=1)
    arrays, ins = {}, []
    for name in _INS:
        a = _np.ascontiguousarray(inputs[name])
        arrays[f"in_{name}"] = a
        ins.append(nc.dram_tensor(f"in_{name}", a.shape, mybir.dt.from_np(a.dtype), kind="ExternalInput").ap())
    outs = [nc.dram_tensor(f"out_{i}", shape, F32, kind="ExternalOutput").ap() for i, shape in enumerate(_OUTS)]
    decoder_step(nc, ins, outs)
    r = _run(nc, [arrays], core_ids=[0])
    return tuple(r.results[0][f"out_{i}"] for i in range(len(_OUTS)))
```

```python
from contextlib import ExitStack

import concourse.bass as bass
from concourse import mybir
from concourse.alu_op_type import AluOpType as ALU

F32 = mybir.dt.float32
F32R = mybir.dt.float32r
BF16 = mybir.dt.bfloat16
I32 = mybir.dt.int32
ACT = mybir.ActivationFunctionType
AX = mybir.AxisListType
ds = bass.ds

P = 128
D = 1024
KT = D // P
SEQ = 2048
NQ = SEQ // P
DB, TN = 8, 4
NS = DB * TN
TOK = SEQ + NS
CH = 5
CW = TOK // CH
FH, XH, HD = 8, 4, 128
XW = XH * HD
BW = D + XW
NM = 256
PAGES = 16
EPS = 1e-6
SCALE = float(HD) ** -0.5
NEG = -1e30
LOWEST = -3e38
HIST = 15


class Core:

    def __init__(self, nc, stack, tag):
        self.nc, self.stack, self.tag = nc, stack, tag
        self.sems = []
        stack.callback(self.clear)

    def clear(self):
        if self.sems:
            self.nc.clear_and_free_semaphores(self.sems)

    def sb(self, name, shape, dt=F32):
        return self.stack.enter_context(self.nc.sbuf_tensor(f"{name}_{self.tag}", shape, dt))

    def sem(self, name):
        free = self.nc.free_semaphores
        self.sems.append(self.nc.alloc_semaphore(f"{name}_{self.tag}", num=free[-1]))
        return self.sems[-1]


def make_constants(nc, stack, banks):
    g = Core(nc, stack, "const")
    ident = g.sb("ident", [P, P])
    ones = g.sb("ones", [P, P])
    ident_b = g.sb("ident_b", [P, P], BF16)
    mask_b = g.sb("mask_b", [P, P], BF16)
    with ExitStack() as s:
        c = Core(nc, s, "mk")
        made = c.sem("const_made")
        block = s.enter_context(nc.Block())

        @block.gpsimd
        def _(pool):
            nc.gpsimd.memset(ident[:, :], 0.0).then_inc(made, 1)
            nc.gpsimd.memset(ident_b[:, :], 0.0).then_inc(made, 1)
            nc.gpsimd.memset(mask_b[:, :], 0.0).then_inc(made, 1)
            nc.gpsimd.memset(ones[:, :], 1.0).then_inc(made, 1)
            pool.wait_ge(made, 4)
            for t in (ident, ident_b):
                nc.gpsimd.affine_select(out=t[:, :], in_=t[:, :], compare_op=ALU.not_equal, fill=1.0,
                                        base=0, pattern=[[-1, P]], channel_multiplier=1).then_inc(made, 1)
            nc.gpsimd.affine_select(out=mask_b[:, :], in_=mask_b[:, :], compare_op=ALU.is_ge, fill=NEG,
                                    base=0, pattern=[[-1, P]], channel_multiplier=1).then_inc(made, 1)
            pool.wait_ge(made, 7)
    return dict(ident=ident, ones=ones, ident_b=ident_b, mask_b=mask_b)


def norm_transpose(nc, tag, const, banks, looped, single, gain, hT_hi, hT_lo):
    n_pairs = looped.shape[0] // P // 2 if looped is not None else 0
    ident = const["ident"]
    with ExitStack() as s:
        c = Core(nc, s, tag)
        g_bc = c.sb("g_bc", [P, D])
        x = c.sb("x", [P, 2, D])
        xn = c.sb("xn", [P, 2, D])
        ss, ms, rt, ri = (c.sb(n, [P, 2]) for n in ("ss", "ms", "rt", "ri"))
        g_in = c.sem("gain_loaded")
        x_in = [c.sem(f"x_loaded{u}") for u in range(2)]
        sq_done = c.sem("sumsq_done")
        ms_done = c.sem("meansq_done")
        rt_done = c.sem("root_done")
        ri_done = c.sem("rinv_done")
        xn_done = c.sem("xn_done")
        tr_done = c.sem("transposed")
        hi_done = c.sem("hi_done")
        lo_done = c.sem("lo_done")
        block = s.enter_context(nc.Block())

        def pairs(eng, body):
            full = lambda i: [(u, P, (2 * i + u) * P, None) for u in range(2)]
            rest = [(u, rows, col, src) for u, (src, rows, col) in enumerate(single)]
            if not n_pairs:
                body(0, rest, None, None)
            else:
                body(0, full(0), None, None)
                with eng.Fori(1, n_pairs) as i:
                    body(i, full(i), i - 1, full(i - 1))
                body(n_pairs, rest, n_pairs - 1, full(n_pairs - 1))
            body(None, None, n_pairs, rest)

        @block.sync
        def _(sp):
            sp.dma_start(g_bc[:, :], gain.partition_broadcast(P)).then_inc(g_in, 16)

            def body(i, tiles, ip, before):
                for u, rows, col, src in tiles or []:
                    sp.wait_ge(xn_done, 2 * i + u + 1)
                    sp.dma_start(x[0:rows, u, :], looped[ds(col, P), :] if src is None else src).then_inc(x_in[u], 16)
            pairs(sp, body)

        @block.scalar
        def _(act):
            act.sem_inc(sq_done, 2)
            act.sem_inc(rt_done, 1)
            act.sem_inc(hi_done, 4)

            def body(i, tiles, ip, before):
                for u, rows, col, src in tiles or []:
                    act.wait_ge(x_in[u], 16 * (i + 1))
                    act.wait_ge(tr_done, 4 * i + 4)
                    nc.scalar.activation(xn[0:rows, u, :], x[0:rows, u, :], ACT.Square,
                                         accum_out=ss[0:rows, u:u + 1]).then_inc(sq_done, 1)
                if tiles:
                    n, rows = len(tiles), tiles[-1][1]
                    act.wait_ge(ms_done, i + 2)
                    nc.scalar.activation(rt[0:rows, 0:n], ms[0:rows, 0:n], ACT.Sqrt).then_inc(rt_done, 1)
                for u, rows, col, src in before or []:
                    for j in range(2):
                        act.wait_ge(tr_done, 4 * ip + 2 * u + j + 5)
                        nc.scalar.copy(hT_hi[:, 4 * j:4 * j + 4, ds(col, rows)],
                                       banks[2 * u + j][:, :].rearrange("p (k n) -> p k n", k=4)[:, :, 0:rows]).then_inc(hi_done, 1)
            pairs(act, body)

        @block.vector
        def _(dve):
            dve.sem_inc(ms_done, 1)
            dve.sem_inc(ri_done, 1)
            dve.sem_inc(xn_done, 2)
            dve.sem_inc(lo_done, 4)
            dve.wait_ge(g_in, 16)

            def body(i, tiles, ip, before):
                if tiles:
                    n, rows = len(tiles), tiles[-1][1]
                    dve.wait_ge(sq_done, 2 * i + n + 2)
                    nc.vector.tensor_scalar(ms[0:rows, 0:n], ss[0:rows, 0:n], 1.0 / D, EPS, ALU.mult, ALU.add).then_inc(ms_done, 1)
                    dve.wait_ge(rt_done, i + 2)
                    nc.vector.reciprocal(ri[0:rows, 0:n], rt[0:rows, 0:n]).then_inc(ri_done, 1)
                    dve.wait_ge(ri_done, i + 2)
                for u, rows, col, src in tiles or []:
                    nc.vector.scalar_tensor_tensor(xn[0:rows, u, :], x[0:rows, u, :], ri[0:rows, u:u + 1],
                                                   g_bc[0:rows, :], ALU.mult, ALU.mult).then_inc(xn_done, 1)
                for u, rows, col, src in before or []:
                    for j in range(2):
                        dve.wait_ge(hi_done, 4 * ip + 2 * u + j + 5)
                        at = (slice(None), slice(4 * j, 4 * j + 4), ds(col, rows))
                        nc.vector.tensor_tensor(hT_lo[at], banks[2 * u + j][:, :].rearrange("p (k n) -> p k n", k=4)[:, :, 0:rows],
                                                hT_hi[at].bitcast(F32), ALU.subtract).then_inc(lo_done, 1)
            pairs(dve, body)

        @block.tensor
        def _(pe):
            pe.sem_inc(tr_done, 4)

            def body(i, tiles, ip, before):
                for u, rows, col, src in tiles or []:
                    pe.wait_ge(xn_done, 2 * i + u + 3)
                    for j in range(2):
                        pe.wait_ge(lo_done, 4 * i + 2 * u + j + 1)
                        for k in range(4):
                            last = nc.tensor.transpose(banks[2 * u + j][:, k * P:k * P + rows],
                                                       xn[0:rows, u, (4 * j + k) * P:(4 * j + k + 1) * P],
                                                       ident[0:rows, 0:rows])
                        last.then_inc(tr_done, 1)
            pairs(pe, body)


def project(nc, tag, banks, w, hT_hi, hT_lo, zT, segments, forget=None):
    n_tiles = sum(seg[1] for seg in segments)
    n_pairs = n_tiles // 2
    with ExitStack() as s:
        c = Core(nc, s, tag)
        w_raw = c.sb("w_raw", [P, 2, KT, P])
        w_hi = c.sb("w_hi", [P, 2, KT, P], F32R)
        w_lo = c.sb("w_lo", [P, 2, KT, P], F32R)
        z_st = c.sb("z_st", [P, 2, TOK])
        w_in = [c.sem(f"w_loaded{u}") for u in range(2)]
        whi_done = c.sem("w_hi_done")
        wlo_done = c.sem("w_lo_done")
        z_done = c.sem("z_done")
        z_read = c.sem("z_read")
        z_out = [c.sem(f"z_stored{u}") for u in range(2)]
        if forget:
            f_col, bias_f, fT, page_table, logf_cache, past = forget
            ptab = c.sb("ptab", [1, DB * PAGES], I32)
            pt_in, past_in = c.sem("page_table_loaded"), c.sem("past_gates_loaded")
            wf_raw = c.sb("wf_raw", [P, KT, FH])
            b_col = c.sb("b_col", [FH, 1])
            wf_in, b_in = c.sem("wf_loaded"), c.sem("bias_loaded")
        block = s.enter_context(nc.Block())
        w_v = w.rearrange("(k p) n -> p k n", p=P)

        def pairs(eng, body):
            base = 0
            for col0, n, row0, func in segments:
                with eng.Fori(0, n // 2) as i:
                    for u in range(2):
                        body(base // 2 + i, u, col0 + (2 * i + u) * P, row0 + (2 * i + u) * P, func)
                base += n

        @block.sync
        def _(sp):
            if forget:
                sp.dma_start(wf_raw[:, :, :], w_v[:, :, f_col:f_col + FH]).then_inc(wf_in, 16)
                sp.dma_start(b_col[:, :], bias_f.unsqueeze(1)).then_inc(b_in, 16)

            def body(pair, u, col, row, func):
                sp.wait_ge(wlo_done, 2 * pair + u + 1)
                sp.dma_start(w_raw[:, u, :, :], w_v[:, :, ds(col, P)]).then_inc(w_in[u], 16)
            pairs(sp, body)

        if forget:
            @block.gpsimd
            def _(pool):
                pool.dma_start(ptab[:, :], page_table.rearrange("(o b) n -> o (b n)", o=1)).then_inc(pt_in, 16)
                pool.wait_ge(pt_in, 16)
                for b in range(DB):
                    with pool.Fori(0, PAGES) as n:
                        page = pool.value_load(ptab[0:1, ds(b * PAGES + n, 1)], min_val=0, max_val=logf_cache.shape[0] - 1)
                        pool.dma_start(past[:, b, ds(n, 1), :].rearrange("p o h -> p (o h)"),
                                       logf_cache[ds(page, 1), :, :].rearrange("o p h -> (o p) h")).then_inc(past_in, 16)
                pool.wait_ge(past_in, 16 * DB * PAGES)

        @block.vector
        def _(dve):
            dve.sem_inc(wlo_done, 2)

            def body(pair, u, col, row, func):
                dve.wait_ge(w_in[u], 16 * (pair + 1))
                dve.wait_ge(z_done, CH * (2 * pair + u + 1))
                nc.vector.tensor_copy(w_hi[:, u, :, :], w_raw[:, u, :, :]).then_inc(whi_done, 1)
                dve.wait_ge(whi_done, 2 * pair + u + 1)
                nc.vector.tensor_tensor(w_lo[:, u, :, :], w_raw[:, u, :, :], w_hi[:, u, :, :].bitcast(F32),
                                        ALU.subtract).then_inc(wlo_done, 1)
            pairs(dve, body)
            if forget:
                dve.wait_ge(wf_in, 16)
                dve.wait_ge(z_done, CH * (n_tiles + 1))
                nc.vector.tensor_copy(w_hi[:, 0, :, 0:FH], wf_raw[:, :, :]).then_inc(whi_done, 1)
                dve.wait_ge(whi_done, n_tiles + 1)
                nc.vector.tensor_tensor(w_lo[:, 0, :, 0:FH], wf_raw[:, :, :], w_hi[:, 0, :, 0:FH].bitcast(F32),
                                        ALU.subtract).then_inc(wlo_done, 1)

        @block.tensor
        def _(pe):
            pe.sem_inc(z_done, 2 * CH)

            def chunk(hi, lo, ch):
                out = banks[ch][:, 0:CW]
                for k in range(KT):
                    h_h, h_l = hT_hi[:, k, ch * CW:(ch + 1) * CW], hT_lo[:, k, ch * CW:(ch + 1) * CW]
                    nc.tensor.matmul(out, hi[:, k, :], h_h, start=(k == 0), stop=False)
                    nc.tensor.matmul(out, hi[:, k, :], h_l, start=False, stop=False)
                    last = nc.tensor.matmul(out, lo[:, k, :], h_h, start=False, stop=(k == KT - 1))
                return last

            def body(pair, u, col, row, func):
                pe.wait_ge(wlo_done, 2 * pair + u + 3)
                for ch in range(CH):
                    pe.wait_ge(z_read, CH * (2 * pair + u) + ch + 1)
                    last = chunk(w_hi[:, u, :, :], w_lo[:, u, :, :], ch)
                    last.then_inc(z_done, 1)
            pairs(pe, body)
            if forget:
                pe.wait_ge(wlo_done, n_tiles + 3)
                for ch in range(CH):
                    pe.wait_ge(z_read, CH * n_tiles + ch + 1)
                    chunk(w_hi[:, 0, :, :], w_lo[:, 0, :, :], ch).then_inc(z_done, 1)

        @block.scalar
        def _(act):
            act.sem_inc(z_read, CH)
            for u in range(2):
                act.sem_inc(z_out[u], 1)

            def body(pair, u, col, row, func):
                act.wait_ge(z_out[u], 16 * pair + 1)
                for ch in range(CH):
                    act.wait_ge(z_done, CH * (2 * pair + u + 2) + ch + 1)
                    nc.scalar.activation(z_st[:, u, ch * CW:(ch + 1) * CW], banks[ch][:, 0:CW],
                                         func).then_inc(z_read, 1)
                act.wait_ge(z_read, CH + CH * (2 * pair + u) + CH)
                act.dma_start(zT[ds(row, P), :], z_st[:, u, :]).then_inc(z_out[u], 16)
            pairs(act, body)
            if forget:
                act.wait_ge(b_in, 16)
                for ch in range(CH):
                    act.wait_ge(z_done, CH * (n_tiles + 2) + ch + 1)
                    nc.scalar.activation(fT[:, ch * CW:(ch + 1) * CW], banks[ch][0:FH, 0:CW], ACT.Identity,
                                         bias=b_col[:, :]).then_inc(z_read, 1)
            for u in range(2):
                act.wait_ge(z_out[u], 16 * n_pairs + 1)


def forget_gates(nc, const, banks, fT, past0, lf_prompt, lf_sample, cT, sufT, cnew, cnew_q):
    ident, ones = const["ident"], const["ones"]
    with ExitStack() as s:
        c = Core(nc, s, "fg")
        upto = c.sb("upto", [P, P])
        after = c.sb("after", [P, P])
        mag = c.sb("mag", [FH, TOK])
        e = c.sb("e", [FH, TOK])
        low = c.sb("low", [FH, TOK])
        lfT = c.sb("lfT", [FH, TOK])
        lf = c.sb("lf", [P, NQ + 1, FH])
        pad = [c.sb(f"pad{n}", [P, NQ // 2 + NQ, FH]) for n in range(2)]
        past = [past0, c.sb("past1", [P, DB, PAGES + PAGES // 2, FH])]
        past_e = c.sb("past_e", [P, DB * FH])
        lfp = c.sb("lfp", [P, PAGES, DB * FH])
        ex = c.sb("ex", [P, PAGES, DB * FH])
        c_row = c.sb("c_row", [FH, SEQ])
        suf_row = c.sb("suf_row", [DB * FH, SEQ])
        cn = c.sb("cn", [FH, 2, NS])
        tri = c.sem("triangles_made")
        act_d, dve_d = c.sem("act_steps"), c.sem("dve_steps")
        zer, scan_d, pscan_d = c.sem("zeroed"), c.sem("scan_steps"), c.sem("past_scan_steps")
        tr_d, lf_d, ct_d, suf_d = c.sem("gates_transposed"), c.sem("lf_ready"), c.sem("c_summed"), c.sem("suf_summed")
        row_d, cn_d, out_d = c.sem("rows_ready"), c.sem("cnew_ready"), c.sem("stored")
        block = s.enter_context(nc.Block())

        @block.sync
        def _(sp):
            sp.wait_ge(lf_d, 2)
            sp.dma_start(lf_prompt.rearrange("n p h -> p n h"), lf[:, 0:NQ, :]).then_inc(out_d, 16)
            sp.dma_start(lf_sample.rearrange("b t h -> (b t) h"), lf[0:NS, NQ, :]).then_inc(out_d, 16)
            sp.wait_ge(cn_d, TN + 1)
            sp.dma_start(cnew[:, :], cn[:, 0, :]).then_inc(out_d, 16)
            sp.dma_start(cnew_q.rearrange("h (t b) -> h t b", t=TN),
                         cn[:, 1, :].rearrange("h (t b) -> h t b", t=TN)).then_inc(out_d, 16)
            sp.wait_ge(row_d, 4)
            sp.dma_start(cT[:, :], c_row[:, :]).then_inc(out_d, 16)
            sp.wait_ge(row_d, 8)
            for q in range(TN):
                sp.dma_start(sufT.rearrange("(r q) n -> q r n", q=TN)[q], suf_row[:, :]).then_inc(out_d, 16)
            sp.wait_ge(out_d, 16 * (5 + TN))

        @block.gpsimd
        def _(pool):
            nc.gpsimd.memset(upto[:, :], 1.0).then_inc(tri, 1)
            nc.gpsimd.memset(after[:, :], 1.0).then_inc(tri, 1)
            nc.gpsimd.memset(pad[0][:, :, :], 0.0).then_inc(zer, 1)
            nc.gpsimd.memset(pad[1][:, :, :], 0.0).then_inc(zer, 1)
            nc.gpsimd.memset(past[0][:, :, PAGES:, :], 0.0).then_inc(zer, 1)
            nc.gpsimd.memset(past[1][:, :, :, :], 0.0).then_inc(zer, 1)
            pool.wait_ge(tri, 2)
            nc.gpsimd.affine_select(out=upto[:, :], in_=upto[:, :], compare_op=ALU.is_ge, fill=0.0, base=0,
                                    pattern=[[1, P]], channel_multiplier=-1).then_inc(tri, 1)
            nc.gpsimd.affine_select(out=after[:, :], in_=after[:, :], compare_op=ALU.is_gt, fill=0.0, base=0,
                                    pattern=[[-1, P]], channel_multiplier=1).then_inc(tri, 1)
            pool.wait_ge(tri, 4)

        @block.scalar
        def _(act):
            nc.scalar.activation(mag[:, :], fT[:, :], ACT.Abs).then_inc(act_d, 1)
            act.wait_ge(act_d, 1)
            nc.scalar.activation(e[:, :], mag[:, :], ACT.Exp, scale=-1.0).then_inc(act_d, 1)
            act.wait_ge(act_d, 2)
            nc.scalar.activation(e[:, :], e[:, :], ACT.Ln, bias=1.0).then_inc(act_d, 1)
            for n in range(4):
                act.wait_ge(ct_d, n + 1)
                nc.scalar.copy(c_row[:, n * 512:(n + 1) * 512], banks[n][0:FH, :]).then_inc(row_d, 1)
            for n in range(4):
                act.wait_ge(suf_d, n + 1)
                nc.scalar.copy(suf_row[:, n * 512:(n + 1) * 512], banks[4 + n % 2][0:DB * FH, :]).then_inc(row_d, 1)

        @block.vector
        def _(dve):
            nc.vector.tensor_scalar_min(low[:, :], fT[:, :], 0.0).then_inc(dve_d, 1)
            dve.wait_ge(dve_d, 1)
            dve.wait_ge(act_d, 3)
            nc.vector.tensor_sub(lfT[:, :], low[:, :], e[:, :]).then_inc(dve_d, 1)
            dve.wait_ge(dve_d, 2)
            news = lfT[:, SEQ:TOK].rearrange("h (b t) -> h b t", t=TN)
            sums = cn[:, 0, :].rearrange("h (b t) -> h b t", t=TN)
            nc.vector.tensor_copy(sums[:, :, 0], news[:, :, 0]).then_inc(cn_d, 1)
            for t in range(1, TN):
                dve.wait_ge(cn_d, t)
                nc.vector.tensor_add(sums[:, :, t], sums[:, :, t - 1], news[:, :, t]).then_inc(cn_d, 1)
            dve.wait_ge(cn_d, TN)
            nc.vector.tensor_copy(cn[:, 1, :].rearrange("h (t b) -> h b t", t=TN), sums).then_inc(cn_d, 1)
            dve.wait_ge(tr_d, 1)
            gates = banks[6][:, 0:(NQ + 1) * FH].rearrange("p (n h) -> p n h", h=FH)
            nc.vector.tensor_copy(lf[:, 0:NQ, :], gates[:, 0:NQ, :]).then_inc(lf_d, 1)
            nc.vector.tensor_copy(lf[0:NS, NQ, :], gates[0:NS, NQ, :]).then_inc(lf_d, 1)
            dve.wait_ge(lf_d, 2)
            dve.wait_ge(zer, 4)
            Z = NQ // 2
            nc.vector.tensor_copy(pad[0][:, Z:, :], lf[:, 0:NQ, :]).then_inc(scan_d, 1)
            for n, step in enumerate((1, 2, 4, 8)):
                dve.wait_ge(scan_d, n + 1)
                nc.vector.tensor_add(pad[(n + 1) % 2][:, Z:, :], pad[n % 2][:, Z:, :],
                                     pad[n % 2][:, Z - step:Z - step + NQ, :]).then_inc(scan_d, 1)
            nc.vector.tensor_copy(lfp[:, :, :].rearrange("p n (b h) -> p b n h", b=DB),
                                  past[0][:, :, 0:PAGES, :]).then_inc(pscan_d, 1)
            for n, step in enumerate((1, 2, 4, 8)):
                dve.wait_ge(pscan_d, n + 1)
                nc.vector.tensor_add(past[(n + 1) % 2][:, :, 0:PAGES, :], past[n % 2][:, :, 0:PAGES, :],
                                     past[n % 2][:, :, step:step + PAGES, :]).then_inc(pscan_d, 1)
            dve.wait_ge(pscan_d, 5)
            nc.vector.tensor_copy(ex[:, :, :].rearrange("p n (b h) -> p b n h", b=DB),
                                  past[0][:, :, 1:PAGES + 1, :]).then_inc(pscan_d, 1)

        @block.tensor
        def _(pe):
            pe.wait_ge(dve_d, 2)
            for n in range(NQ + 1):
                rows = min(P, TOK - n * P)
                last = nc.tensor.transpose(banks[6][0:rows, n * FH:(n + 1) * FH], lfT[:, n * P:n * P + rows],
                                           ident[0:FH, 0:FH])
            last.then_inc(tr_d, 1)
            pe.wait_ge(scan_d, 5)
            pe.wait_ge(tri, 4)
            Z = NQ // 2
            for n in range(NQ):
                out = banks[n // 4][0:FH, n % 4 * P:(n % 4 + 1) * P]
                nc.tensor.matmul(out, lf[:, n, :], upto[:, :], start=True, stop=False)
                last = nc.tensor.matmul(out, pad[0][:, Z - 1 + n, :], ones[:, :], start=False, stop=True)
                if n % 4 == 3:
                    last.then_inc(ct_d, 1)
            pe.wait_ge(pscan_d, 6)
            for n in range(PAGES):
                g = n // 4
                if n % 4 == 0 and g >= 2:
                    pe.wait_ge(row_d, 4 + g - 1)
                out = banks[4 + g % 2][0:DB * FH, n % 4 * P:(n % 4 + 1) * P]
                nc.tensor.matmul(out, lfp[:, n, :], after[:, :], start=True, stop=False)
                last = nc.tensor.matmul(out, ex[:, n, :], ones[:, :], start=False, stop=True)
                if n % 4 == 3:
                    last.then_inc(suf_d, 1)


def fox_attention(nc, const, banks, zT, cT, bT, k_out, v_out):
    ident, ones, ident_b, mask_b = (const[n] for n in ("ident", "ones", "ident_b", "mask_b"))
    QB = 2
    QW = QB * P
    NCH = NQ // QB
    ND = NQ // 4
    pieces = [(q + 4) // 4 for q in range(NQ)]
    first = [sum(pieces[:q]) for q in range(NQ + 1)]
    NP = first[NQ]
    TG = 8
    S_BANKS, T_BANKS = banks[0:4], banks[4:6]
    O_BANK, R_BANK = banks[6], banks[7]
    NB = 4
    LAG = 2
    with ExitStack() as s:
        c = Core(nc, s, "fa")
        q_raw, k_raw, v_raw = (c.sb(n, [P, SEQ]) for n in ("q_raw", "k_raw", "v_raw"))
        q_hi, q_lo, k_hi, k_lo = (c.sb(n, [P, SEQ], F32R) for n in ("q_hi", "q_lo", "k_hi", "k_lo"))
        v_hi, v_lo = (c.sb(n, [P, NQ, P], F32R) for n in ("v_hi", "v_lo"))
        c_bc = c.sb("c_bc", [P, SEQ])
        decay = c.sb("decay", [P, SEQ])
        tok = c.sb("tok", [P, 4, 4, P])
        sc = c.sb("sc", [P, NB, SEQ])
        pT_hi, pT_lo = (c.sb(n, [P, 2, NQ, QW], F32R) for n in ("pT_hi", "pT_lo"))
        gate = c.sb("gate", [P, 2, QW])
        mix = c.sb("mix", [P, 2, QW])
        mx = c.sb("mx", [P, NB, 4])
        nm = c.sb("nm", [P, NB])
        rs = c.sb("rs", [P, 2, QB])
        rr = c.sb("rr", [P, 2, QB])
        dg = c.sb("dg", [P, QB, P])

        q_in, k_in, v_in, c_in = (c.sem(n) for n in ("q_loaded", "k_loaded", "v_loaded", "c_loaded"))
        g_in = [c.sem(f"gate_loaded{n}") for n in range(2)]
        hi_d = c.sem("qk_hi_done")
        lo_d = c.sem("qk_lo_done")
        kvt = c.sem("kv_transposed")
        kve = c.sem("kv_tokens_ready")
        vhi, vlo = c.sem("v_hi_done"), c.sem("v_lo_done")
        tok_out = [c.sem(f"tokens_stored{n}") for n in range(4)]
        dec_d = c.sem("decay_ready")
        s_done = c.sem("scores_done")
        seen = c.sem("scores_seen")
        s_used = c.sem("scores_used")
        nm_d = c.sem("maxima_ready")
        p_done = c.sem("exp_done")
        t_done = c.sem("p_transposed")
        th_d = c.sem("pT_hi_done")
        tl_d = c.sem("pT_lo_done")
        rr_d = c.sem("row_inverse_ready")
        dg_d = c.sem("diagonals_ready")
        r_done = c.sem("inverse_spread")
        o_done = c.sem("pv_done")
        gr_d = c.sem("gate_scaled")
        mix_d = c.sem("mix_ready")
        mix_out = c.sem("mix_stored")
        stored = c.sem("mix_stored_seen")
        block = s.enter_context(nc.Block())

        @block.sync
        def _(sp):
            with sp.Fori(0, FH) as h:
                sp.wait_ge(lo_d, 2 * h + 1)
                sp.dma_start(q_raw[:, :], zT[ds(h * P, P), 0:SEQ]).then_inc(q_in, 16)
                sp.wait_ge(kvt, TG * h + 1)
                sp.dma_start(k_raw[:, :], zT[ds(FH * P + h * P, P), 0:SEQ]).then_inc(k_in, 16)
                sp.dma_start(v_raw[:, :], zT[ds(2 * FH * P + h * P, P), 0:SEQ]).then_inc(v_in, 16)
                sp.wait_ge(dec_d, ND * h + 1)
                sp.dma_start(c_bc[:, :], cT[ds(h, 1), :].rearrange("o n -> (o n)").partition_broadcast(P)).then_inc(c_in, 16)
                for j in range(NCH):
                    sp.wait_ge(mix_d, NCH * h + j + 1)
                    sp.dma_start(gate[:, j % 2, :], zT[ds(3 * D + XW + h * P, P), QW * j:QW * (j + 1)]).then_inc(g_in[j % 2], 16)

        @block.gpsimd
        def _(pool):
            pool.sem_inc(stored, 2)
            with pool.Fori(0, FH) as h:
                for j in range(NCH):
                    pool.wait_ge(rr_d, NCH * h + j + 1)
                    pool.wait_ge(r_done, NCH * h + j + 1)
                    nc.gpsimd.tensor_tensor(dg[:, :, :], ident[:, :].unsqueeze(1).broadcast_to([P, QB, P]),
                                            rr[:, j % 2, :].unsqueeze(2).broadcast_to([P, QB, P]), ALU.mult).then_inc(dg_d, 1)
                    pool.wait_ge(mix_d, NCH * h + j + 3)
                    if j:
                        pool.wait_ge(mix_out, 16 * (NCH * h + j))
                        pool.sem_inc(stored, 1)
                    pool.dma_start(bT[ds(h * P, P), QW * j:QW * (j + 1)], mix[:, j % 2, :]).then_inc(mix_out, 16)
                    if j == NCH - 1:
                        pool.wait_ge(mix_out, 16 * (NCH * h + j + 1))
                        pool.sem_inc(stored, 1)

        def steps():
            for q in range(NQ + LAG + 3):
                yield (q if q < NQ else None, q - LAG if LAG <= q < NQ + LAG else None,
                       divmod(q - LAG - QB, QB) if LAG + QB <= q < NQ + LAG + QB else None,
                       (q - LAG - 2 * QB) // QB if q >= LAG + 2 * QB and (q - LAG) % QB == 0 else None)

        def parts(qs, qt):
            return max(pieces[qs] if qs is not None else 0, pieces[qt] if qt is not None else 0)

        @block.tensor
        def _(pe):
            pe.sem_inc(t_done, NP)
            pe.sem_inc(o_done, 2)
            for sem in (kvt, r_done, s_done):
                pe.sem_inc(sem, 1)
            with pe.Fori(0, FH) as h:
                for g in range(TG):
                    raw = k_raw if g < 4 else v_raw
                    if g == 0:
                        pe.wait_ge(k_in, 16 * (h + 1))
                        pe.wait_ge(tl_d, NP * h + 2)
                    if g == 4:
                        pe.wait_ge(v_in, 16 * (h + 1))
                    if g >= 2:
                        pe.wait_ge(kve, TG * h + g - 1)
                    for n in range(4):
                        last = nc.tensor.transpose(T_BANKS[g % 2][:, n * P:(n + 1) * P],
                                                   raw[:, (g % 4 * 4 + n) * P:(g % 4 * 4 + n + 1) * P], ident[:, :])
                    last.then_inc(kvt, 1)
                pe.wait_ge(lo_d, 2 * h + 3)
                for qs, qt, product, _ in steps():
                    if product is not None and product[1] == 1:
                        j = product[0]
                        pe.wait_ge(dg_d, NCH * h + j + 1)
                        pe.wait_ge(mix_d, NCH * h + j + 2)
                        nc.tensor.matmul(R_BANK[:, 0:QW], ones[:, :],
                                         dg[:, :, :].rearrange("p a n -> p (a n)"), start=True, stop=True).then_inc(r_done, 1)
                    n_parts = max(1, parts(qs, qt))
                    for p in range(n_parts):
                        if qs is not None and p < pieces[qs]:
                            g = first[qs] + p
                            k0, w = 512 * p, min(512, (qs + 1) * P - 512 * p)
                            out = S_BANKS[g % 4][:, 0:w]
                            qh, ql = q_hi[:, qs * P:(qs + 1) * P], q_lo[:, qs * P:(qs + 1) * P]
                            last_piece = p == pieces[qs] - 1
                            pe.wait_ge(s_used, NP * h + g + 1)
                            nc.tensor.matmul(out, qh, k_hi[:, k0:k0 + w], start=True, stop=False)
                            nc.tensor.matmul(out, ql, k_hi[:, k0:k0 + w], start=False, stop=False)
                            last = nc.tensor.matmul(out, qh, k_lo[:, k0:k0 + w], start=False, stop=not last_piece)
                            if last_piece:
                                last = nc.tensor.matmul(out[:, w - P:w], ident_b[:, :], mask_b[:, :], start=False, stop=True)
                            last.then_inc(s_done, 1)
                        if product is not None:
                            j, half = product
                            n_keys = QB * (j + 1) // 2
                            late = 1 if half == 0 and n_parts > 1 else 0
                            at, of = max(0, p - late), n_parts - late
                            shared = range(n_keys * at // of, n_keys * (at + 1) // of) if p >= late else ()
                            for n in (n_keys * half + x for x in shared):
                                if n == 0:
                                    pe.wait_ge(mix_d, NCH * h + j + 2)
                                    pe.wait_ge(tl_d, NP * h + first[QB * (j + 1)] + 2)
                                if n % 4 == 0:
                                    pe.wait_ge(vlo, 4 * h + n // 4 + 2)
                                c0 = max(0, n - QB * j) * P
                                out = O_BANK[:, c0:QW]
                                ph, pl = pT_hi[:, j % 2, n, c0:QW], pT_lo[:, j % 2, n, c0:QW]
                                nc.tensor.matmul(out, v_hi[:, n, :], ph, start=(n == 0), stop=False)
                                nc.tensor.matmul(out, v_lo[:, n, :], ph, start=False, stop=False)
                                last = nc.tensor.matmul(out, v_hi[:, n, :], pl, start=False, stop=(n == QB * (j + 1) - 1))
                                if n == QB * (j + 1) - 1:
                                    last.then_inc(o_done, 1)
                        if qt is not None and p < pieces[qt]:
                            g = first[qt] + p
                            if p == 0:
                                pe.wait_ge(p_done, NQ * h + qt + 1)
                            if g < 2:
                                pe.wait_ge(kve, TG * h + TG - 1 + g)
                            else:
                                pe.wait_ge(tl_d, NP * h + g + 1)
                            for n in range(min(4, qt + 1 - 4 * p)):
                                last = nc.tensor.transpose(T_BANKS[g % 2][:, n * P:(n + 1) * P],
                                                           sc[:, qt % NB, (4 * p + n) * P:(4 * p + n + 1) * P], ident[:, :])
                            last.then_inc(t_done, 1)

        @block.scalar
        def _(act):
            for sem in tok_out:
                act.sem_inc(sem, 1)
            with act.Fori(0, FH) as h:
                act.wait_ge(s_done, NP * h + 1)
                act.wait_ge(q_in, 16 * (h + 1))
                nc.scalar.activation(q_hi[:, :], q_raw[:, :], ACT.Copy, scale=SCALE).then_inc(hi_d, 1)
                act.wait_ge(k_in, 16 * (h + 1))
                nc.scalar.activation(k_hi[:, :], k_raw[:, :], ACT.Copy).then_inc(hi_d, 1)
                for g in range(TG):
                    act.wait_ge(kvt, TG * h + g + 2)
                    n = g % 4
                    act.wait_ge(tok_out[n], 16 * (2 * h + g // 4) + 1)
                    if g < 4:
                        act.wait_ge(vlo, 4 * h + 1)
                    nc.scalar.copy(tok[:, n, :, :], T_BANKS[g % 2][:, :].rearrange("p (n d) -> p n d", n=4)).then_inc(kve, 1)
                    act.wait_ge(kve, TG * h + g + 1)
                    dst = (k_out if g < 4 else v_out)[4 * n:4 * n + 4, :, ds(h, 1), :]
                    act.dma_start(dst.rearrange("n p o d -> p n (o d)"), tok[:, n, :, :]).then_inc(tok_out[n], 16)
                for qs, qt, _, _ in steps():
                    if qt is not None:
                        for p in range(pieces[qt]):
                            g = first[qt] + p
                            a, jt = qt % QB, qt // QB
                            nk = min(4, qt + 1 - 4 * p)
                            act.wait_ge(t_done, NP + NP * h + g + 1)
                            if p == 0:
                                act.wait_ge(o_done, NCH * h + jt + 1)
                            nc.scalar.copy(pT_hi[:, jt % 2, 4 * p:4 * p + nk, a * P:(a + 1) * P],
                                           T_BANKS[g % 2][:, 0:nk * P].rearrange("p (n q) -> p n q", q=P)).then_inc(th_d, 1)
                    if qs is not None:
                        act.wait_ge(nm_d, NQ * h + qs + 1)
                        w = (qs + 1) * P
                        nc.scalar.activation(sc[:, qs % NB, 0:w], sc[:, qs % NB, 0:w], ACT.Exp,
                                             bias=nm[:, qs % NB:qs % NB + 1],
                                             accum_out=rs[:, qs // QB % 2, qs % QB:qs % QB + 1]).then_inc(p_done, 1)
            for n in range(4):
                act.wait_ge(tok_out[n], 16 * 2 * FH + 1)

        @block.vector
        def _(dve):
            dve.sem_inc(s_used, 4)
            dve.sem_inc(tl_d, 2)
            dve.sem_inc(mix_d, 2)
            for sem in (lo_d, dec_d, vlo):
                dve.sem_inc(sem, 1)
            with dve.Fori(0, FH) as h:
                dve.wait_ge(hi_d, 2 * h + 1)
                nc.vector.scalar_tensor_tensor(q_lo[:, :], q_raw[:, :], SCALE, q_hi[:, :].bitcast(F32), ALU.mult,
                                               ALU.subtract).then_inc(lo_d, 1)
                dve.wait_ge(hi_d, 2 * h + 2)
                nc.vector.tensor_tensor(k_lo[:, :], k_raw[:, :], k_hi[:, :].bitcast(F32), ALU.subtract).then_inc(lo_d, 1)
                dve.wait_ge(c_in, 16 * (h + 1))
                for qs, qt, _, j in steps():
                    if j is not None:
                        dve.wait_ge(r_done, NCH * h + j + 2)
                        dve.wait_ge(g_in[j % 2], 16 * (NCH // 2 * h + j // 2 + 1))
                        nc.vector.tensor_tensor(gate[:, j % 2, :], gate[:, j % 2, :], R_BANK[:, 0:QW], ALU.mult).then_inc(gr_d, 1)
                        dve.wait_ge(gr_d, NCH * h + j + 1)
                        dve.wait_ge(o_done, NCH * h + j + 3)
                        dve.wait_ge(stored, NCH * h + j + 1)
                        nc.vector.tensor_tensor(mix[:, j % 2, :], gate[:, j % 2, :], O_BANK[:, 0:QW], ALU.mult).then_inc(mix_d, 1)
                    if qs is not None and qs % 4 == 0:
                        jn, w = qs // 4, 512 * (qs // 4 + 1)
                        dve.wait_ge(s_used, 4 + NP * h + first[qs])
                        nc.vector.tensor_scalar(decay[:, 0:w], c_bc[:, 0:w], c_bc[:, qs * P:qs * P + 1], -1.0,
                                                ALU.subtract, ALU.mult).then_inc(dec_d, 1)
                        dve.wait_ge(dec_d, ND * h + jn + 2)
                    for p in range(parts(qs, qt)):
                        if qs is not None and p < pieces[qs]:
                            g, b = first[qs] + p, qs % NB
                            k0, w = 512 * p, min(512, (qs + 1) * P - 512 * p)
                            if p == 0:
                                dve.wait_ge(t_done, NP * h + (NP + first[qs - NB + 1] if qs >= NB else first[qs + NQ - NB + 1]))
                            dve.wait_ge(s_done, NP * h + g + 2)
                            dve.sem_inc(seen, 1)
                            nc.vector.tensor_tensor_reduce(out=sc[:, b, k0:k0 + w], in0=S_BANKS[g % 4][:, 0:w],
                                                           in1=decay[:, k0:k0 + w], scale=1.0, scalar=LOWEST, op0=ALU.add,
                                                           op1=ALU.max, accum_out=mx[:, b, p:p + 1]).then_inc(s_used, 1)
                        if qt is not None and p < pieces[qt]:
                            g = first[qt] + p
                            a = qt % QB
                            nk = min(4, qt + 1 - 4 * p)
                            at = (slice(None), qt // QB % 2, slice(4 * p, 4 * p + nk), slice(a * P, (a + 1) * P))
                            dve.wait_ge(th_d, NP * h + g + 1)
                            nc.vector.tensor_tensor(pT_lo[at], T_BANKS[g % 2][:, 0:nk * P].rearrange("p (n q) -> p n q", q=P),
                                                    pT_hi[at].bitcast(F32), ALU.subtract).then_inc(tl_d, 1)
                        if qs is not None and p == pieces[qs] - 1:
                            b = qs % NB
                            dve.wait_ge(s_used, 4 + NP * h + first[qs + 1])
                            nc.vector.tensor_reduce(nm[:, b:b + 1], mx[:, b, 0:pieces[qs]], axis=AX.X, op=ALU.max,
                                                    negate=True).then_inc(nm_d, 1)
                    if qt is not None and qt % QB == 0 and (qs is None or qs % QB == 0):
                        jr = qt // QB
                        dve.wait_ge(p_done, NQ * h + QB * (jr + 1))
                        nc.vector.reciprocal(rr[:, jr % 2, :], rs[:, jr % 2, :]).then_inc(rr_d, 1)
                    if qs is not None and qs < 4:
                        n = qs
                        dve.wait_ge(kve, TG * h + 4 + n + 1)
                        dve.wait_ge(o_done, NCH * h + 2)
                        nc.vector.tensor_copy(v_hi[:, 4 * n:4 * n + 4, :], tok[:, n, :, :]).then_inc(vhi, 1)
                        dve.wait_ge(vhi, 4 * h + n + 1)
                        nc.vector.tensor_tensor(v_lo[:, 4 * n:4 * n + 4, :], tok[:, n, :, :],
                                                v_hi[:, 4 * n:4 * n + 4, :].bitcast(F32), ALU.subtract).then_inc(vlo, 1)


def memory_kv(nc, tag, const, banks, mem, gain, w, k_out, v_out):
    NT = NM // P
    with ExitStack() as outer:
        m = Core(nc, outer, tag)
        mT_hi, mT_lo = (m.sb(n, [P, KT, NM], F32R) for n in ("mT_hi", "mT_lo"))
        norm_transpose(nc, tag + "n", const, banks, None, [(mem[0:P, :], P, 0), (mem[P:NM, :], P, P)], gain, mT_hi, mT_lo)
        with ExitStack() as s:
            c = Core(nc, s, tag + "p")
            raw = c.sb("raw", [P, 2, 2 * XW])
            w_hi, w_lo = (c.sb(n, [P, KT, 2 * XW], F32R) for n in ("w_hi", "w_lo"))
            kv = c.sb("kv", [P, NT, 2, XW])
            w_in = [c.sem(f"w_loaded{n}") for n in range(2)]
            hi_d, lo_d = c.sem("w_hi_done"), c.sem("w_lo_done")
            mm, ev, out_d = c.sem("multiplied"), c.sem("copied"), c.sem("stored")
            block = s.enter_context(nc.Block())

            @block.sync
            def _(sp):
                for k in range(KT):
                    if k >= 2:
                        sp.wait_ge(lo_d, k - 1)
                    sp.dma_start(raw[:, k % 2, :], w[k * P:(k + 1) * P, :]).then_inc(w_in[k % 2], 16)
                for t in range(NT):
                    for half, dst in enumerate((k_out, v_out)):
                        sp.wait_ge(ev, 2 * t + half + 1)
                        sp.dma_start(dst[t * P:(t + 1) * P, :], kv[:, t, half, :]).then_inc(out_d, 16)
                sp.wait_ge(out_d, 16 * 2 * NT)

            @block.vector
            def _(dve):
                for k in range(KT):
                    dve.wait_ge(w_in[k % 2], 16 * (k // 2 + 1))
                    nc.vector.tensor_copy(w_hi[:, k, :], raw[:, k % 2, :]).then_inc(hi_d, 1)
                    dve.wait_ge(hi_d, k + 1)
                    nc.vector.tensor_tensor(w_lo[:, k, :], raw[:, k % 2, :], w_hi[:, k, :].bitcast(F32),
                                            ALU.subtract).then_inc(lo_d, 1)

            @block.tensor
            def _(pe):
                for k in range(KT):
                    pe.wait_ge(lo_d, k + 1)
                    for t in range(NT):
                        for half in range(2):
                            out = banks[2 * t + half][:, :]
                            cols = slice(half * XW, (half + 1) * XW)
                            a_hi, a_lo = mT_hi[:, k, t * P:(t + 1) * P], mT_lo[:, k, t * P:(t + 1) * P]
                            nc.tensor.matmul(out, a_hi, w_hi[:, k, cols], start=(k == 0), stop=False)
                            nc.tensor.matmul(out, a_lo, w_hi[:, k, cols], start=False, stop=False)
                            last = nc.tensor.matmul(out, a_hi, w_lo[:, k, cols], start=False, stop=(k == KT - 1))
                            if k == KT - 1:
                                last.then_inc(mm, 1)

            @block.scalar
            def _(act):
                for n in range(2 * NT):
                    act.wait_ge(mm, n + 1)
                    nc.scalar.copy(kv[:, n // 2, n % 2, :], banks[n][:, :]).then_inc(ev, 1)


def memory_attention(nc, tag, const, banks, zT, xq_row, gate_row, bT, k_mem, v_mem):
    ident, ones = const["ident"], const["ones"]
    NT = NM // P
    NCH, NPR = NQ // 4, NQ // 2
    LAG, NB = 2, 4
    S_BANKS, T_BANKS, O_BANKS, R_BANK, K_BANK = banks[0:2], banks[2:4], banks[4:6], banks[6], banks[7]
    with ExitStack() as s:
        c = Core(nc, s, tag)
        kv_raw = c.sb("kv_raw", [P, 2, NT, XW])
        k_hi, k_lo = (c.sb(n, [P, XH, NM], F32R) for n in ("k_hi", "k_lo"))
        v_hi, v_lo = (c.sb(n, [P, NT, XW], F32R) for n in ("v_hi", "v_lo"))
        q_raw = c.sb("q_raw", [P, 2, 512])
        q_hi, q_lo = (c.sb(n, [P, 2, 512], F32R) for n in ("q_hi", "q_lo"))
        gate, mix = c.sb("gate", [P, 2, 512]), c.sb("mix", [P, 2, 512])
        pr = c.sb("pr", [P, NB, 2, NM])
        pT_hi, pT_lo = (c.sb(n, [P, 2, NT, 512], F32R) for n in ("pT_hi", "pT_lo"))
        nm, rs = c.sb("nm", [P, 2, 2]), c.sb("rs", [P, 2, 4])
        rr, dg = c.sb("rr", [P, 2, 4]), c.sb("dg", [P, 4, P])
        kx = c.sb("kx", [P, 2, NM], F32R)
        vx = c.sb("vx", [P, 2, NT, P], F32R)
        head_part, head_d = c.sem("head_part_copied"), c.sem("head_ready")
        kv_in, kt_d, khi_d, klo_d = (c.sem(n) for n in ("kv_loaded", "k_transposed", "k_hi_done", "k_lo_done"))
        vhi_d, vlo_d = c.sem("v_hi_done"), c.sem("v_lo_done")
        q_in, g_in = ([c.sem(f"{n}{u}") for u in range(2)] for n in ("q_loaded", "gate_loaded"))
        mix_out, stored = c.sem("mix_stored"), c.sem("mix_stored_seen")
        qhi_d, qlo_d = c.sem("q_hi_done"), c.sem("q_lo_done")
        s_done, nm_d, p_done, t_done, th_d, tl_d = (c.sem(n) for n in (
            "scores_done", "maxima_ready", "exp_done", "p_transposed", "pT_hi_done", "pT_lo_done"))
        rr_d, dg_d, r_done, o_done, gr_d, mix_d = (c.sem(n) for n in (
            "row_inverse_ready", "diagonals_ready", "inverse_spread", "pv_done", "gate_scaled", "mix_ready"))
        block = s.enter_context(nc.Block())

        @block.sync
        def _(sp):
            sp.dma_start(kv_raw[:, 0, :, :], k_mem.rearrange("(t p) n -> p t n", p=P)).then_inc(kv_in, 16)
            sp.dma_start(kv_raw[:, 1, :, :], v_mem.rearrange("(t p) n -> p t n", p=P)).then_inc(kv_in, 16)
            with sp.Fori(0, XH) as h:
                for j in range(NCH):
                    sp.wait_ge(qlo_d, NCH * h + j + 1)
                    sp.dma_start(q_raw[:, j % 2, :], zT[ds(xq_row + h * P, P), 512 * j:512 * (j + 1)]).then_inc(q_in[j % 2], 16)

        @block.gpsimd
        def _(pool):
            pool.sem_inc(stored, 2)
            with pool.Fori(0, XH) as h:
                for j in range(NCH):
                    pool.wait_ge(mix_d, NCH * h + j + 1)
                    pool.dma_start(gate[:, j % 2, :], zT[ds(gate_row + h * P, P), 512 * j:512 * (j + 1)]).then_inc(g_in[j % 2], 16)
                    pool.wait_ge(rr_d, NCH * h + j + 1)
                    pool.wait_ge(r_done, NCH * h + j + 1)
                    nc.gpsimd.tensor_tensor(dg[:, :, :], ident[:, :].unsqueeze(1).broadcast_to([P, 4, P]),
                                            rr[:, j % 2, :].unsqueeze(2).broadcast_to([P, 4, P]), ALU.mult).then_inc(dg_d, 1)
                    pool.wait_ge(mix_d, NCH * h + j + 3)
                    if j:
                        pool.wait_ge(mix_out, 16 * (NCH * h + j))
                        pool.sem_inc(stored, 1)
                    pool.dma_start(bT[ds(D + h * P, P), 512 * j:512 * (j + 1)], mix[:, j % 2, :]).then_inc(mix_out, 16)
                    if j == NCH - 1:
                        pool.wait_ge(mix_out, 16 * (NCH * h + j + 1))
                        pool.sem_inc(stored, 1)

        def scores(pe, h, n):
            if n % 2 == 0:
                pe.wait_ge(qlo_d, NCH * h + n // 2 + 3)
            pe.wait_ge(p_done, 2 * (NPR * h + n) + 1)
            for a in range(2):
                cols = slice((n % 2 * 2 + a) * P, (n % 2 * 2 + a + 1) * P)
                qh, ql = q_hi[:, n // 2 % 2, cols], q_lo[:, n // 2 % 2, cols]
                out = S_BANKS[n % 2][:, a * NM:(a + 1) * NM]
                yield out, qh, ql

        @block.tensor
        def _(pe):
            pe.sem_inc(s_done, 3)
            pe.sem_inc(r_done, 1)
            pe.sem_inc(t_done, NB)
            pe.sem_inc(o_done, 2)
            pe.wait_ge(kv_in, 32)
            for n in range(XH // 2):
                if n >= 1:
                    pe.wait_ge(klo_d, n)
                for a in range(2):
                    for t in range(NT):
                        h = 2 * n + a
                        last = nc.tensor.transpose(K_BANK[:, a * NM + t * P:a * NM + (t + 1) * P],
                                                   kv_raw[:, 0, t, h * P:(h + 1) * P], ident[:, :])
                last.then_inc(kt_d, 1)
            pe.wait_ge(klo_d, XH // 2)
            pe.wait_ge(vlo_d, 1)

            with pe.Fori(0, XH) as h:
                pe.wait_ge(head_d, h + 1)
                for n in range(NPR + LAG + 1):
                    if n < NPR:
                        for a, (out, qh, ql) in enumerate(scores(pe, h, n)):
                            nc.tensor.matmul(out, qh, kx[:, 0, :], start=True, stop=False)
                            nc.tensor.matmul(out, ql, kx[:, 0, :], start=False, stop=False)
                            last = nc.tensor.matmul(out, qh, kx[:, 1, :], start=False, stop=True)
                        last.then_inc(s_done, 1)
                    if n >= LAG + 2 and n % 2 == 0:
                        j = (n - LAG - 2) // 2
                        jj = NCH * h + j
                        pe.wait_ge(tl_d, NPR * h + 2 * j + 2 + 2)
                        pe.wait_ge(mix_d, jj + 2)
                        out = O_BANKS[j % 2][:, :]
                        for t in range(NT):
                            nc.tensor.matmul(out, vx[:, 0, t, :], pT_hi[:, j % 2, t, :], start=(t == 0), stop=False)
                            nc.tensor.matmul(out, vx[:, 1, t, :], pT_hi[:, j % 2, t, :], start=False, stop=False)
                            last = nc.tensor.matmul(out, vx[:, 0, t, :], pT_lo[:, j % 2, t, :], start=False, stop=(t == NT - 1))
                        last.then_inc(o_done, 1)
                        pe.wait_ge(dg_d, jj + 1)
                        pe.wait_ge(gr_d, jj + 1)
                        nc.tensor.matmul(R_BANK[:, :], ones[:, :], dg[:, :, :].rearrange("p a n -> p (a n)"),
                                         start=True, stop=True).then_inc(r_done, 1)
                    if LAG <= n < NPR + LAG:
                        m = n - LAG
                        pe.wait_ge(p_done, 2 * (NPR * h + m) + 2 + 3)
                        pe.wait_ge(tl_d, NPR * h + m + 1)
                        for t in range(NT):
                            for a in range(2):
                                last = nc.tensor.transpose(T_BANKS[m % 2][:, (2 * t + a) * P:(2 * t + a + 1) * P],
                                                           pr[:, m % NB, a, t * P:(t + 1) * P], ident[:, :])
                        last.then_inc(t_done, 1)

        @block.scalar
        def _(act):
            def queries(h, j):
                act.wait_ge(q_in[j % 2], 16 * (NCH // 2 * h + j // 2 + 1))
                act.wait_ge(s_done, NPR * h + 2 * j + 1)
                nc.scalar.activation(q_hi[:, j % 2, :], q_raw[:, j % 2, :], ACT.Copy, scale=SCALE).then_inc(qhi_d, 1)

            act.sem_inc(p_done, 3)
            for n in range(XH // 2):
                act.wait_ge(kt_d, n + 1)
                nc.scalar.copy(k_hi[:, 2 * n:2 * n + 2, :], K_BANK[:, :].rearrange("p (a m) -> p a m", a=2)).then_inc(khi_d, 1)
            with act.Fori(0, XH) as h:
                queries(h, 0)
                for n in range(NPR + LAG + 1):
                    if n % 2 == 0 and n + 2 < NPR:
                        queries(h, n // 2 + 1)
                    if LAG <= n < NPR + LAG:
                        m = n - LAG
                        act.wait_ge(t_done, NPR * h + m + NB + 1)
                        if m % 2 == 0:
                            act.wait_ge(o_done, NCH * h + m // 2 + 1)
                        nc.scalar.copy(pT_hi[:, m // 2 % 2, :, m % 2 * 256:m % 2 * 256 + 256],
                                       T_BANKS[m % 2][:, :].rearrange("p (t q) -> p t q", t=NT)).then_inc(th_d, 1)
                    if n < NPR:
                        for a in range(2):
                            act.wait_ge(nm_d, NPR * h + n + 1)
                            if a == 0:
                                act.wait_ge(t_done, NPR * h + n + 1)
                            nc.scalar.activation(pr[:, n % NB, a, :], S_BANKS[n % 2][:, a * NM:(a + 1) * NM], ACT.Exp,
                                                 bias=nm[:, n % 2, a:a + 1],
                                                 accum_out=rs[:, n // 2 % 2, n % 2 * 2 + a:n % 2 * 2 + a + 1]).then_inc(p_done, 1)
        @block.vector
        def _(dve):
            def queries(h, j):
                dve.wait_ge(qhi_d, NCH * h + j + 1)
                nc.vector.scalar_tensor_tensor(q_lo[:, j % 2, :], q_raw[:, j % 2, :], SCALE,
                                               q_hi[:, j % 2, :].bitcast(F32), ALU.mult, ALU.subtract).then_inc(qlo_d, 1)

            dve.sem_inc(tl_d, 2)
            dve.sem_inc(qlo_d, 2)
            dve.sem_inc(mix_d, 2)
            dve.sem_inc(gr_d, 1)
            for n in range(XH // 2):
                dve.wait_ge(khi_d, n + 1)
                nc.vector.tensor_tensor(k_lo[:, 2 * n:2 * n + 2, :], K_BANK[:, :].rearrange("p (a m) -> p a m", a=2),
                                        k_hi[:, 2 * n:2 * n + 2, :].bitcast(F32), ALU.subtract).then_inc(klo_d, 1)
            dve.wait_ge(kv_in, 32)
            nc.vector.tensor_copy(v_hi[:, :, :], kv_raw[:, 1, :, :]).then_inc(vhi_d, 1)
            dve.wait_ge(vhi_d, 1)
            nc.vector.tensor_tensor(v_lo[:, :, :], kv_raw[:, 1, :, :], v_hi[:, :, :].bitcast(F32), ALU.subtract).then_inc(vlo_d, 1)
            dve.wait_ge(vlo_d, 1)
            dve.wait_ge(klo_d, XH // 2)
            with dve.Fori(0, XH) as h:
                queries(h, 0)
                dve.wait_ge(o_done, NCH * h + 2)
                nc.vector.tensor_copy(kx[:, 0, :], k_hi[:, ds(h, 1), :].rearrange("p o m -> p (o m)").bitcast(F32)).then_inc(head_part, 1)
                nc.vector.tensor_copy(kx[:, 1, :], k_lo[:, ds(h, 1), :].rearrange("p o m -> p (o m)").bitcast(F32)).then_inc(head_part, 1)
                nc.vector.tensor_copy(vx[:, 0, :, :], v_hi[:, :, ds(h * P, P)].bitcast(F32)).then_inc(head_part, 1)
                dve.wait_ge(head_part, 3 * h + 3)
                nc.vector.tensor_copy(vx[:, 1, :, :], v_lo[:, :, ds(h * P, P)].bitcast(F32)).then_inc(head_d, 1)
                for n in range(NPR + LAG + 1):
                    if n < NPR:
                        dve.wait_ge(s_done, NPR * h + n + 4)
                        dve.wait_ge(p_done, 2 * (NPR * h + n) + 1)
                        nc.vector.tensor_reduce(nm[:, n % 2, :], S_BANKS[n % 2][:, :].rearrange("p (a m) -> p a m", a=2),
                                                axis=AX.X, op=ALU.max, negate=True).then_inc(nm_d, 1)
                    if n % 2 == 0 and n + 2 < NPR:
                        queries(h, n // 2 + 1)
                    if LAG <= n < NPR + LAG:
                        m = n - LAG
                        dve.wait_ge(th_d, NPR * h + m + 1)
                        at = (slice(None), m // 2 % 2, slice(None), slice(m % 2 * 256, m % 2 * 256 + 256))
                        nc.vector.tensor_tensor(pT_lo[at], T_BANKS[m % 2][:, :].rearrange("p (t q) -> p t q", t=NT),
                                                pT_hi[at].bitcast(F32), ALU.subtract).then_inc(tl_d, 1)
                        if m % 2 == 1:
                            dve.wait_ge(p_done, 2 * (NPR * h + m) + 5)
                            nc.vector.reciprocal(rr[:, m // 2 % 2, :], rs[:, m // 2 % 2, :]).then_inc(rr_d, 1)
                    if n >= LAG + 2 and n % 2 == 0:
                        j = (n - LAG - 2) // 2
                        jj = NCH * h + j
                        dve.wait_ge(r_done, jj + 2)
                        dve.wait_ge(g_in[j % 2], 16 * (NCH // 2 * h + j // 2 + 1))
                        nc.vector.tensor_tensor(gate[:, j % 2, :], gate[:, j % 2, :], R_BANK[:, :], ALU.mult).then_inc(gr_d, 1)
                        dve.wait_ge(gr_d, jj + 2)
                        dve.wait_ge(o_done, jj + 3)
                        dve.wait_ge(stored, NCH * h + j + 1)
                        nc.vector.tensor_tensor(mix[:, j % 2, :], gate[:, j % 2, :], O_BANKS[j % 2][:, :], ALU.mult).then_inc(mix_d, 1)


def output_projection(nc, tag, banks, bT, w, gain, x_prompt, x_sample, y_prompt, y_sample):
    NK = BW // P
    with ExitStack() as s:
        c = Core(nc, s, tag)
        w_raw = c.sb("w_raw", [P, 2, D])
        w_hi, w_lo = (c.sb(n, [P, NK, D], F32R) for n in ("w_hi", "w_lo"))
        b_raw = c.sb("b_raw", [P, 2, NK, P])
        b_hi, b_lo = (c.sb(n, [P, 2, NK, P], F32R) for n in ("b_hi", "b_lo"))
        x = c.sb("x", [P, 2, D])
        y = c.sb("y", [P, 2, D])
        g_bc = c.sb("g_bc", [P, D])
        ss, st = c.sb("ss", [P, 2, 2]), c.sb("st", [P, 2, 4])
        w_in, b_in, x_in = ([c.sem(f"{n}{u}") for u in range(2)] for n in ("w_loaded", "b_loaded", "x_loaded"))
        y_out, stored = c.sem("y_stored"), c.sem("y_stored_seen")
        g_in, whi_d, wlo_d = c.sem("gain_loaded"), c.sem("w_hi_done"), c.sem("w_lo_done")
        bhi_d, blo_d = c.sem("b_hi_done"), c.sem("b_lo_done")
        mm = c.sem("multiplied")
        sq_d, ms_d, rt_d, ri_d = (c.sem(n) for n in ("sumsq_done", "meansq_done", "root_done", "rinv_done"))
        yn_d, yx_d = c.sem("y_normed"), c.sem("y_ready")
        block = s.enter_context(nc.Block())
        b_v = bT.rearrange("(k p) n -> p k n", p=P)
        T = NQ + 1

        def tiles(eng, body):
            with eng.Fori(0, NQ // 2) as i:
                for u in range(2):
                    body(i, u, 2 * i + u, P, (2 * i + u) * P, x_prompt, y_prompt)
            body(NQ // 2, 0, NQ, NS, SEQ, None, None)

        @block.sync
        def _(sp):
            sp.dma_start(g_bc[:, :], gain.partition_broadcast(P)).then_inc(g_in, 16)

            def body(pair, u, t, rows, col, xs, ys):
                sp.wait_ge(blo_d, t + 1)
                sp.dma_start(b_raw[:, u, :, 0:rows], b_v[:, :, ds(col, rows)]).then_inc(b_in[u], 16)
                sp.wait_ge(yx_d, t + 1)
                src = x_sample[:, :] if xs is None else xs[ds(col, rows), :]
                sp.dma_start(x[0:rows, u, :], src).then_inc(x_in[u], 16)
            tiles(sp, body)

        @block.gpsimd
        def _(pool):
            pool.sem_inc(stored, 2)
            def body(pair, u, t, rows, col, xs, ys):
                pool.wait_ge(yx_d, t + 3)
                dst = y_sample[:, :] if ys is None else ys[ds(col, rows), :]
                pool.dma_start(dst, y[0:rows, u, :]).then_inc(y_out, 16)
                pool.wait_ge(y_out, 16 * (t + 1))
                pool.sem_inc(stored, 1)
            tiles(pool, body)

        @block.tensor
        def _(pe):
            pe.sem_inc(mm, 4)

            def body(pair, u, t, rows, col, xs, ys):
                pe.wait_ge(blo_d, t + 3)
                for half in range(2):
                    pe.wait_ge(yn_d, 2 * t + half + 1)
                    out = banks[2 * u + half][:, :]
                    cols = slice(half * 512, (half + 1) * 512)
                    for k in range(NK):
                        if half == 0 and not isinstance(t, int) and u == 0:
                            pe.wait_ge(wlo_d, k + 1)
                        bh, bl = b_hi[:, u, k, :], b_lo[:, u, k, :]
                        nc.tensor.matmul(out, bh, w_hi[:, k, cols], start=(k == 0), stop=False)
                        nc.tensor.matmul(out, bl, w_hi[:, k, cols], start=False, stop=False)
                        last = nc.tensor.matmul(out, bh, w_lo[:, k, cols], start=False, stop=(k == NK - 1))
                    last.then_inc(mm, 1)
            tiles(pe, body)

        @block.scalar
        def _(act):
            for k in range(NK):
                if k >= 2:
                    act.wait_ge(wlo_d, k - 1)
                act.dma_start(w_raw[:, k % 2, :], w[k * P:(k + 1) * P, :]).then_inc(w_in[k % 2], 16)

            def body(pair, u, t, rows, col, xs, ys):
                act.wait_ge(stored, t + 1)
                for half in range(2):
                    act.wait_ge(mm, 2 * t + half + 5)
                    nc.scalar.activation(y[0:rows, u, half * 512:(half + 1) * 512], banks[2 * u + half][0:rows, :],
                                         ACT.Square, accum_out=ss[0:rows, u, half:half + 1]).then_inc(sq_d, 1)
                act.wait_ge(ms_d, 2 * t + 2)
                nc.scalar.activation(st[0:rows, u, 2:3], st[0:rows, u, 1:2], ACT.Sqrt).then_inc(rt_d, 1)
            tiles(act, body)

        @block.vector
        def _(dve):
            dve.sem_inc(blo_d, 2)
            dve.sem_inc(yx_d, 2)
            dve.sem_inc(yn_d, 4)

            def split(pair, u, t, rows):
                dve.wait_ge(b_in[u], 16 * (pair + 1))
                dve.wait_ge(mm, 2 * t + 2)
                nc.vector.tensor_copy(b_hi[:, u, :, 0:rows], b_raw[:, u, :, 0:rows]).then_inc(bhi_d, 1)
                dve.wait_ge(bhi_d, t + 1)
                nc.vector.tensor_tensor(b_lo[:, u, :, 0:rows], b_raw[:, u, :, 0:rows], b_hi[:, u, :, 0:rows].bitcast(F32),
                                        ALU.subtract).then_inc(blo_d, 1)

            split(0, 0, 0, P)
            for k in range(NK):
                dve.wait_ge(w_in[k % 2], 16 * (k // 2 + 1))
                nc.vector.tensor_copy(w_hi[:, k, :], w_raw[:, k % 2, :]).then_inc(whi_d, 1)
                dve.wait_ge(whi_d, k + 1)
                nc.vector.tensor_tensor(w_lo[:, k, :], w_raw[:, k % 2, :], w_hi[:, k, :].bitcast(F32),
                                        ALU.subtract).then_inc(wlo_d, 1)
            dve.wait_ge(g_in, 16)

            def body(pair, u, t, rows, col, xs, ys):
                if u == 0 and rows == P:
                    split(pair, 1, t + 1, P)
                elif rows == P:
                    split_next(pair, t)
                dve.wait_ge(sq_d, 2 * t + 2)
                nc.vector.tensor_tensor(st[0:rows, u, 0:1], ss[0:rows, u, 0:1], ss[0:rows, u, 1:2], ALU.add).then_inc(ms_d, 1)
                dve.wait_ge(ms_d, 2 * t + 1)
                nc.vector.tensor_scalar(st[0:rows, u, 1:2], st[0:rows, u, 0:1], 1.0 / D, EPS, ALU.mult, ALU.add).then_inc(ms_d, 1)
                dve.wait_ge(rt_d, t + 1)
                nc.vector.reciprocal(st[0:rows, u, 3:4], st[0:rows, u, 2:3]).then_inc(ri_d, 1)
                dve.wait_ge(ri_d, t + 1)
                for half in range(2):
                    cols = slice(half * 512, (half + 1) * 512)
                    nc.vector.scalar_tensor_tensor(y[0:rows, u, cols], banks[2 * u + half][0:rows, :], st[0:rows, u, 3:4],
                                                   g_bc[0:rows, cols], ALU.mult, ALU.mult).then_inc(yn_d, 1)
                dve.wait_ge(yn_d, 2 * t + 6)
                dve.wait_ge(x_in[u], 16 * (pair + 1))
                nc.vector.tensor_tensor(y[0:rows, u, :], y[0:rows, u, :], x[0:rows, u, :], ALU.add).then_inc(yx_d, 1)

            def split_next(pair, t):
                split(pair + 1, 0, t + 1, NS_OR_P)

            NS_OR_P = P
            with dve.Fori(0, NQ // 2 - 1) as i:
                for u in range(2):
                    body(i, u, 2 * i + u, P, None, True, True)
            last = NQ // 2 - 1
            NS_OR_P = NS
            for u in range(2):
                body(last, u, 2 * last + u, P, None, True, True)
            body(NQ // 2, 0, NQ, NS, None, None, None)


def sample_attention(nc, tag, const, banks, zT, q_row, gate_row, mix_row, bT, heads, pages, k_page, v_page,
                     page_table=None, sufT=None, cnew=None, cnew_q=None, k_new=None, v_new=None):
    ident = const["ident"]
    fox = sufT is not None
    R = heads * TN
    LO = 32
    GP = 2
    NG = pages // GP
    NB = 2 if NG > 1 else 1
    TB = heads // 4
    KS = min(4, pages)
    VB = 3
    NV = pages + (1 if fox else 0)
    NSC = NG + (1 if fox else 0)
    HW = heads * HD
    W = pages * P
    WP = NV * P
    S_BANKS, T_BANKS, O_BANKS, PT_BANK, X_BANK = banks[0:2], banks[2:4], banks[4:6], banks[6], banks[7]
    with ExitStack() as s:
        c = Core(nc, s, tag)
        q_raw, g_all, out_all = (c.sb(n, [P, heads, NS]) for n in ("q_raw", "gate", "out_all"))
        qs_hi, qs_lo = c.sb("qs_hi", [P, heads, NS], F32R), c.sb("qs_lo", [P, heads, NS], F32R)
        qx = c.sb("qx", [P, heads * (P + TN) + P], F32R)
        k_raw = c.sb("k_raw", [P, KS, HW])
        kT_hi, kT_lo = (c.sb(n, [P, NB, heads, GP * P], F32R) for n in ("kT_hi", "kT_lo"))
        v_raw = c.sb("v_raw", [P, NV, HW])
        v_hi, v_lo = (c.sb(n, [P, VB, HW], F32R) for n in ("v_hi", "v_lo"))
        low = c.sb("low", [LO, GP * P])
        sc = c.sb("sc", [LO, W + (TN if fox else 0)])
        pb = c.sb("pb", [LO, WP])
        pT = c.sb("pT", [P, NV, P], F32R)
        o_sb = c.sb("o_sb", [2 * LO, HW])
        eye2 = c.sb("eye2", [2 * LO, LO])
        nm, rs, rr = c.sb("nm", [LO, 1]), c.sb("rs", [LO, 1]), c.sb("rr", [LO, 1])
        if fox:
            suf = c.sb("suf", [LO, W])
            c_key, c_bias, mask = c.sb("c_key", [R, DB, TN]), c.sb("c_bias", [R, DB, TN]), c.sb("mask", [R, TN])
            c_qry, low_n = c.sb("c_qry", [R, DB]), c.sb("low_n", [LO, TN])
            maskf = c.sb("maskf", [TN, TN])
            kn_raw = c.sb("kn_raw", [P, heads, NS])
            kn_hi, kn_lo = (c.sb(n, [P, heads, NS], F32R) for n in ("kn_hi", "kn_lo"))
            ptab, ptab_v = (c.sb(n, [1, DB * PAGES], I32) for n in ("ptab", "ptab_v"))
            suf_in, tab_in, tabv_in, vn_in, kn_in, mf_d, bias_d, kn_d = (c.sem(n) for n in (
                "suffix_loaded", "table_loaded", "table_v_loaded", "v_new_loaded", "setup_loaded", "mask_made",
                "new_bias_ready", "k_new_split"))
        zero_d, set_in, set_d, eye_d = (c.sem(n) for n in ("zeroed", "queries_loaded", "queries_split", "eye2_made"))
        k_in = [c.sem(f"k_loaded{n}") for n in range(KS)]
        v_in = [c.sem(f"v_loaded{n}") for n in range(pages)]
        kt_d = c.sem("k_transposed")
        kth_d = c.sem("kT_hi_done")
        ktl_d = c.sem("kT_lo_done")
        qx_d = c.sem("queries_placed")
        s_done = c.sem("scores_done")
        low_d = c.sem("low_rows_copied")
        hi_d = c.sem("high_rows_biased")
        sc_d = c.sem("scores_ready")
        nm_d, p_d, rr_d, pn_d = (c.sem(n) for n in ("maximum_ready", "exp_done", "inverse_ready", "p_normalised"))
        pt_d = c.sem("p_transposed")
        p_seen = c.sem("p_seen")
        pth_d, ptl_d = c.sem("pT_hi_done"), c.sem("pT_lo_done")
        vh_d = c.sem("v_hi_done")
        vl_d = c.sem("v_lo_done")
        pv_d = c.sem("pv_done")
        o_d = c.sem("o_copied")
        x_d = c.sem("o_transposed")
        m_d = c.sem("mixed")
        out_d = c.sem("stored")
        NPT = 2 if fox else 1
        block = s.enter_context(nc.Block())
        cols = slice(SEQ, TOK)

        def bodies(eng, body):
            body(0, None)
            with eng.Fori(1, DB) as b:
                body(b, b - 1)
            body(None, DB - 1)

        @block.sync
        def _(sp):
            row = lambda r0: zT[r0:r0 + HW, cols].rearrange("(h p) n -> p h n", p=P)
            sp.dma_start(q_raw[:, :, :], row(q_row)).then_inc(set_in, 16)
            sp.dma_start(g_all[:, :, :], row(gate_row)).then_inc(set_in, 16)
            if fox:
                sp.dma_start(ptab[:, :], page_table.rearrange("(o b) n -> o (b n)", o=1)).then_inc(tab_in, 16)
                sp.dma_start(kn_raw[:, :, :], row(D)).then_inc(kn_in, 16)
                sp.wait_ge(mf_d, 2)
                for h in range(heads):
                    at = slice(TN * h, TN * h + TN)
                    sp.dma_start(mask[at, :], maskf[:, :]).then_inc(kn_in, 16)
                    sp.dma_start(c_key[at, :, :].rearrange("q b t -> q (b t)"),
                                 cnew[h, :].partition_broadcast(TN)).then_inc(kn_in, 16)
                    sp.dma_start(c_qry[at, :], cnew_q[h, :].rearrange("(t b) -> t b", t=TN)).then_inc(kn_in, 16)
                sp.wait_ge(tab_in, 16)

            def body(bk, bv):
                if bk is None:
                    return
                if fox:
                    sp.wait_ge(sc_d, NSC * bk)
                    sp.dma_start(suf[0:R, :], sufT[ds(bk * R, R), :]).then_inc(suf_in, 16)
                for p in range(pages):
                    src = k_page(sp, bk, p, ptab if fox else None)
                    sp.wait_ge(kt_d, TB * (pages * bk + p + 1))
                    sp.dma_start(k_raw[:, p % KS, :], src).then_inc(k_in[p % KS], 16)
            bodies(sp, body)
            sp.wait_ge(m_d, DB + 1)
            sp.dma_start(bT[mix_row:mix_row + HW, cols].rearrange("(h p) n -> p h n", p=P), out_all[:, :, :]).then_inc(out_d, 16)
            sp.wait_ge(out_d, 16)

        @block.gpsimd
        def _(pool):
            if fox:
                pool.dma_start(ptab_v[:, :], page_table.rearrange("(o b) n -> o (b n)", o=1)).then_inc(tabv_in, 16)
                nc.gpsimd.memset(maskf[:, :], 0.0).then_inc(mf_d, 1)
                pool.wait_ge(mf_d, 1)
                nc.gpsimd.affine_select(out=maskf[:, :], in_=maskf[:, :], compare_op=ALU.is_ge, fill=NEG, base=0,
                                        pattern=[[-1, TN]], channel_multiplier=1).then_inc(mf_d, 1)
                nc.gpsimd.memset(v_raw[:, pages, :], 0.0).then_inc(zero_d, 1)
            nc.gpsimd.memset(qx[:, :].bitcast(F32), 0.0).then_inc(zero_d, 1)
            nc.gpsimd.memset(pT[:, :, :].bitcast(F32), 0.0).then_inc(zero_d, 1)
            nc.gpsimd.memset(pb[:, :], 0.0).then_inc(zero_d, 1)
            if fox:
                pool.wait_ge(tabv_in, 16)
                pool.wait_ge(zero_d, 4)

            def body(bk, bv):
                if bk is None:
                    return
                for p in range(pages):
                    src = v_page(pool, bk, p, ptab_v if fox else None)
                    pool.wait_ge(vl_d, NV * bk + p + 1)
                    pool.dma_start(v_raw[:, p, :], src).then_inc(v_in[p], 16)
                if fox:
                    pool.wait_ge(vl_d, NV * bk + NV)
                    pool.dma_start(v_raw[0:TN, pages, :], v_new[ds(TN * bk, TN), :]).then_inc(vn_in, 16)
            bodies(pool, body)

        EV = GP * TB
        PV0 = EV + 2
        NE = max(EV * (NG + 1) + 1, PV0 + TB * NV)

        def stages(e):
            page = lambda x: x // TB if x % TB == 0 and 0 <= x < TB * NV else None
            return (e if e < EV * NG else None,
                    divmod(e - EV, EV) if EV <= e < EV * (NG + 1) else None,
                    e // EV - 2 if e % EV == 0 and e >= 2 * EV and e // EV - 2 < NG else None,
                    page(e - PV0 + 3), page(e - PV0 + 2),
                    divmod(e - PV0, TB) if PV0 <= e < PV0 + TB * NV else None)

        @block.tensor
        def _(pe):
            pe.sem_inc(kt_d, TB * KS)
            pe.sem_inc(s_done, NB)
            pe.sem_inc(pv_d, NV)
            pe.sem_inc(x_d, 1)
            pe.wait_ge(zero_d, 4 if fox else 3)
            pe.wait_ge(eye_d, 1)
            if fox:
                pe.wait_ge(kn_d, 2)

            def body(bk, bv):
                for e in range(NE):
                    i, scored, _, _, _, multiplied = stages(e)
                    if bk is not None and i is not None:
                        p, n = divmod(i, TB)
                        if n == 0:
                            pe.wait_ge(k_in[p % KS], 16 * ((pages // KS) * bk + p // KS + 1))
                        pe.wait_ge(ktl_d, TB * pages * bk + i + 1)
                        for h in range(4):
                            last = nc.tensor.transpose(T_BANKS[i % 2][:, h * P:(h + 1) * P],
                                                       k_raw[:, p % KS, (4 * n + h) * P:(4 * n + h + 1) * P], ident[:, :])
                        last.then_inc(kt_d, 1)
                    if bk is not None and scored is not None:
                        gs, part = scored
                        if gs == 0 and part == 0:
                            pe.wait_ge(qx_d, 2 * bk + 2)
                        if part == 0:
                            pe.wait_ge(ktl_d, TB * (pages * bk + (gs + 1) * GP) + 2)
                            pe.wait_ge(hi_d, NSC * bk + gs + 1)
                            pe.wait_ge(low_d, NSC * bk + gs - NB + 1 if gs >= NB else NSC * bk)
                        out = S_BANKS[gs % NB][:, 0:GP * P]
                        for h in range(part * heads // EV, (part + 1) * heads // EV):
                            q = qx[:, h * P:(h + 1) * P]
                            nc.tensor.matmul(out, q, kT_hi[:, gs % NB, h, :], start=(h == 0), stop=False)
                            last = nc.tensor.matmul(out, q, kT_lo[:, gs % NB, h, :], start=False, stop=(h == heads - 1))
                        if part == EV - 1:
                            last.then_inc(s_done, 1)
                        if fox and scored == (NG - 1, EV - 1):
                            pe.wait_ge(ptl_d, NPT * bk)
                            out = PT_BANK[:, 0:TN]
                            for h in range(heads):
                                q = qx[:, h * P:(h + 1) * P]
                                nc.tensor.matmul(out, q, kn_hi[:, h, ds(TN * bk, TN)], start=(h == 0), stop=False)
                                last = nc.tensor.matmul(out, q, kn_lo[:, h, ds(TN * bk, TN)], start=False, stop=(h == heads - 1))
                            last.then_inc(s_done, 1)
                    if bv is not None and e == EV:
                        pe.wait_ge(pn_d, bv + 1)
                        for p in range(NV):
                            if p == 0:
                                pe.wait_ge(low_d, NSC * (bv + 1))
                                pe.wait_ge(hi_d, NSC * (bv + 1) + NB)
                            if p == 16:
                                pe.wait_ge(m_d, bv + 1)
                            bank = PT_BANK[:, p * LO:(p + 1) * LO] if p < 16 else X_BANK[:, 0:LO]
                            if p in (0, 16):
                                pe.sem_inc(p_seen, 1)
                            last = nc.tensor.transpose(bank[:, 0:R], pb[0:R, p * P:(p + 1) * P], ident[0:R, 0:R])
                            if p in (min(NV, 16) - 1, 16):
                                last.then_inc(pt_d, 1)
                    if bv is not None and multiplied is not None:
                        p, n = multiplied
                        if p == 0 and n == 0:
                            pe.wait_ge(ptl_d, NPT * bv + NPT)
                            pe.wait_ge(o_d, TB * bv + 1)
                        if n == 0:
                            pe.wait_ge(vl_d, NV + NV * bv + p + 1)
                        out = O_BANKS[n][:, :]
                        vs = slice(n * 512, (n + 1) * 512)
                        nc.tensor.matmul(out, pT[:, p, :], v_hi[:, p % VB, vs], start=(p == 0), stop=False)
                        last = nc.tensor.matmul(out, pT[:, p, :], v_lo[:, p % VB, vs], start=False, stop=(p == NV - 1))
                        if n == TB - 1:
                            last.then_inc(pv_d, 1)
                if bv is not None:
                    pe.wait_ge(o_d, TB * bv + TB + 1)
                    if not fox:
                        pe.wait_ge(m_d, bv + 1)
                    for h in range(heads):
                        last = nc.tensor.matmul(X_BANK[:, h * LO:(h + 1) * LO], o_sb[:, h * P:(h + 1) * P], eye2[:, :],
                                                start=True, stop=True)
                    last.then_inc(x_d, 1)
            bodies(pe, body)

        @block.scalar
        def _(act):
            act.sem_inc(o_d, 1)
            act.wait_ge(set_in, 32)
            nc.scalar.activation(qs_hi[:, :, :], q_raw[:, :, :], ACT.Copy, scale=SCALE).then_inc(set_d, 1)
            act.wait_ge(zero_d, 4 if fox else 3)

            def body(bk, bv):
                for e in range(NE):
                    i, _, gs, pv, _, _ = stages(e)
                    if bk is not None and i is not None:
                        g, (p, n) = i // EV, divmod(i, TB)
                        act.wait_ge(kt_d, TB * KS + TB * pages * bk + i + 1)
                        act.wait_ge(s_done, NSC * bk + g + 1)
                        nc.scalar.copy(kT_hi[:, g % NB, 4 * n:4 * n + 4, (p % GP) * P:(p % GP + 1) * P],
                                       T_BANKS[i % 2][:, :].rearrange("p (h n) -> p h n", h=4)).then_inc(kth_d, 1)
                    if bv is not None and e == EV:
                        act.wait_ge(pt_d, NPT * bv + 1)
                        act.wait_ge(pv_d, NV * bv + NV)
                        n = min(NV, 16)
                        nc.scalar.copy(pT[:, 0:n, 0:R], PT_BANK[:, 0:n * LO].rearrange("p (n r) -> p n r", r=LO)[:, :, 0:R]).then_inc(pth_d, 1)
                        if fox:
                            act.wait_ge(pt_d, NPT * bv + 2)
                            nc.scalar.copy(pT[:, 16, 0:R], X_BANK[:, 0:R]).then_inc(pth_d, 1)
                    if bv is not None and pv is not None:
                        act.wait_ge(v_in[pv] if pv < pages else vn_in, 16 * (bv + 1))
                        prev = max(x for x in range(-NV, pv) if x % NV % VB == pv % VB)
                        act.wait_ge(pv_d, NV + NV * bv + prev + 1)
                        nc.scalar.copy(v_hi[:, pv % VB, :], v_raw[:, pv, :]).then_inc(vh_d, 1)
                    if bk is not None and gs is not None:
                        act.wait_ge(s_done, NB + NSC * bk + gs + 1)
                        act.wait_ge(sc_d, NSC * bk + gs)
                        nc.scalar.copy(low[0:R, :], S_BANKS[gs % NB][LO:LO + R, 0:GP * P]).then_inc(low_d, 1)
                        if fox and gs == NG - 1:
                            act.wait_ge(s_done, NB + NSC * bk + NSC)
                            nc.scalar.copy(low_n[0:R, :], PT_BANK[LO:LO + R, 0:TN]).then_inc(low_d, 1)
                if bv is not None:
                    for n in range(TB):
                        act.wait_ge(pv_d, NV + NV * bv + NV)
                        act.wait_ge(x_d, bv + 1)
                        nc.scalar.copy(o_sb[:, n * 512:(n + 1) * 512], O_BANKS[n][0:2 * LO, :]).then_inc(o_d, 1)
                if bk is not None:
                    act.wait_ge(nm_d, bk + 1)
                    act.wait_ge(pt_d, NPT * bk)
                    w = W + (TN if fox else 0)
                    nc.scalar.activation(pb[0:R, 0:w], sc[0:R, 0:w], ACT.Exp, bias=nm[0:R, :],
                                         accum_out=rs[0:R, :]).then_inc(p_d, 1)
            bodies(act, body)

        @block.vector
        def _(dve):
            dve.sem_inc(ktl_d, 2)
            dve.sem_inc(hi_d, NB)
            dve.sem_inc(vl_d, NV)
            dve.sem_inc(m_d, 1)
            nc.vector.tensor_add(eye2[:, :], ident[0:2 * LO, 0:LO], ident[0:2 * LO, LO:2 * LO]).then_inc(eye_d, 1)
            dve.wait_ge(set_d, 1)
            dve.wait_ge(zero_d, 4 if fox else 3)
            nc.vector.scalar_tensor_tensor(qs_lo[:, :, :], q_raw[:, :, :], SCALE, qs_hi[:, :, :].bitcast(F32), ALU.mult,
                                           ALU.subtract).then_inc(set_d, 1)
            if fox:
                dve.wait_ge(kn_in, 16 * (1 + 3 * heads))
                nc.vector.tensor_copy(kn_hi[:, :, :], kn_raw[:, :, :]).then_inc(kn_d, 1)
                dve.wait_ge(kn_d, 1)
                nc.vector.tensor_tensor(kn_lo[:, :, :], kn_raw[:, :, :], kn_hi[:, :, :].bitcast(F32), ALU.subtract).then_inc(kn_d, 1)
                nc.vector.tensor_tensor(c_bias[:, :, :], c_qry[:, :].unsqueeze(2).broadcast_to([R, DB, TN]),
                                        c_key[:, :, :], ALU.subtract).then_inc(bias_d, 1)
                dve.wait_ge(bias_d, 1)
                nc.vector.tensor_tensor(c_bias[:, :, :], c_bias[:, :, :], mask[:, :].unsqueeze(1).broadcast_to([R, DB, TN]),
                                        ALU.add).then_inc(bias_d, 1)
                dve.wait_ge(bias_d, 2)
            dve.wait_ge(set_d, 2)
            dve.wait_ge(set_in, 32)

            def diag(t, off):
                return t[:, off:off + heads * (P + TN)].rearrange("p (h x) -> p h x", x=P + TN)[:, :, 0:TN]

            def body(bk, bv):
                if bk is not None:
                    dve.wait_ge(s_done, NB + NSC * bk)
                    nc.vector.tensor_copy(diag(qx, 0), qs_hi[:, :, ds(TN * bk, TN)].bitcast(F32)).then_inc(qx_d, 1)
                    nc.vector.tensor_copy(diag(qx, LO), qs_lo[:, :, ds(TN * bk, TN)].bitcast(F32)).then_inc(qx_d, 1)
                for e in range(NE):
                    i, _, gs, _, pv, _ = stages(e)
                    if bk is not None and i is not None:
                        g, (p, n) = i // EV, divmod(i, TB)
                        at = (slice(None), g % NB, slice(4 * n, 4 * n + 4), slice((p % GP) * P, (p % GP + 1) * P))
                        dve.wait_ge(kth_d, TB * pages * bk + i + 1)
                        nc.vector.tensor_tensor(kT_lo[at], T_BANKS[i % 2][:, :].rearrange("p (h n) -> p h n", h=4),
                                                kT_hi[at].bitcast(F32), ALU.subtract).then_inc(ktl_d, 1)
                    if bv is not None and e == EV // 2:
                        dve.wait_ge(p_d, bv + 1)
                        nc.vector.reciprocal(rr[0:R, :], rs[0:R, :]).then_inc(rr_d, 1)
                        dve.wait_ge(rr_d, bv + 1)
                        w = W + (TN if fox else 0)
                        nc.vector.tensor_scalar(pb[0:R, 0:w], pb[0:R, 0:w], rr[0:R, :], None, ALU.mult).then_inc(pn_d, 1)
                    if bv is not None and e == EV:
                        n = min(NV, 16)
                        dve.wait_ge(pth_d, NPT * bv + 1)
                        nc.vector.tensor_tensor(pT[:, 0:n, LO:LO + R],
                                                PT_BANK[:, 0:n * LO].rearrange("p (n r) -> p n r", r=LO)[:, :, 0:R],
                                                pT[:, 0:n, 0:R].bitcast(F32), ALU.subtract).then_inc(ptl_d, 1)
                        if fox:
                            dve.wait_ge(pth_d, NPT * bv + 2)
                            nc.vector.tensor_tensor(pT[:, 16, LO:LO + R], X_BANK[:, 0:R], pT[:, 16, 0:R].bitcast(F32),
                                                    ALU.subtract).then_inc(ptl_d, 1)
                    if bv is not None and pv is not None:
                        dve.wait_ge(vh_d, NV * bv + pv + 1)
                        nc.vector.tensor_tensor(v_lo[:, pv % VB, :], v_raw[:, pv, :], v_hi[:, pv % VB, :].bitcast(F32),
                                                ALU.subtract).then_inc(vl_d, 1)
                    if bk is not None and gs is not None:
                        k0 = gs * GP * P
                        dst = sc[0:R, k0:k0 + GP * P]
                        src = S_BANKS[gs % NB][0:R, 0:GP * P]
                        if gs == 0:
                            dve.wait_ge(p_d, bk)
                        if fox:
                            dve.wait_ge(suf_in, 16 * (bk + 1))
                            dve.wait_ge(s_done, NB + NSC * bk + gs + 1)
                            nc.vector.scalar_tensor_tensor(dst, suf[0:R, k0:k0 + GP * P], c_qry[:, ds(bk, 1)], src,
                                                           ALU.add, ALU.add).then_inc(hi_d, 1)
                            dve.wait_ge(hi_d, NB + NSC * bk + gs + 1)
                            dve.wait_ge(low_d, NSC * bk + gs + 1)
                            nc.vector.tensor_tensor(dst, dst, low[0:R, :], ALU.add).then_inc(sc_d, 1)
                        else:
                            dve.wait_ge(low_d, NSC * bk + gs + 1)
                            nc.vector.tensor_tensor(dst, src, low[0:R, :], ALU.add).then_inc(hi_d, 1)
                            dve.wait_ge(hi_d, NB + NSC * bk + gs + 1)
                            dve.sem_inc(sc_d, 1)
                        if fox and gs == NG - 1:
                            dst = sc[0:R, W:W + TN]
                            dve.wait_ge(s_done, NB + NSC * bk + NSC)
                            nc.vector.tensor_tensor(dst, c_bias[:, ds(bk, 1), :].rearrange("r o t -> r (o t)"),
                                                    PT_BANK[0:R, 0:TN], ALU.add).then_inc(hi_d, 1)
                            dve.wait_ge(hi_d, NB + NSC * bk + NSC)
                            dve.wait_ge(low_d, NSC * bk + NSC)
                            nc.vector.tensor_tensor(dst, dst, low_n[0:R, :], ALU.add).then_inc(sc_d, 1)
                        if gs == NG - 1:
                            dve.wait_ge(sc_d, NSC * bk + NSC)
                            nc.vector.tensor_reduce(nm[0:R, :], sc[0:R, :], axis=AX.X, op=ALU.max, negate=True).then_inc(nm_d, 1)
                if bv is not None:
                    dve.wait_ge(x_d, bv + 2)
                    at = (slice(None), slice(None), ds(TN * bv, TN))
                    own = X_BANK[:, 0:heads * (LO + TN)].rearrange("p (h x) -> p h x", x=LO + TN)[:, :, 0:TN]
                    nc.vector.tensor_tensor(out_all[at], own, g_all[at], ALU.mult).then_inc(m_d, 1)
            bodies(dve, body)


def pool_mixing(nc, const, banks, zT, state, w_group, scale, bT, state_prompt, state_sample):
    ident = const["ident"]
    G, CT = 4, 2
    Z = 16
    EXT = HIST + TN
    TAIL = TOK - (SEQ - HIST)
    with ExitStack() as s:
        c = Core(nc, s, "pm")
        u = c.sb("u", [P, 2, CT, Z + SEQ])
        acc = [c.sb(f"acc{n}", [P, CT, Z + SEQ]) for n in range(2)]
        tail, tail_t = c.sb("tail", [P, KT, TAIL]), c.sb("tail_t", [TAIL, D])
        st_raw, ext = c.sb("st_raw", [DB * HIST, D]), c.sb("ext", [P, KT, DB, EXT])
        exa = [c.sb(f"exa{n}", [P, CT, DB, EXT]) for n in range(2)]
        inv = c.sb("inv", [P, Z])
        dd = c.sb("dd", [P, CT, TOK])
        d_hi, d_lo = (c.sb(n, [P, CT, TOK], F32R) for n in ("d_hi", "d_lo"))
        wg_raw = c.sb("wg_raw", [P, G, CT, CT * P])
        wg_hi, wg_lo = (c.sb(n, [P, G, CT, CT * P], F32R) for n in ("wg_hi", "wg_lo"))
        sc_col = c.sb("sc_col", [P, KT])
        gate = c.sb("gate", [P, CT, TOK])
        mix = c.sb("mix", [P, CT, TOK])
        u_in, g_in, m_out = ([c.sem(f"{n}{i}") for i in range(2)] for n in ("u_loaded", "gate_loaded", "mix_stored"))
        tl_in, st_in, w_in, s_in = (c.sem(n) for n in ("tail_loaded", "state_loaded", "w_loaded", "scale_loaded"))
        z_d, inv_d, wh_d, wl_d = (c.sem(n) for n in ("zeroed", "inverse_counts", "w_hi_done", "w_lo_done"))
        tt_d, tc_d, stt_d, ext_d = (c.sem(n) for n in ("tail_transposed", "tail_copied", "state_transposed", "state_copied"))
        sum_v, sum_p, ex_d = c.sem("sums_dve"), c.sem("sums_pool"), c.sem("sample_sums")
        d_d, dh_d, dl_d, y_d, mx_d, out_d = (c.sem(n) for n in ("d_ready", "d_hi_done", "d_lo_done", "y_done", "mix_ready", "stored"))
        block = s.enter_context(nc.Block())
        levels = [g + 1 for g in range(G)]
        before = [sum(levels[:g]) for g in range(G + 1)]

        @block.sync
        def _(sp):
            sp.dma_start(tail[:, :, :], zT[0:D, SEQ - HIST:TOK].rearrange("(k p) n -> p k n", p=P)).then_inc(tl_in, 16)
            sp.dma_start(st_raw[:, :], state.rearrange("b n d -> (b n) d")).then_inc(st_in, 16)
            for g in range(G):
                if g == 0:
                    sp.wait_ge(z_d, 4)
                if g >= 2:
                    sp.wait_ge(d_d, 4 * (g - 1))
                sp.dma_start(u[:, g % 2, :, Z:], zT[g * CT * P:(g + 1) * CT * P, 0:SEQ].rearrange("(c p) n -> p c n", p=P)).then_inc(u_in[g % 2], 16)
                if g == 0:
                    sp.dma_start(wg_raw[:, :, :, :], w_group.rearrange("g (c p) n -> p g c n", p=P)).then_inc(w_in, 16)
                    sp.dma_start(sc_col[:, :], scale.rearrange("(k p) -> p k", p=P), allow_slow_non_contiguous=True).then_inc(s_in, 16)
                if g >= 1:
                    sp.wait_ge(mx_d, CT * CH * g)
                r0 = D + XW + g * CT * P
                sp.dma_start(gate[:, :, :], zT[r0:r0 + CT * P, :].rearrange("(c p) n -> p c n", p=P)).then_inc(g_in[g % 2], 16)
            sp.dma_start(state_sample[:, 0:HIST - TN, :], state[:, TN:HIST, :]).then_inc(out_d, 16)
            sp.wait_ge(tc_d, 2)
            sp.dma_start(state_prompt[:, :], tail_t[0:HIST, :]).then_inc(out_d, 16)
            for b in range(DB):
                sp.dma_start(state_sample[b, HIST - TN:HIST, :], tail_t[HIST + TN * b:HIST + TN * (b + 1), :]).then_inc(out_d, 16)
            sp.wait_ge(out_d, 16 * (2 + DB))

        @block.gpsimd
        def _(pool):
            nc.gpsimd.memset(u[:, 0, :, 0:Z], 0.0).then_inc(z_d, 1)
            nc.gpsimd.memset(u[:, 1, :, 0:Z], 0.0).then_inc(z_d, 1)
            for n in range(2):
                nc.gpsimd.memset(acc[n][:, :, 0:Z], 0.0).then_inc(z_d, 1)
            for t in range(Z):
                nc.gpsimd.memset(inv[:, t:t + 1], 1.0 / (t + 1)).then_inc(inv_d, 1)
            pool.wait_ge(z_d, 4)
            for g in range(G):
                pool.wait_ge(u_in[g % 2], 16 * (g // 2 + 1))
                src = u[:, g % 2, 1, :]
                for n in range(levels[g]):
                    if n:
                        pool.wait_ge(sum_p, before[g] + n)
                    elif g:
                        pool.wait_ge(d_d, 4 * g)
                    dst = acc[n % 2][:, 1, :]
                    nc.gpsimd.tensor_tensor(dst[:, Z:], src[:, Z:], src[:, Z - 2 ** n:Z + SEQ - 2 ** n], ALU.add).then_inc(sum_p, 1)
                    src = dst

        @block.vector
        def _(dve):
            dve.wait_ge(w_in, 16)
            nc.vector.tensor_copy(wg_hi[:, :, :, :], wg_raw[:, :, :, :]).then_inc(wh_d, 1)
            dve.wait_ge(wh_d, 1)
            nc.vector.tensor_tensor(wg_lo[:, :, :, :], wg_raw[:, :, :, :], wg_hi[:, :, :, :].bitcast(F32), ALU.subtract).then_inc(wl_d, 1)
            dve.wait_ge(z_d, 4)
            dve.wait_ge(tl_in, 16)
            nc.vector.tensor_copy(ext[:, :, :, HIST:], tail[:, :, HIST:].rearrange("p k (b t) -> p k b t", b=DB)).then_inc(ext_d, 1)
            for n in range(2):
                dve.wait_ge(stt_d, n + 1)
                nc.vector.tensor_copy(ext[:, 4 * n:4 * n + 4, :, 0:HIST],
                                      banks[6 + n][:, 0:4 * DB * HIST].rearrange("p (k b n) -> p k b n", k=4, b=DB)).then_inc(ext_d, 1)
            dve.wait_ge(ext_d, 3)
            dve.wait_ge(inv_d, Z)
            dve.wait_ge(s_in, 16)
            n_ex = 0
            for g in range(G):
                w = 2 ** (g + 1)
                dve.wait_ge(u_in[g % 2], 16 * (g // 2 + 1))
                src, exs = u[:, g % 2, 0, :], ext[:, CT * g:CT * g + CT, :, :]
                for n in range(levels[g]):
                    sh = 2 ** n
                    if n:
                        dve.wait_ge(sum_v, before[g] + n)
                        dve.wait_ge(ex_d, n_ex)
                    dst = acc[n % 2][:, 0, :]
                    nc.vector.tensor_tensor(dst[:, Z:], src[:, Z:], src[:, Z - sh:Z + SEQ - sh], ALU.add).then_inc(sum_v, 1)
                    src = dst
                    lo = 2 * sh - 1
                    for ct in range(CT):
                        nc.vector.tensor_tensor(exa[n % 2][:, ct, :, lo:], exs[:, ct, :, lo:], exs[:, ct, :, lo - sh:EXT - sh], ALU.add).then_inc(ex_d, 1)
                    n_ex += CT
                    exs = exa[n % 2][:, :, :, :]
                last = acc[(levels[g] - 1) % 2]
                dve.wait_ge(sum_v, before[g + 1])
                dve.wait_ge(sum_p, before[g + 1])
                dve.wait_ge(ex_d, n_ex)
                if g:
                    dve.wait_ge(dl_d, g)
                nc.vector.scalar_tensor_tensor(dd[:, :, 0:SEQ], last[:, :, Z:], 1.0 / w, u[:, g % 2, :, Z:], ALU.mult,
                                               ALU.subtract).then_inc(d_d, 1)
                for ct in range(CT):
                    last_d = nc.vector.scalar_tensor_tensor(
                        dd[:, ct, SEQ:].rearrange("p (b t) -> p b t", t=TN), exs[:, ct, :, HIST:], 1.0 / w,
                        ext[:, CT * g + ct, :, HIST:], ALU.mult, ALU.subtract)
                last_d.then_inc(d_d, 1)
                dve.wait_ge(d_d, 4 * g + 2)
                head = last[:, :, Z:Z + w]
                nc.vector.tensor_tensor(dd[:, :, 0:w], head, inv[:, 0:w].unsqueeze(1).broadcast_to([P, CT, w]), ALU.mult).then_inc(d_d, 1)
                dve.wait_ge(d_d, 4 * g + 3)
                nc.vector.tensor_tensor(dd[:, :, 0:w], dd[:, :, 0:w], u[:, g % 2, :, Z:Z + w], ALU.subtract).then_inc(d_d, 1)
                dve.wait_ge(dh_d, g + 1)
                nc.vector.tensor_tensor(d_lo[:, :, :], dd[:, :, :], d_hi[:, :, :].bitcast(F32), ALU.subtract).then_inc(dl_d, 1)
                dve.wait_ge(g_in[g % 2], 16 * (g // 2 + 1))
                for i in range(CT * CH):
                    ct, ch = i // CH, i % CH
                    at = (slice(None), ct, slice(ch * CW, (ch + 1) * CW))
                    if i == 0 and g:
                        dve.wait_ge(m_out[(g - 1) % 2], 16 * ((g - 1) // 2 + 1))
                    dve.wait_ge(y_d, CT * CH * g + i + 1)
                    nc.vector.scalar_tensor_tensor(mix[at], banks[ch][:, 0:CW], sc_col[:, CT * g + ct:CT * g + ct + 1],
                                                   gate[at], ALU.mult, ALU.mult).then_inc(mx_d, 1)

        @block.tensor
        def _(pe):
            pe.wait_ge(tl_in, 16)
            for k in range(KT):
                last = nc.tensor.transpose(banks[5 if k < 4 else 0][0:TAIL, k % 4 * P:(k % 4 + 1) * P], tail[:, k, :], ident[:, :])
                if k % 4 == 3:
                    last.then_inc(tt_d, 1)
            pe.wait_ge(st_in, 16)
            for k in range(KT):
                n = DB * HIST
                last = nc.tensor.transpose(banks[6 + k // 4][:, k % 4 * n:(k % 4 + 1) * n], st_raw[:, k * P:(k + 1) * P], ident[0:n, 0:n])
                if k % 4 == 3:
                    last.then_inc(stt_d, 1)
            pe.wait_ge(wl_d, 1)
            pe.wait_ge(tc_d, 2)
            for g in range(G):
                pe.wait_ge(dl_d, g + 1)
                for i in range(CT * CH):
                    dt, ch = i // CH, i % CH
                    n = CT * CH * g + i
                    if n >= CH:
                        pe.wait_ge(mx_d, n - CH + 1)
                    out = banks[ch][:, 0:CW]
                    for ct in range(CT):
                        wh, wl = wg_hi[:, g, ct, dt * P:(dt + 1) * P], wg_lo[:, g, ct, dt * P:(dt + 1) * P]
                        dh, dl = d_hi[:, ct, ch * CW:(ch + 1) * CW], d_lo[:, ct, ch * CW:(ch + 1) * CW]
                        nc.tensor.matmul(out, wh, dh, start=(ct == 0), stop=False)
                        nc.tensor.matmul(out, wh, dl, start=False, stop=False)
                        last = nc.tensor.matmul(out, wl, dh, start=False, stop=(ct == CT - 1))
                    last.then_inc(y_d, 1)

        @block.scalar
        def _(act):
            for n in range(2):
                act.wait_ge(tt_d, n + 1)
                nc.scalar.copy(tail_t[:, n * 512:(n + 1) * 512], banks[5 if n == 0 else 0][0:TAIL, :]).then_inc(tc_d, 1)
            for g in range(G):
                act.wait_ge(d_d, 4 * g + 4)
                if g:
                    act.wait_ge(y_d, CT * CH * g)
                nc.scalar.copy(d_hi[:, :, :], dd[:, :, :]).then_inc(dh_d, 1)
                act.wait_ge(mx_d, CT * CH * (g + 1))
                r0 = g * CT * P
                act.dma_start(bT[r0:r0 + CT * P, :].rearrange("(c p) n -> p c n", p=P), mix[:, :, :]).then_inc(m_out[g % 2], 16)
            for n in range(2):
                act.wait_ge(m_out[n], 16 * 2)


def decoder_step(nc, ins, outs):
    (x_prompt, x_sample, mem_prompt, cache_k, cache_v, cache_logf, cache_mem_k, cache_mem_v, state_pool, page_table,
     norm_pre, norm_post, mem_norm, w_mem_kv, fox_w_in, fox_b_f, pool_w_in, pool_w_group, pool_scale, w_out) = ins
    (y_prompt, y_sample, fox_k_p, fox_v_p, fox_lf_p, fox_k_s, fox_v_s, fox_lf_s, mem_k, mem_v, pool_p, pool_s) = outs
    xp = x_prompt.rearrange("a t d -> (a t) d")
    xs = x_sample.rearrange("b t d -> (b t) d")
    yp = y_prompt.rearrange("a t d -> (a t) d")
    ys = y_sample.rearrange("b t d -> (b t) d")

    def scratch(name, shape):
        return nc.dram_tensor(name, shape, F32, kind="Internal").ap()

    z0 = scratch("z0", (3 * D + XW + BW, TOK))
    z1 = scratch("z1", (D + XW + BW, TOK))
    bT = scratch("bT", (BW, TOK))
    x1p, x1s = scratch("x1p", (SEQ, D)), scratch("x1s", (NS, D))
    cT, sufT = scratch("cT", (FH, SEQ)), scratch("sufT", (DB * FH * TN, PAGES * P))
    cnew, cnew_q = scratch("cnew", (FH, NS)), scratch("cnew_q", (FH, NS))

    with ExitStack() as s:
        banks = [s.enter_context(nc.psum_tensor(f"bank{i}", [P, 512], F32)) for i in range(8)]
        const = make_constants(nc, s, banks)

        def mem(l, z, q_row, gate_row):
            kp, vp = (t[l].rearrange("a m h d -> (a m) (h d)") for t in (mem_k, mem_v))
            memory_kv(nc, f"mk{l}", const, banks, mem_prompt.rearrange("a m d -> (a m) d"), mem_norm[l], w_mem_kv[l], kp, vp)
            memory_attention(nc, f"ma{l}", const, banks, z, q_row, gate_row, bT, kp, vp)

            def page(cache):
                return lambda eng, b, p, tab: cache[l][ds(b, 1), p * P:(p + 1) * P, :, :].rearrange("o t h d -> (o t) (h d)")
            sample_attention(nc, f"sm{l}", const, banks, z, q_row, gate_row, D, bT, XH, NM // P, page(cache_mem_k), page(cache_mem_v))

        with ExitStack() as s0:
            fT = s0.enter_context(nc.sbuf_tensor("fT", [FH, TOK], F32))
            past = s0.enter_context(nc.sbuf_tensor("past", [P, DB, PAGES + PAGES // 2, FH], F32))
            with ExitStack() as s1:
                hi, lo = (s1.enter_context(nc.sbuf_tensor(f"h0{n}", [P, KT, TOK], F32R)) for n in ("hi", "lo"))
                norm_transpose(nc, "n0", const, banks, xp, [(xs, NS, SEQ)], norm_pre[0], hi, lo)
                o = 3 * D + FH
                project(nc, "p0", banks, fox_w_in, hi, lo, z0,
                        [(0, 3 * KT, 0, ACT.Copy), (o, XH, 3 * D, ACT.Copy), (o + XW, BW // P, 3 * D + XW, ACT.Silu)],
                        (3 * D, fox_b_f, fT, page_table, cache_logf, past))
            forget_gates(nc, const, banks, fT, past, fox_lf_p, fox_lf_s, cT, sufT, cnew, cnew_q)
        sample_kv_out(nc, const, banks, z0, fox_k_s, fox_v_s)
        fox_attention(nc, const, banks, z0, cT, bT, fox_k_p, fox_v_p)

        def page(cache):
            def of(eng, b, p, tab):
                n = eng.value_load(tab[0:1, ds(b * PAGES + p, 1)], min_val=0, max_val=cache.shape[0] - 1)
                return cache[ds(n, 1), :, :, :].rearrange("o t h d -> (o t) (h d)")
            return of
        sample_attention(nc, "sf", const, banks, z0, 0, 3 * D + XW, 0, bT, FH, PAGES, page(cache_k), page(cache_v),
                         page_table, sufT, cnew, cnew_q, fox_k_s, fox_v_s.rearrange("b t h d -> (b t) (h d)"))
        mem(0, z0, 3 * D, 3 * D + XW + D)
        output_projection(nc, "o0", banks, bT, w_out[0], norm_post[0], xp, xs, x1p, x1s)

        with ExitStack() as s1:
            hi, lo = (s1.enter_context(nc.sbuf_tensor(f"h1{n}", [P, KT, TOK], F32R)) for n in ("hi", "lo"))
            norm_transpose(nc, "n1", const, banks, x1p, [(x1s, NS, SEQ)], norm_pre[1], hi, lo)
            project(nc, "p1", banks, pool_w_in, hi, lo, z1,
                    [(0, KT + XH, 0, ACT.Copy), (D + XW, BW // P, D + XW, ACT.Silu)])
        pool_mixing(nc, const, banks, z1, state_pool, pool_w_group, pool_scale, bT,
                    pool_p.rearrange("a n d -> (a n) d"), pool_s)
        mem(1, z1, D, D + XW + D)
        output_projection(nc, "o1", banks, bT, w_out[1], norm_post[1], x1p, x1s, yp, ys)


def sample_kv_out(nc, const, banks, zT, k_out, v_out):
    with ExitStack() as s:
        c = Core(nc, s, "so")
        raw, tok = c.sb("raw", [P, 2, FH, NS]), c.sb("tok", [NS, 2, D])
        ld, tr, cp, out = (c.sem(n) for n in ("loaded", "transposed", "copied", "stored"))
        block = s.enter_context(nc.Block())

        @block.sync
        def _(sp):
            for n in range(2):
                sp.dma_start(raw[:, n, :, :], zT[(n + 1) * D:(n + 2) * D, SEQ:TOK].rearrange("(h p) n -> p h n", p=P)).then_inc(ld, 16)
            sp.wait_ge(cp, 4)
            for n, dst in enumerate((k_out, v_out)):
                sp.dma_start(dst.rearrange("b t h d -> (b t) (h d)"), tok[:, n, :]).then_inc(out, 16)
            sp.wait_ge(out, 32)

        @block.tensor
        def _(pe):
            pe.wait_ge(ld, 32)
            for i in range(2 * FH):
                last = nc.tensor.transpose(banks[i // 4][0:NS, i % 4 * P:(i % 4 + 1) * P], raw[:, i // FH, i % FH, :], const["ident"][:, :])
                if i % 4 == 3:
                    last.then_inc(tr, 1)

        @block.scalar
        def _(act):
            for n in range(4):
                act.wait_ge(tr, n + 1)
                nc.scalar.copy(tok[:, n // 2, n % 2 * 512:(n % 2 + 1) * 512], banks[n][0:NS, :]).then_inc(cp, 1)


_INS = ["x_prompt", "x_sample", "mem_prompt", "cache_fox_k", "cache_fox_v", "cache_fox_logf", "cache_mem_k", "cache_mem_v",
        "state_pool", "page_table", "norm_pre", "norm_post", "mem_norm", "w_mem_kv", "fox_w_in", "fox_b_f", "pool_w_in",
        "pool_w_group", "pool_scale", "w_out"]
_OUTS = [(1, SEQ, D), (DB, TN, D), (NQ, P, FH, HD), (NQ, P, FH, HD), (NQ, P, FH), (DB, TN, FH, HD), (DB, TN, FH, HD),
         (DB, TN, FH), (2, 1, NM, XH, HD), (2, 1, NM, XH, HD), (1, HIST, D), (DB, HIST, D)]


def kernel(**inputs):
    import numpy as _np
    import concourse.bacc as _bacc
    from concourse.bass_utils import run_bass_kernel_spmd as _run

    nc = _bacc.Bacc("TRN2", target_bir_lowering=False, num_devices=1)
    arrays, ins = {}, []
    for name in _INS:
        a = _np.ascontiguousarray(inputs[name])
        arrays[f"in_{name}"] = a
        ins.append(nc.dram_tensor(f"in_{name}", a.shape, mybir.dt.from_np(a.dtype), kind="ExternalInput").ap())
    outs = [nc.dram_tensor(f"out_{i}", shape, F32, kind="ExternalOutput").ap() for i, shape in enumerate(_OUTS)]
    decoder_step(nc, ins, outs)
    r = _run(nc, [arrays], core_ids=[0])
    return tuple(r.results[0][f"out_{i}"] for i in range(len(_OUTS)))
```
